# Optimizing a Trainium2 kernel written in Bass

```python
import jax, jax.numpy as jnp
from jax import lax
import numpy as np

D_MODEL = 1024
BATCH = 1
SEQ = 256
DEPTH = 1

POOL_WINDOWS = (2, 4, 8, 16)
POOL_GROUPS = 4
POOL_CH = D_MODEL // 8
POOL_WIDTH = POOL_GROUPS * POOL_CH
CONV_WIDTH = D_MODEL // 2
CONV_K = 31
SGU_CHUNK = 128
SGU_HEADS = 4
SGU_HEAD_DIM = D_MODEL // 8
SGU_WIDTH = SGU_HEADS * SGU_HEAD_DIM
N_BRANCH = 3
BRANCH_WIDTH = 512
IN_WIDTH = POOL_WIDTH + 2 * CONV_WIDTH + 2 * SGU_WIDTH + N_BRANCH * D_MODEL
N_EXPERTS = 32
TOP_K = 4
D_FF = D_MODEL
SWIGLU_LIMIT = 7.0
SWIGLU_ALPHA = 1.702
MOE_BLOCK = 256
PLE_DIM = 256
EPS = 1e-6

kernel_name = "hybrid_pool_conv_sgu_moe_block"

def rms_norm(x, g):
    xf = x.astype(jnp.float32)
    y = xf * lax.rsqrt(jnp.mean(xf * xf, axis=-1, keepdims=True) + EPS)
    return (y * g.astype(jnp.float32)).astype(x.dtype)

def layer_norm(x, g, b):
    xf = x.astype(jnp.float32)
    mu = jnp.mean(xf, axis=-1, keepdims=True)
    var = jnp.mean(jnp.square(xf - mu), axis=-1, keepdims=True)
    y = (xf - mu) * lax.rsqrt(var + EPS)
    return (y * g.astype(jnp.float32) + b.astype(jnp.float32)).astype(x.dtype)

def causal_multiscale_pool(z, pool_w, pool_scale):
    B, S, _ = z.shape
    zf = z.astype(jnp.float32).reshape(B, S, POOL_GROUPS, POOL_CH)
    cs = jnp.cumsum(zf, axis=1)
    t = jnp.arange(S)
    outs = []
    for g, w in enumerate(POOL_WINDOWS):
        c = cs[:, :, g]
        prev = jnp.pad(c, ((0, 0), (w, 0), (0, 0)))[:, :S]
        count = jnp.minimum(t + 1, w).astype(jnp.float32)[None, :, None]
        outs.append((c - prev) / count - zf[:, :, g])
    pooled = jnp.stack(outs, axis=2).astype(z.dtype)
    mixed = jnp.einsum('bsgc,gcd->bsgd', pooled, pool_w).reshape(B, S, POOL_WIDTH)
    return mixed * pool_scale

def causal_depthwise_conv(z, w, b):
    K, C = w.shape
    y = lax.conv_general_dilated(z, w[:, None, :], window_strides=(1,), padding=((K - 1, 0),),
                                 dimension_numbers=('NWC', 'WIO', 'NWC'), feature_group_count=C)
    return y + b

def conformer_conv(z, conv_w, conv_b, norm_g, norm_b):
    a, gate = jnp.split(z, 2, axis=-1)
    y = a * jax.nn.sigmoid(gate)
    y = causal_depthwise_conv(y, conv_w, conv_b)
    y = layer_norm(y, norm_g, norm_b)
    return jax.nn.silu(y)

def chunked_spatial_gating(u, v, norm_g, norm_b, sgu_w, sgu_b):
    B, S, _ = v.shape
    n = S // SGU_CHUNK
    v = layer_norm(v, norm_g, norm_b)
    vh = v.reshape(B, n, SGU_CHUNK, SGU_HEADS, SGU_HEAD_DIM)
    mask = jnp.tril(jnp.ones((SGU_CHUNK, SGU_CHUNK), dtype=bool))
    w = jnp.where(mask[None], sgu_w, jnp.zeros_like(sgu_w))
    mixed = jnp.einsum('hts,bnshc->bnthc', w, vh) + sgu_b.T[None, None, :, :, None]
    return u * mixed.reshape(B, S, SGU_WIDTH)

def mixer_block(h, w_in, b_in, pool_w, pool_scale, conv_w, conv_b, conv_norm_g, conv_norm_b,
                sgu_norm_g, sgu_norm_b, sgu_w, sgu_b, branch_w, branch_b, w_out):
    B, S, D = h.shape
    z = h @ w_in + b_in
    cuts = np.cumsum([POOL_WIDTH, 2 * CONV_WIDTH, SGU_WIDTH, SGU_WIDTH]).tolist()
    za, zb, zu, zv, zg = jnp.split(z, cuts, axis=-1)
    ya = causal_multiscale_pool(za, pool_w, pool_scale)
    yb = conformer_conv(zb, conv_w, conv_b, conv_norm_g, conv_norm_b)
    yc = chunked_spatial_gating(zu, zv, sgu_norm_g, sgu_norm_b, sgu_w, sgu_b)
    branches = jnp.stack([ya, yb, yc], axis=2)
    proj = jnp.einsum('bskc,kcd->bskd', branches, branch_w) + branch_b
    gates = jax.nn.sigmoid(zg.reshape(B, S, N_BRANCH, D))
    merged = jnp.einsum('bskd,bskd->bsd', gates, proj)
    return merged @ w_out

def moe_ffn(h, router_w, router_b, w_up, b_up, w_down, b_down):
    B, S, D = h.shape
    hf = h.reshape(B * S, D)
    T = hf.shape[0]
    logits = (hf @ router_w + router_b).astype(jnp.float32)
    top_val, top_idx = lax.top_k(logits, TOP_K)
    weights = jax.nn.softmax(top_val, axis=-1)
    flat_e = top_idx.reshape(-1)
    order = jnp.argsort(flat_e)
    sorted_e = flat_e[order]
    tok = (order // TOP_K).astype(jnp.int32)
    gate = weights.reshape(-1)[order].astype(h.dtype)
    counts = jnp.bincount(flat_e, length=N_EXPERTS)
    padded = (counts + MOE_BLOCK - 1) // MOE_BLOCK * MOE_BLOCK
    pad_start = jnp.cumsum(padded) - padded
    start = jnp.cumsum(counts) - counts
    dest = pad_start[sorted_e] + jnp.arange(T * TOP_K) - start[sorted_e]
    n_blocks = -(-(T * TOP_K) // MOE_BLOCK) + N_EXPERTS
    rows = n_blocks * MOE_BLOCK
    slot_tok = jnp.zeros((rows,), jnp.int32).at[dest].set(tok)
    slot_gate = jnp.zeros((rows,), h.dtype).at[dest].set(gate)
    block_e = jnp.searchsorted(jnp.cumsum(padded), jnp.arange(n_blocks) * MOE_BLOCK, side='right')
    block_e = jnp.minimum(block_e, N_EXPERTS - 1)

    def run_block(args):
        tok_b, gate_b, e = args
        xb = hf[tok_b]
        gu = xb @ w_up[e] + b_up[e]
        x_glu, x_lin = jnp.split(gu, 2, axis=-1)
        x_glu = jnp.minimum(x_glu, SWIGLU_LIMIT)
        x_lin = jnp.clip(x_lin, -SWIGLU_LIMIT, SWIGLU_LIMIT)
        act = x_glu * jax.nn.sigmoid(SWIGLU_ALPHA * x_glu) * (x_lin + 1.0)
        y = act @ w_down[e] + b_down[e]
        return y * gate_b[:, None]

    ys = lax.map(run_block, (slot_tok.reshape(n_blocks, MOE_BLOCK),
                             slot_gate.reshape(n_blocks, MOE_BLOCK), block_e))
    out = jnp.zeros_like(hf).at[slot_tok].add(ys.reshape(rows, D))
    return out.reshape(B, S, D)

def setup_inputs(seed: int = 0) -> dict:
    key = jax.random.key(seed)
    ks = iter(jax.random.split(key, 40))
    f32 = jnp.float32
    L, D = DEPTH, D_MODEL

    def nrm(shape, scale):
        return jax.random.normal(next(ks), shape, f32) * scale

    def gain(shape):
        return 1.0 + nrm(shape, 0.05)

    return {
        "x": nrm((BATCH, SEQ, D), 1.0),
        "p": nrm((L, BATCH, SEQ, PLE_DIM), 1.0),
        "mix_norm": gain((L, D)),
        "w_in": nrm((L, D, IN_WIDTH), D ** -0.5),
        "b_in": nrm((L, IN_WIDTH), 0.02),
        "pool_w": nrm((L, POOL_GROUPS, POOL_CH, POOL_CH), POOL_CH ** -0.5),
        "pool_scale": gain((L, POOL_WIDTH)),
        "conv_w": nrm((L, CONV_K, CONV_WIDTH), CONV_K ** -0.5),
        "conv_b": nrm((L, CONV_WIDTH), 0.02),
        "conv_norm_g": gain((L, CONV_WIDTH)),
        "conv_norm_b": nrm((L, CONV_WIDTH), 0.02),
        "sgu_norm_g": gain((L, SGU_WIDTH)),
        "sgu_norm_b": nrm((L, SGU_WIDTH), 0.02),
        "sgu_w": nrm((L, SGU_HEADS, SGU_CHUNK, SGU_CHUNK), 0.5 * SGU_CHUNK ** -0.5),
        "sgu_b": gain((L, SGU_HEADS, SGU_CHUNK)),
        "branch_w": nrm((L, N_BRANCH, BRANCH_WIDTH, D), BRANCH_WIDTH ** -0.5),
        "branch_b": nrm((L, N_BRANCH, D), 0.02),
        "w_out": nrm((L, D, D), D ** -0.5),
        "moe_norm": gain((L, D)),
        "router_w": nrm((L, D, N_EXPERTS), D ** -0.5),
        "router_b": nrm((L, N_EXPERTS), 0.01),
        "expert_w_up": nrm((L, N_EXPERTS, D, 2 * D_FF), D ** -0.5),
        "expert_b_up": nrm((L, N_EXPERTS, 2 * D_FF), 0.02),
        "expert_w_down": nrm((L, N_EXPERTS, D_FF, D), D_FF ** -0.5),
        "expert_b_down": nrm((L, N_EXPERTS, D), 0.02),
        "ple_norm": gain((L, D)),
        "ple_gate_w": nrm((L, D, D), D ** -0.5),
        "ple_proj_w": nrm((L, PLE_DIM, D), PLE_DIM ** -0.5),
        "final_norm": gain((D,)),
    }

def reference(x, p, mix_norm, w_in, b_in, pool_w, pool_scale, conv_w, conv_b, conv_norm_g,
              conv_norm_b, sgu_norm_g, sgu_norm_b, sgu_w, sgu_b, branch_w, branch_b, w_out,
              moe_norm, router_w, router_b, expert_w_up, expert_b_up, expert_w_down,
              expert_b_down, ple_norm, ple_gate_w, ple_proj_w, final_norm):
    for i in range(DEPTH):
        h = rms_norm(x, mix_norm[i])
        x = x + mixer_block(h, w_in[i], b_in[i], pool_w[i], pool_scale[i], conv_w[i], conv_b[i],
                            conv_norm_g[i], conv_norm_b[i], sgu_norm_g[i], sgu_norm_b[i],
                            sgu_w[i], sgu_b[i], branch_w[i], branch_b[i], w_out[i])
        h = rms_norm(x, moe_norm[i])
        x = x + moe_ffn(h, router_w[i], router_b[i], expert_w_up[i], expert_b_up[i],
                        expert_w_down[i], expert_b_down[i])
        h = rms_norm(x, ple_norm[i])
        x = x + jax.nn.sigmoid(h @ ple_gate_w[i]) * (p[i] @ ple_proj_w[i])
    return rms_norm(x, final_norm)


_drawn_inputs = setup_inputs


def setup_inputs(seed=0):
    import zlib

    import numpy as np

    out = dict(_drawn_inputs(seed))
    spreads = {}
    factors = {'sgu_norm_b': 6.997,
     'expert_b_up': 6.664,
     'expert_b_down': 7.608,
     'ple_norm': 7.828,
     'conv_norm_b': 3.404,
     'sgu_norm_g': 3.917,
     'router_b': 3.415}
    for name, (base, spread) in spreads.items():
        noise = np.random.default_rng([zlib.crc32(name.encode()), seed]).standard_normal(out[name].shape)
        drawn = base * np.exp(spread * noise) if base else spread * noise
        out[name] = __import__('jax').numpy.asarray(drawn.astype(out[name].dtype))
    for name, factor in factors.items():
        out[name] = (out[name] * factor).astype(out[name].dtype)
    return out
```

```python
from contextlib import ExitStack

import concourse.bass as bass
from concourse import mybir

F32 = mybir.dt.float32
I32 = mybir.dt.int32
U32 = mybir.dt.uint32
ALU = mybir.AluOpType
ACT = mybir.ActivationFunctionType
AX = mybir.AxisListType.X

P = 128
T = 256
TT = T // P
D = 1024
KT = D // P
CH = 512
CT = CH // P
CONV_K = 31
POOL_PAD = 16
N_EXP = 32
TOP_K = 4
SLOTS = 64
ROUNDS = T // SLOTS
N_BRANCH = 3
PLE = 256
EPS = 1e-6
LIMIT = 7.0
ALPHA = 1.702

UNIT = 2048
UP_SLOTS, DOWN_SLOTS = 16, 4
UP_UNITS, DOWN_UNITS = 8, 4
PER_EXPERT = UP_UNITS + DOWN_UNITS
MIX_SLOTS = 12
MIX_FIRST = 4

CHUNKS = [("gate", 1024), ("a", 512), ("pool", 0), ("v", 2048), ("u", 1536)] + \
         [("g", 2560 + CH * g) for g in range(N_BRANCH * D // CH)]
N_CHUNKS = len(CHUNKS)
MIX_UNITS = 2 * N_CHUNKS + 2 * N_BRANCH + KT // 2
BRANCH_UNIT0 = 2 * N_CHUNKS
OUT_UNIT0 = BRANCH_UNIT0 + 2 * N_BRANCH

PARAMS = [("mix_norm", 8), ("b_in", 44), ("pool_scale", 4), ("conv_b", 4), ("conv_norm_g", 4),
          ("conv_norm_b", 4), ("branch_b", 24), ("moe_norm", 8), ("ple_norm", 8)]
ROW = {}
N_ROWS = 0
for _name, _rows in PARAMS:
    ROW[_name] = N_ROWS
    N_ROWS += _rows


def mix_slot(unit):
    return (unit + MIX_FIRST) % MIX_SLOTS, sum((u - unit) % MIX_SLOTS == 0 for u in range(unit + 1))


MIX_USES = [sum(mix_slot(u)[0] == s for u in range(MIX_UNITS)) for s in range(UP_SLOTS)]


def build(nc, x, p, mix_norm, w_in, b_in, pool_w, pool_scale, conv_w, conv_b, conv_norm_g,
          conv_norm_b, sgu_norm_g, sgu_norm_b, sgu_w, sgu_b, branch_w, branch_b, w_out, moe_norm,
          router_w, router_b, expert_w_up, expert_b_up, expert_w_down, expert_b_down, ple_norm,
          ple_gate_w, ple_proj_w, final_norm, out):
    with ExitStack() as ctx:
        def sb(name, shape, dt=F32):
            return ctx.enter_context(nc.sbuf_tensor(name, shape, dt))

        def sem(name):
            return ctx.enter_context(nc.semaphore(name))

        up_ring = sb("up_ring", [P, UP_SLOTS, UNIT])
        down_ring = sb("down_ring", [P, DOWN_SLOTS, UNIT])
        x_sb = sb("x_sb", [P, TT, D])
        xs = sb("xs", [P, TT, D])
        hT = sb("hT", [P, KT, T])
        work = sb("work", [P, 6 * 512])
        ident = sb("ident", [P, P])
        ones = sb("ones", [P, P])
        mean_mat = sb("mean_mat", [P, P])
        before = sb("before", [P, P])
        slot_ids = sb("slot_ids", [P, 2, SLOTS])
        prm = sb("prm", [P, N_ROWS])
        conv_taps = sb("conv_taps", [P, CONV_K, CT])
        pool_mix = sb("pool_mix", [P, CT, P])
        pT = sb("pT", [P, PLE // P, T])
        rw = sb("rw", [P, KT, N_EXP])
        rb = sb("rb", [P, N_EXP])
        QPAD = ROUNDS * N_EXP + 2
        pos = sb("pos", [P, TT, QPAD])
        gate_w = sb("gate_w", [P, TT, QPAD])
        small = sb("small", [P, 64])
        flag = sb("flag", [P, 2], I32)

        eps = small[:, 0:1]
        ssq = small[:, 1:3]
        rms = small[:, 3:5]
        rstd = small[:, 5:7]
        vstat = small[:, 8:20]
        vmv = small[:, 20:24]
        vrms = small[:, 24:26]
        vrstd = small[:, 26:28]
        wsum = small[:, 28:30]
        wrec = small[:, 30:32]
        most = small[:, 32:33]

        spare = up_ring[:, MIX_SLOTS:, :].rearrange("p a b -> p (a b)")
        PW = POOL_PAD + T
        z_pool = spare[:, 0:4 * PW].rearrange("p (g t) -> p g t", g=4)
        sum2 = spare[:, 1088:2176].rearrange("p (g t) -> p g t", g=4)
        sum4 = spare[:, 2176:2992].rearrange("p (g t) -> p g t", g=3)
        sum8 = spare[:, 2992:3536].rearrange("p (g t) -> p g t", g=2)
        sum16 = spare[:, 3536:3808].rearrange("p (g t) -> p g t", g=1)
        inv_count = spare[:, 3808:4832].rearrange("p (g t) -> p g t", g=4)
        pooled = spare[:, 4832:5856].rearrange("p (g t) -> p g t", g=4)
        yaT = spare[:, 5856:6880].rearrange("p (g t) -> p g t", g=4)
        p_sb = spare[:, 5856:6368].rearrange("p (a b) -> p a b", a=TT)
        sguT = spare[:, 6880:7392].rearrange("p (h t) -> p h t", h=4)
        sgub = spare[:, 7392:7904].rearrange("p (h t) -> p h t", h=4)
        squares = spare[:, 1088:2112].rearrange("p (g t) -> p g t", g=4)
        sgu_mix = spare[:, 2176:3200].rearrange("p (g t) -> p g t", g=4)
        gated = spare[:, 0:768].rearrange("p (g t) -> p g t", g=3)
        spare_d = down_ring[:, :, :].rearrange("p a b -> p (a b)")
        gates = spare_d[:, 0:6144].rearrange("p (k c t) -> p k c t", k=N_BRANCH, c=KT)
        CW = CONV_K - 1 + T
        y_pad = spare_d[:, 6144:6144 + 4 * CW].rearrange("p (c t) -> p c t", c=CT)
        conv_rstd = spare_d[:, 7288:7544]
        prm_rows = spare_d[:, 7544:7672]
        tap_rows = spare_d[:, 7672:7800]
        convT = xs[:, 0, :].rearrange("p (c t) -> p c t", c=CT)
        uT = xs[:, 1, :].rearrange("p (c t) -> p c t", c=CT)
        v_sb = work[:, 0:1024].rearrange("p (n c) -> p n c", n=TT)
        v_bias = work[:, 1024:1536]
        v_gain = work[:, 1536:2048]
        v_shift = work[:, 2048:2560]
        sgu_in = work[:, 2560:3072].rearrange("p (h t) -> p h t", h=4)
        sig_gate = inv_count

        onehot = work[:, 1024:1280].rearrange("p (a j e) -> p a j e", a=TT, j=TOP_K)
        weighted = work[:, 1280:1536].rearrange("p (a j e) -> p a j e", a=TT, j=TOP_K)
        logits = work[:, 2304:2368].rearrange("p (a e) -> p a e", a=TT)
        chosen = work[:, 2368:2432].rearrange("p (a e) -> p a e", a=TT)
        pos0 = work[:, 2432:2496].rearrange("p (a e) -> p a e", a=TT)
        top = work[:, 2496:2512].rearrange("p (a e) -> p a e", a=TT)
        top_i = work[:, 2512:2528].bitcast(U32).rearrange("p (a e) -> p a e", a=TT)
        top_f = work[:, 2528:2544].rearrange("p (a e) -> p a e", a=TT)
        top_e = work[:, 2544:2552].rearrange("p (a e) -> p a e", a=TT)
        gateT = work[0:N_EXP, 2560:2816]
        b_down = work[0:N_EXP, 0:1024]

        glu = work[:, 0:512]
        lin = work[:, 512:1024]
        sig = work[:, 1024:1536]
        b_up = work[:, 1536:2048]
        select = work[:, 2048:2304].rearrange("p (b a s) -> p b a s", b=2, a=TT)
        weight = work[:, 2304:2560].rearrange("p (a s) -> p a s", a=TT)
        weightT = work[:, 2560:2816].rearrange("p (a t) -> p a t", a=TT)
        pick_bias = work[:, 2816:3072].rearrange("p (c s) -> p c s", c=4)
        hT_flat = hT[:, :, :].rearrange("p a b -> p (a b)")
        xe = hT_flat[:, 0:1024].rearrange("p (b k s) -> p b k s", b=2, k=KT)
        actT = hT_flat[:, 1024:1536].rearrange("p (m g s) -> p m g s", m=4, g=2)
        y_sb = hT_flat[:, 1536:2048]
        ident_e = ident[:, :].rearrange("p (c e) -> p c e", c=4)

        ple_sig = up_ring[:, 8:9, :].rearrange("p a (b c) -> p (a b) c", b=TT)
        final_out = up_ring[:, 9:10, :].rearrange("p a (b c) -> p (a b) c", b=TT)
        final_gain = work[:, 0:1024]

        ps = ctx.enter_context(nc.psum_tensor("ps", [P, 8, 512], F32))
        GLU, LIN, GATHER, ACTT, WT, Y, COMB = 0, 1, 2, 3, 4, 5, 6

        def quarter(bank, n=4):
            return ps[:, bank:bank + 2, :].rearrange("p a (b t) -> p (a b) t", t=T)[:, 0:n, :]

        x_loaded = sem("x_loaded")
        rows_loaded = sem("rows_loaded")
        p_loaded = sem("p_loaded")
        sgu_loaded = sem("sgu_loaded")
        vbc_loaded = sem("vbc_loaded")
        mats_loaded = sem("mats_loaded")
        bdown_loaded = sem("bdown_loaded")
        bup_loaded = sem("bup_loaded")
        gain_loaded = sem("gain_loaded")
        up_loaded = [sem(f"up_loaded{s}") for s in range(UP_SLOTS)]
        down_loaded = [sem(f"down_loaded{s}") for s in range(DOWN_SLOTS)]
        w_used = sem("w_used")
        consts_ready = sem("consts_ready")
        pool_order = sem("pool_order")
        dve_order = sem("dve_order")
        act_order = sem("act_order")
        sgu_masked = sem("sgu_masked")
        rowsT_done = sem("rowsT_done")
        prm_ready = sem("prm_ready")
        pT_done = sem("pT_done")
        sguT_done = sem("sguT_done")
        sguT_ready = sem("sguT_ready")
        x_ready = sem("x_ready")
        rms_ready = sem("rms_ready")
        xs_ready = sem("xs_ready")
        xsT_done = sem("xsT_done")
        hT_act = sem("hT_act")
        hT_dve = sem("hT_dve")
        chunk_read = sem("chunk_read")
        a_read = sem("a_read")
        conv_step = sem("conv_step")
        y_pad_ready = sem("y_pad_ready")
        pool_sums_free = sem("pool_sums_free")
        inv_ready = sem("inv_ready")
        count_ready = sem("count_ready")
        pooled_ready = sem("pooled_ready")
        pool_mixed = sem("pool_mixed")
        yaT_ready = sem("yaT_ready")
        v_rms_ready = sem("v_rms_ready")
        v_var_ready = sem("v_var_ready")
        v_ready = sem("v_ready")
        sgu_done = sem("sgu_done")
        ycT_ready = sem("ycT_ready")
        mean_done = sem("mean_done")
        centred = sem("centred")
        sq_ready = sem("sq_ready")
        var_done = sem("var_done")
        conv_rms_ready = sem("conv_rms_ready")
        conv_normed = sem("conv_normed")
        ybT_ready = sem("ybT_ready")
        proj_done = sem("proj_done")
        proj_read = sem("proj_read")
        merged_ready = sem("merged_ready")
        logits_done = sem("logits_done")
        top_ready = sem("top_ready")
        top_exp = sem("top_exp")
        chosen_ready = sem("chosen_ready")
        pos_done = sem("pos_done")
        gates_ready = sem("gates_ready")
        gateT_done = sem("gateT_done")
        gateT_ready = sem("gateT_ready")
        bdown_done = sem("bdown_done")
        bdown_added = sem("bdown_added")
        flag_ready = sem("flag_ready")
        select_ready = sem("select_ready")
        gather_done = sem("gather_done")
        xe_ready = sem("xe_ready")
        pick_ready = sem("pick_ready")
        weight_ready = sem("weight_ready")
        weightT_done = sem("weightT_done")
        weightT_ready = sem("weightT_ready")
        up_done = sem("up_done")
        glu_ready = sem("glu_ready")
        lin_ready = sem("lin_ready")
        sig_ready = sem("sig_ready")
        prod_ready = sem("prod_ready")
        act_ready = sem("act_ready")
        actT_done = sem("actT_done")
        actT_ready = sem("actT_ready")
        y_ready = sem("y_ready")
        comb_done = sem("comb_done")
        x_added = sem("x_added")
        ple_loaded = sem("ple_loaded")
        ple_proj_done = sem("ple_proj_done")
        ple_gate_done = sem("ple_gate_done")
        ple_sig_ready = sem("ple_sig_ready")
        ple_x_ready = sem("ple_x_ready")
        final_rms = sem("final_rms")
        final_ready = sem("final_ready")
        stored = sem("stored")

        mixer_small = {"mix_norm": mix_norm, "b_in": b_in, "pool_scale": pool_scale, "conv_b": conv_b,
                       "conv_norm_g": conv_norm_g, "conv_norm_b": conv_norm_b, "branch_b": branch_b,
                       "moe_norm": moe_norm, "ple_norm": ple_norm}

        def rows128(ap):
            if len(ap.shape) == 3:
                ap = ap.rearrange("a b c -> a (b c)")
            return ap.rearrange("a (r c) -> (a r) c", c=P)

        def on_all(ap_row):
            return ap_row.partition_broadcast(P)

        def wait_past(eng, semaphore, value):
            if isinstance(value, int) and value <= 0:
                return
            eng.wait_ge(semaphore, value)

        def used_before(q):
            return MIX_UNITS + PER_EXPERT * q

        def up_value(slot, turn):
            return 16 * (MIX_USES[slot] + turn)

        block = ctx.enter_context(nc.Block())

        @block.sync
        def _(sp):
            sp.dma_start(x_sb[:, :, :], x[0].rearrange("(a p) d -> p a d", p=P)).then_inc(x_loaded, 16)

            def mix_source(u):
                if u < BRANCH_UNIT0:
                    col = CHUNKS[u // 2][1]
                    rows = w_in[0, (u % 2) * 512:(u % 2 + 1) * 512, col:col + CH]
                    return rows.rearrange("(c p) n -> p c n", p=P)
                if u < OUT_UNIT0:
                    half, br = divmod(u - BRANCH_UNIT0, N_BRANCH)
                    return branch_w[0, br, :, half * 512:(half + 1) * 512].rearrange("(c p) n -> p c n", p=P)
                m = u - OUT_UNIT0
                return w_out[0, m * 256:(m + 1) * 256, :].rearrange("(c p) n -> p c n", p=P)

            for u in range(MIX_UNITS):
                if u == 2:
                    sp.wait_ge(rows_loaded, 16 * (len(PARAMS) + 1))
                if u == 4:
                    sp.wait_ge(mats_loaded, 48)
                if u >= MIX_SLOTS:
                    sp.wait_ge(w_used, u - MIX_SLOTS + 1)
                slot = mix_slot(u)[0]
                src = mix_source(u)
                dst = up_ring[:, slot, :].rearrange("p (c n) -> p c n", c=src.shape[1])
                sp.dma_start(dst, src).then_inc(up_loaded[slot], 16)

            def load_up(j, c, e):
                sp.dma_start(up_ring[:, UP_UNITS * j + c, :],
                             up_rows(e)[:, c, :]).then_inc(up_loaded[UP_UNITS * j + c], 16)

            def up_rows(e):
                return expert_w_up[0, bass.ds(e, 1)].rearrange("a (c p) n -> p (a c) n", p=P)

            def load_down(c, e):
                rows = expert_w_down[0, bass.ds(e, 1)].rearrange("a (c p) n -> p (a c) n", p=P)
                sp.dma_start(down_ring[:, c, :].rearrange("p (c n) -> p c n", c=2),
                             rows[:, 2 * c:2 * c + 2, :]).then_inc(down_loaded[c], 16)

            for c in range(MIX_SLOTS):
                sp.wait_ge(w_used, MIX_UNITS - MIX_SLOTS + c + 1)
                load_up(c // UP_UNITS, c % UP_UNITS, c // UP_UNITS)
                if c == UP_UNITS - 1:
                    sp.wait_ge(merged_ready, KT)
                    for c4 in range(DOWN_UNITS):
                        load_down(c4, 0)
                    for c4 in range(MIX_SLOTS, UP_SLOTS):
                        load_up(1, c4 - UP_UNITS, 1)
            with sp.Fori(1, N_EXP // 2) as i:
                for j in range(2):
                    for c in range(UP_UNITS):
                        sp.wait_ge(w_used, used_before(2 * i + j - 2) + c + 1)
                        load_up(j, c, 2 * i + j)
                    for c in range(DOWN_UNITS):
                        sp.wait_ge(w_used, used_before(2 * i + j - 2) + UP_UNITS + c + 1)
                        load_down(c, 2 * i + j - 1)
            for c in range(DOWN_UNITS):
                sp.wait_ge(w_used, used_before(N_EXP - 2) + UP_UNITS + c + 1)
                load_down(c, N_EXP - 1)

            sp.wait_ge(flag_ready, 1)
            overflow = sp.value_load(flag[0:1, 0:1], min_val=0, max_val=1)
            with sp.If(overflow > 0):
                with sp.Fori(1, ROUNDS) as r:
                    with sp.Fori(0, N_EXP // 2) as i:
                        for j in range(2):
                            q = N_EXP * r + 2 * i + j
                            for c in range(UP_UNITS):
                                sp.wait_ge(w_used, used_before(q - 2) + c + 1)
                                load_up(j, c, 2 * i + j)
                            for c in range(DOWN_UNITS):
                                sp.wait_ge(w_used, used_before(q - 1) + UP_UNITS + c + 1)
                                load_down(c, 2 * i + j)
                sp.wait_ge(w_used, used_before(ROUNDS * N_EXP))
            sp.wait_ge(w_used, used_before(N_EXP - 2) + UP_UNITS)
            sp.dma_start(up_ring[:, 4, :].rearrange("p (c n) -> p c n", c=2),
                         ple_proj_w[0].rearrange("(c p) n -> p c n", p=P)).then_inc(ple_loaded, 16)
            for m in range(4):
                sp.dma_start(up_ring[:, m, :].rearrange("p (c n) -> p c n", c=2),
                             ple_gate_w[0, m * 256:(m + 1) * 256, :].rearrange("(c p) n -> p c n", p=P)
                             ).then_inc(ple_loaded, 16)
            for a in range(TT):
                sp.wait_ge(final_ready, a + 1)
                sp.dma_start(out[0, a * P:(a + 1) * P, :], final_out[:, a, :]).then_inc(stored, 16)
            sp.wait_ge(stored, 16 * TT)

        @block.gpsimd
        def _(pool):
            nc.gpsimd.memset(ident[:, :], 0.0).then_inc(pool_order, 1)
            nc.gpsimd.memset(before[:, :], 1.0).then_inc(pool_order, 1)
            nc.gpsimd.memset(ones[:, :], 1.0).then_inc(consts_ready, 1)
            nc.gpsimd.memset(mean_mat[:, :], 1.0 / CH).then_inc(consts_ready, 1)
            nc.gpsimd.iota(slot_ids[:, :, :], [[0, 2], [1, SLOTS]], base=0, channel_multiplier=0,
                           allow_small_or_imprecise_dtypes=True).then_inc(consts_ready, 1)
            nc.gpsimd.memset(z_pool[:, :, 0:POOL_PAD], 0.0).then_inc(consts_ready, 1)
            nc.gpsimd.memset(y_pad[:, :, 0:CONV_K - 1], 0.0).then_inc(consts_ready, 1)
            pool.wait_ge(pool_order, 2)
            nc.gpsimd.affine_select(out=ident[:, :], in_=ident[:, :], compare_op=ALU.not_equal, fill=1.0,
                                    base=0, pattern=[[-1, P]], channel_multiplier=1).then_inc(consts_ready, 1)
            nc.gpsimd.affine_select(out=before[:, :], in_=before[:, :], compare_op=ALU.is_gt, fill=0.0,
                                    base=0, pattern=[[1, P]], channel_multiplier=-1).then_inc(consts_ready, 1)
            pool.wait_ge(sgu_loaded, 32)
            nc.gpsimd.affine_select(out=sgu_in[:, :, :], in_=sgu_in[:, :, :], compare_op=ALU.is_ge, fill=0.0,
                                    base=0, pattern=[[0, 4], [-1, P]], channel_multiplier=1).then_inc(sgu_masked, 1)
            pool.wait_ge(a_read, 1)
            nc.gpsimd.iota(inv_count[:, :, :], [[0, 4], [1, T]], base=1, channel_multiplier=0,
                           allow_small_or_imprecise_dtypes=True).then_inc(pool_order, 1)
            pool.wait_ge(pool_order, 3)
            for g in range(4):
                last = nc.gpsimd.tensor_scalar(inv_count[:, g, :], inv_count[:, g, :], float(2 << g), None, ALU.min)
            last.then_inc(count_ready, 1)
            pool.wait_ge(chunk_read, 2)
            nc.gpsimd.tensor_tensor(sum2[:, :, 1:PW], z_pool[:, :, 1:PW], z_pool[:, :, 0:PW - 1],
                                    ALU.add).then_inc(pool_order, 1)
            pool.wait_ge(pool_order, 4)
            nc.gpsimd.tensor_tensor(sum4[:, :, 3:PW], sum2[:, 1:4, 3:PW], sum2[:, 1:4, 1:PW - 2],
                                    ALU.add).then_inc(pool_order, 1)
            pool.wait_ge(pool_order, 5)
            nc.gpsimd.tensor_tensor(sum8[:, :, 7:PW], sum4[:, 1:3, 7:PW], sum4[:, 1:3, 3:PW - 4],
                                    ALU.add).then_inc(pool_order, 1)
            pool.wait_ge(pool_order, 6)
            nc.gpsimd.tensor_tensor(sum16[:, :, 15:PW], sum8[:, 1:2, 15:PW], sum8[:, 1:2, 7:PW - 8],
                                    ALU.add).then_inc(pool_order, 1)
            pool.wait_ge(pool_order, 7)
            pool.wait_ge(inv_ready, 1)
            for g, s in enumerate((sum2, sum4, sum8, sum16)):
                nc.gpsimd.tensor_tensor(pooled[:, g, :], s[:, 0, POOL_PAD:PW], inv_count[:, g, :],
                                        ALU.mult).then_inc(pool_order, 1)
            pool.wait_ge(pool_order, 11)
            nc.gpsimd.tensor_tensor(pooled[:, :, :], pooled[:, :, :], z_pool[:, :, POOL_PAD:PW],
                                    ALU.subtract).then_inc(pooled_ready, 1)

        @block.scalar
        def _(act):
            for name, _ in PARAMS:
                rows = rows128(mixer_small[name])
                act.dma_start(prm_rows[ROW[name]:ROW[name] + rows.shape[0], :], rows).then_inc(rows_loaded, 16)
            act.dma_start(tap_rows[0:CONV_K * CT, :], conv_w[0].rearrange("k (c n) -> (k c) n", n=P)
                          ).then_inc(rows_loaded, 16)
            act.dma_start(sgu_in[:, :, :], sgu_w[0].rearrange("h t s -> t h s")).then_inc(sgu_loaded, 16)
            act.dma_start(sgub[:, :, :], on_all(sgu_b[0])).then_inc(sgu_loaded, 16)
            act.dma_start(p_sb[:, :, :], p[0, 0].rearrange("(a p) d -> p a d", p=P)).then_inc(p_loaded, 16)
            act.dma_start(v_bias, on_all(b_in[0, 2048:2560])).then_inc(vbc_loaded, 16)
            act.dma_start(v_gain, on_all(sgu_norm_g[0])).then_inc(vbc_loaded, 16)
            act.dma_start(v_shift, on_all(sgu_norm_b[0])).then_inc(vbc_loaded, 16)
            act.dma_start(pool_mix[:, :, :], pool_w[0].rearrange("g c d -> c g d")).then_inc(mats_loaded, 16)
            act.dma_start(rw[:, :, :], router_w[0].rearrange("(c p) e -> p c e", p=P)).then_inc(mats_loaded, 16)
            act.dma_start(rb[:, :], on_all(router_b[0])).then_inc(mats_loaded, 16)

            steps = [0]

            def own(ins):
                steps[0] += 1
                ins.then_inc(act_order, 1)
                act.wait_ge(act_order, steps[0])

            def row_rms(a0, a1):
                for a in range(a0, a1):
                    own(nc.scalar.activation(xs[:, a, :], x_sb[:, a, :], ACT.Square, accum_out=ssq[:, a:a + 1]))
                return nc.scalar.activation(rms[:, a0:a1], ssq[:, a0:a1], ACT.Sqrt, bias=eps, scale=1.0 / D)

            def scale_high(bank, gain):
                for k in range(4, KT):
                    last = nc.scalar.activation(hT[:, k, :], ps[:, bank + k // 2, 256 * (k % 2):256 * (k % 2) + 256], ACT.Copy,
                                                scale=prm[:, gain + k:gain + k + 1])
                last.then_inc(hT_act, 1)

            act.wait_ge(x_loaded, 16)
            act.wait_ge(prm_ready, 1)
            row_rms(0, TT).then_inc(rms_ready, 1)
            act.wait_ge(xsT_done, 1)
            scale_high(4, ROW["mix_norm"])

            act.wait_ge(consts_ready, 7)
            for n, (name, col) in enumerate(CHUNKS):
                if name == "a":
                    continue
                act.wait_ge(w_used, 2 * n + 2)
                bank = 2 * (n % 2)
                tile4 = quarter(bank)
                if name == "v":
                    last = nc.scalar.activation(v_sb[:, :, :], ps[:, bank:bank + 2, :], ACT.Copy)
                for c in range(CT):
                    if name == "v":
                        break
                    bias = prm[:, ROW["b_in"] + col // P + c:ROW["b_in"] + col // P + c + 1]
                    func = ACT.Sigmoid if name in ("gate", "g") else ACT.Identity
                    if name == "gate":
                        dst = sig_gate[:, c, :]
                    elif name == "pool":
                        dst = z_pool[:, c, POOL_PAD:PW]
                    elif name == "u":
                        dst = uT[:, c, :]
                    else:
                        k, d0 = divmod(col - 2560, D)
                        dst = gates[:, k, d0 // P + c, :]
                    last = nc.scalar.activation(dst, tile4[:, c, :], func, bias=bias)
                last.then_inc(chunk_read, 1)
                if n == 5:
                    act.wait_ge(v_var_ready, 1)
                    nc.scalar.activation(vrms, vmv.rearrange("p (a b) -> p a b", b=2)[:, :, 1], ACT.Sqrt,
                                         bias=eps).then_inc(v_rms_ready, 1)
                if n == 8:
                    act.wait_ge(centred, 1)
                    nc.scalar.activation(squares[:, :, :], convT[:, :, :], ACT.Square).then_inc(sq_ready, 1)
                if n == 9:
                    act.wait_ge(var_done, 1)
                    nc.scalar.activation(conv_rstd, ps[:, 5, 0:T], ACT.Sqrt, bias=eps).then_inc(conv_rms_ready, 1)
                    act.wait_ge(conv_normed, 1)
                    for c in range(CT):
                        g, b = ROW["conv_norm_g"] + c, ROW["conv_norm_b"] + c
                        last = nc.scalar.activation(convT[:, c, :], convT[:, c, :], ACT.Silu,
                                                    scale=prm[:, g:g + 1], bias=prm[:, b:b + 1])
                    last.then_inc(ybT_ready, 1)

            act.wait_ge(x_ready, 1)
            row_rms(0, TT).then_inc(rms_ready, 1)
            act.dma_start(b_down, expert_b_down[0]).then_inc(bdown_loaded, 16)
            for c in range(4):
                act.dma_start(b_up[N_EXP * c:N_EXP * (c + 1), :],
                              expert_b_up[0, :, 512 * c:512 * (c + 1)]).then_inc(bup_loaded, 16)
            act.wait_ge(xsT_done, 2)
            scale_high(4, ROW["moe_norm"])
            act.wait_ge(top_ready, 1)
            nc.scalar.activation(top_e[:, :, :], top_e[:, :, :], ACT.Exp).then_inc(top_exp, 1)
            act.wait_ge(gateT_done, 1)
            nc.scalar.activation(gateT, ps[0:N_EXP, WT, 0:T], ACT.Copy).then_inc(gateT_ready, 1)

            def expert(q):
                act.wait_ge(glu_ready, q + 1)
                wait_past(act, prod_ready, 2 * q)
                nc.scalar.activation(sig, glu, ACT.Sigmoid, scale=ALPHA).then_inc(sig_ready, 1)
                act.wait_ge(actT_done, q + 1)
                act.wait_ge(w_used, used_before(q))
                nc.scalar.activation(actT[:, :, :, :].rearrange("p m g s -> p (m g s)"), ps[:, ACTT, :],
                                     ACT.Copy).then_inc(actT_ready, 1)
                act.wait_ge(weightT_done, q + 1)
                wait_past(act, comb_done, 2 * q)
                nc.scalar.activation(weightT[:, :, :].rearrange("p a t -> p (a t)"), ps[:, WT, 0:2 * P],
                                     ACT.Copy).then_inc(weightT_ready, 1)
                act.wait_ge(w_used, used_before(q + 1))
                nc.scalar.activation(y_sb, ps[:, Y, :], ACT.Copy).then_inc(y_ready, 1)

            for q in range(2):
                expert(q)
            with act.Fori(1, N_EXP // 2) as i:
                for j in range(2):
                    expert(2 * i + j)
            act.wait_ge(flag_ready, 1)
            overflow = act.value_load(flag[0:1, 0:1], min_val=0, max_val=1)
            with act.If(overflow > 0):
                with act.Fori(N_EXP // 2, ROUNDS * N_EXP // 2) as i:
                    for j in range(2):
                        expert(2 * i + j)

            act.wait_ge(x_ready, 2)
            act.dma_start(final_gain, on_all(final_norm)).then_inc(gain_loaded, 16)
            row_rms(0, TT).then_inc(rms_ready, 1)
            act.wait_ge(xsT_done, 3)
            scale_high(0, ROW["ple_norm"])
            for a in range(TT):
                for h in range(2):
                    act.wait_ge(ple_gate_done, 2 * a + h + 1)
                    nc.scalar.activation(ple_sig[:, a, h * 512:(h + 1) * 512], ps[:, 2 * a + h, :],
                                         ACT.Sigmoid).then_inc(ple_sig_ready, 1)
            for a in range(TT):
                act.wait_ge(ple_x_ready, a + 1)
                row_rms(a, a + 1).then_inc(final_rms, 1)

        @block.vector
        def _(dve):
            steps = [0]

            def own(ins):
                steps[0] += 1
                ins.then_inc(dve_order, 1)
                dve.wait_ge(dve_order, steps[0])

            def normalise(n):
                dve.wait_ge(rms_ready, n)
                own(nc.vector.reciprocal(rstd, rms))
                for a in range(TT):
                    last = nc.vector.tensor_scalar(xs[:, a, :], x_sb[:, a, :], rstd[:, a:a + 1], None, ALU.mult)
                last.then_inc(xs_ready, 1)

            def scale_low(n, bank, gain):
                dve.wait_ge(xsT_done, n)
                for k in range(4):
                    last = nc.vector.tensor_scalar(hT[:, k, :], ps[:, bank + k // 2, 256 * (k % 2):256 * (k % 2) + 256],
                                                   prm[:, gain + k:gain + k + 1], None, ALU.mult)
                last.then_inc(hT_dve, 1)

            nc.vector.memset(eps, EPS)
            dve.wait_ge(rowsT_done, 1)
            nc.vector.tensor_copy(conv_taps[:, :, :].rearrange("p k c -> p (k c)"), ps[:, 0, P:P + CONV_K * CT])
            nc.vector.tensor_copy(prm[:, :], ps[:, 0, 0:N_ROWS]).then_inc(prm_ready, 1)
            dve.wait_ge(prm_ready, 1)
            dve.wait_ge(x_loaded, 16)
            normalise(1)
            scale_low(1, 4, ROW["mix_norm"])
            dve.wait_ge(pT_done, 1)
            nc.vector.tensor_copy(pT[:, :, :].rearrange("p a t -> p (a t)"), ps[:, 1, :])
            dve.wait_ge(sguT_done, 1)
            nc.vector.tensor_copy(sguT[:, :, :].rearrange("p h t -> p (h t)"), ps[:, 2, :]).then_inc(sguT_ready, 1)

            dve.wait_ge(w_used, 4)
            dve.wait_ge(chunk_read, 1)
            dve.wait_ge(consts_ready, 7)
            for c in range(CT):
                b = ROW["b_in"] + 4 + c
                last = nc.vector.scalar_tensor_tensor(out=y_pad[:, c, CONV_K - 1:CW], in0=quarter(2)[:, c, :],
                                                      scalar=prm[:, b:b + 1], in1=sig_gate[:, c, :],
                                                      op0=ALU.add, op1=ALU.mult)
            last.then_inc(a_read, 1)
            dve.wait_ge(a_read, 1)
            for c in range(CT):
                b = ROW["conv_b"] + c
                nc.vector.tensor_scalar(convT[:, c, :], y_pad[:, c, 0:T], conv_taps[:, 0, c:c + 1],
                                        prm[:, b:b + 1], ALU.mult, ALU.add).then_inc(conv_step, 1)
            with dve.Fori(1, CONV_K) as k:
                for c in range(CT):
                    dve.wait_ge(conv_step, 4 * k + (c - 3))
                    nc.vector.scalar_tensor_tensor(out=convT[:, c, :], in0=y_pad[:, c, bass.ds(k, T)],
                                                   scalar=conv_taps[:, bass.ds(k, 1), c],
                                                   in1=convT[:, c, :], op0=ALU.mult, op1=ALU.add
                                                   ).then_inc(conv_step, 1)
            dve.wait_ge(count_ready, 1)
            nc.vector.reciprocal(inv_count[:, :, :], inv_count[:, :, :]).then_inc(inv_ready, 1)

            dve.wait_ge(chunk_read, 3)
            dve.wait_ge(vbc_loaded, 48)
            for a in range(TT):
                own(nc.vector.tensor_tensor(v_sb[:, a, :], v_sb[:, a, :], v_bias, ALU.add))
                own(nc.vector.bn_stats(vstat[:, 6 * a:6 * a + 6], v_sb[:, a, :]))
                last = nc.vector.bn_aggr(vmv[:, 2 * a:2 * a + 2], vstat[:, 6 * a:6 * a + 6])
            last.then_inc(v_var_ready, 1)
            dve.wait_ge(v_rms_ready, 1)
            own(nc.vector.reciprocal(vrstd, vrms))
            for a in range(TT):
                own(nc.vector.tensor_scalar(v_sb[:, a, :], v_sb[:, a, :], vmv[:, 2 * a:2 * a + 1],
                                            vrstd[:, a:a + 1], ALU.subtract, ALU.mult))
                own(nc.vector.tensor_tensor(v_sb[:, a, :], v_sb[:, a, :], v_gain, ALU.mult))
                last = nc.vector.tensor_tensor(v_sb[:, a, :], v_sb[:, a, :], v_shift, ALU.add)
            last.then_inc(v_ready, 1)

            dve.wait_ge(pool_mixed, 1)
            for c in range(CT):
                s = ROW["pool_scale"] + c
                last = nc.vector.tensor_scalar(yaT[:, c, :], quarter(4)[:, c, :], prm[:, s:s + 1], None, ALU.mult)
            last.then_inc(yaT_ready, 1)
            dve.wait_ge(sgu_done, 1)
            dve.wait_ge(sgu_loaded, 32)
            dve.wait_ge(pooled_ready, 1)
            for n in range(TT):
                own(nc.vector.tensor_tensor(sgu_mix[:, :, n * P:(n + 1) * P], quarter(6)[:, :, n * P:(n + 1) * P],
                                            sgub[:, :, :], ALU.add))
            dve.wait_ge(chunk_read, 4)
            nc.vector.tensor_tensor(uT[:, :, :], uT[:, :, :], sgu_mix[:, :, :], ALU.mult).then_inc(ycT_ready, 1)

            dve.wait_ge(mean_done, 1)
            nc.vector.tensor_tensor(convT[:, :, :], convT[:, :, :],
                                    ps[:, 4:5, 0:T].to_broadcast([P, CT, T]), ALU.subtract).then_inc(centred, 1)
            dve.wait_ge(conv_rms_ready, 1)
            own(nc.vector.reciprocal(conv_rstd, conv_rstd))
            nc.vector.tensor_tensor(convT[:, :, :], convT[:, :, :],
                                    conv_rstd.rearrange("p (a t) -> p a t", a=1).to_broadcast([P, CT, T]),
                                    ALU.mult).then_inc(conv_normed, 1)

            dve.wait_ge(chunk_read, N_CHUNKS - 1)
            for d in range(KT):
                if d % 4 == 3:
                    dve.wait_ge(w_used, BRANCH_UNIT0 + N_BRANCH * (d // 4 + 1))
                else:
                    dve.wait_ge(proj_done, d + 1 - d // 4)
                for k in range(N_BRANCH):
                    b = ROW["branch_b"] + KT * k + d
                    last = nc.vector.scalar_tensor_tensor(out=gated[:, k, :], in0=quarter(2 * (d % 2))[:, k, :],
                                                          scalar=prm[:, b:b + 1], in1=gates[:, k, d, :],
                                                          op0=ALU.add, op1=ALU.mult)
                last.then_inc(proj_read, 1)
                dve.wait_ge(proj_read, d + 1)
                own(nc.vector.tensor_tensor(gated[:, 0, :], gated[:, 0, :], gated[:, 1, :], ALU.add))
                nc.vector.tensor_tensor(hT[:, d, :], gated[:, 0, :], gated[:, 2, :], ALU.add
                                        ).then_inc(merged_ready, 1)
                dve.wait_ge(merged_ready, d + 1)
            dve.wait_ge(w_used, MIX_UNITS)
            for a in range(TT):
                last = nc.vector.tensor_tensor(x_sb[:, a, :], x_sb[:, a, :],
                                               ps[:, 4 + 2 * a:6 + 2 * a, :].rearrange("p a b -> p (a b)"), ALU.add)
            last.then_inc(x_ready, 1)

            normalise(2)
            scale_low(2, 4, ROW["moe_norm"])

            dve.wait_ge(logits_done, 1)
            own(nc.vector.tensor_tensor(logits[:, :, :], ps[:, 0, 0:TT * N_EXP].rearrange("p (a e) -> p a e", a=TT),
                                        rb[:, :].rearrange("p (a e) -> p a e", a=1).to_broadcast([P, TT, N_EXP]),
                                        ALU.add))
            for a in range(TT):
                own(nc.vector.max(top[:, a, :], logits[:, a, :]))
                own(nc.vector.max_index(top_i[:, a, :], top[:, a, :], logits[:, a, :]))
            nc.vector.tensor_tensor(top_e[:, :, :], top[:, :, 0:TOP_K],
                                    top[:, :, 0:1].to_broadcast([P, TT, TOP_K]), ALU.subtract).then_inc(top_ready, 1)
            own(nc.vector.tensor_copy(top_f[:, :, :], top_i[:, :, :]))
            for a in range(TT):
                own(nc.vector.tensor_tensor(onehot[:, a, :, :],
                                            slot_ids[:, 0:1, 0:N_EXP].to_broadcast([P, TOP_K, N_EXP]),
                                            top_f[:, a, 0:TOP_K].unsqueeze(2).to_broadcast([P, TOP_K, N_EXP]),
                                            ALU.is_equal))
            for a in range(TT):
                last = nc.vector.tensor_reduce(chosen[:, a, :], onehot[:, a, :, :].rearrange("p j e -> p e j"),
                                               axis=AX, op=ALU.add)
            last.then_inc(chosen_ready, 1)
            dve.wait_ge(pos_done, 1)
            own(nc.vector.tensor_copy(pos0[:, :, :], ps[:, 1, 0:TT * N_EXP].rearrange("p (a e) -> p a e", a=TT)))
            own(nc.vector.scalar_tensor_tensor(out=pos0[:, :, :], in0=pos0[:, :, :], scalar=1.0,
                                               in1=chosen[:, :, :], op0=ALU.add, op1=ALU.mult))
            for r in range(ROUNDS):
                nc.vector.tensor_scalar(pos[:, :, N_EXP * r:N_EXP * (r + 1)], pos0[:, :, :],
                                        -1.0 - SLOTS * r, None, ALU.add)
            own(nc.vector.memset(pos[:, :, ROUNDS * N_EXP:QPAD], -1.0))

            def make_select(q):
                for a in range(TT):
                    last = nc.vector.tensor_scalar(select_of(q)[:, a, :], slot_ids[:, 0, :],
                                                   pos[:, a, bass.ds(q, 1)], None, ALU.is_equal)
                last.then_inc(select_ready, 1)

            half = [0]

            def select_of(q):
                return select[:, half[0]]

            make_select(0)
            own(nc.vector.reduce_max(most, ps[:, 1, 64:64 + N_EXP], AX))
            nc.vector.tensor_scalar(flag[:, 0:1], most, float(SLOTS), None, ALU.is_gt).then_inc(flag_ready, 1)
            dve.wait_ge(top_exp, 1)
            own(nc.vector.tensor_reduce(wsum, top_e[:, :, :], axis=AX, op=ALU.add))
            own(nc.vector.reciprocal(wrec, wsum))
            own(nc.vector.tensor_tensor(top_e[:, :, :], top_e[:, :, :],
                                        wrec.unsqueeze(2).to_broadcast([P, TT, TOP_K]), ALU.mult))
            for a in range(TT):
                own(nc.vector.tensor_tensor(weighted[:, a, :, :], onehot[:, a, :, :],
                                            top_e[:, a, :].unsqueeze(2).to_broadcast([P, TOP_K, N_EXP]), ALU.mult))
            for a in range(TT):
                own(nc.vector.tensor_reduce(gate_w[:, a, 0:N_EXP], weighted[:, a, :, :].rearrange("p j e -> p e j"),
                                            axis=AX, op=ALU.add))
            for r in range(1, ROUNDS):
                last = nc.vector.tensor_copy(gate_w[:, :, N_EXP * r:N_EXP * (r + 1)], gate_w[:, :, 0:N_EXP])
            last.then_inc(gates_ready, 1)
            dve.wait_ge(gates_ready, 1)

            def scale_xe(q, b):
                dve.wait_ge(gather_done, q + 1)
                gain = prm[:, ROW["moe_norm"]:ROW["moe_norm"] + KT].unsqueeze(2).to_broadcast([P, KT, SLOTS])
                nc.vector.tensor_tensor(xe[:, b, :, :], ps[:, GATHER, :].rearrange("p (k s) -> p k s", k=KT),
                                        gain, ALU.mult).then_inc(xe_ready, 1)

            scale_xe(0, 0)
            dve.wait_ge(bdown_done, 1)
            for a in range(TT):
                last = nc.vector.tensor_tensor(x_sb[:, a, :], x_sb[:, a, :],
                                               ps[:, 4 + 2 * a:6 + 2 * a, :].rearrange("p a b -> p (a b)"), ALU.add)
            last.then_inc(bdown_added, 1)
            dve.wait_ge(bdown_added, 1)

            def expert(q, e, j, first=False):
                wait_past(dve, up_done, q)
                nc.vector.tensor_copy(pick_bias[:, :, :],
                                      ident_e[:, :, bass.ds(e, 1)].to_broadcast([P, 4, SLOTS])).then_inc(pick_ready, 1)
                wait_past(dve, weightT_done, q)
                for a in range(TT):
                    last = nc.vector.tensor_scalar(weight[:, a, :], slot_ids[:, :, :].rearrange("p a s -> p (a s)"),
                                                   pos[:, a, bass.ds(q, 1)], gate_w[:, a, bass.ds(q, 1)],
                                                   ALU.is_equal, ALU.mult)
                last.then_inc(weight_ready, 1)
                dve.wait_ge(gather_done, q + 1)
                half[0] = 1 - j
                make_select(q + 1)
                dve.wait_ge(up_done, q + 1)
                nc.vector.tensor_scalar(glu, ps[:, GLU, :], LIMIT, None, ALU.min).then_inc(glu_ready, 1)
                nc.vector.tensor_scalar(lin, ps[:, LIN, :], LIMIT, -LIMIT, ALU.min, ALU.max).then_inc(lin_ready, 1)
                dve.wait_ge(glu_ready, q + 1)
                dve.wait_ge(lin_ready, q + 1)
                nc.vector.scalar_tensor_tensor(out=lin, in0=lin, scalar=1.0, in1=glu, op0=ALU.add,
                                               op1=ALU.mult).then_inc(prod_ready, 1)
                dve.wait_ge(prod_ready, 2 * q + 1)
                dve.wait_ge(sig_ready, q + 1)
                nc.vector.tensor_tensor(lin, lin, sig, ALU.mult).then_inc(prod_ready, 1)
                if not first:
                    add_result(q - 1, 0)
                scale_xe(q + 1, 1 - j)
                if not first:
                    add_result(q - 1, 1)

            def add_result(q, a):
                dve.wait_ge(comb_done, 2 * q + a + 1)
                nc.vector.tensor_tensor(x_sb[:, a, :], x_sb[:, a, :],
                                        ps[:, COMB:COMB + 2, :].rearrange("p a b -> p (a b)"),
                                        ALU.add).then_inc(x_added, 1)

            for q in range(2):
                expert(q, q, q, first=q == 0)
            with dve.Fori(1, N_EXP // 2) as i:
                for j in range(2):
                    expert(2 * i + j, 2 * i + j, j)
            overflow = dve.value_load(flag[0:1, 0:1], min_val=0, max_val=1)
            with dve.If(overflow > 0):
                with dve.Fori(1, ROUNDS) as r:
                    with dve.Fori(0, N_EXP // 2) as i:
                        for j in range(2):
                            expert(N_EXP * r + 2 * i + j, 2 * i + j, j)
                for a in range(TT):
                    add_result(ROUNDS * N_EXP - 1, a)
                dve.wait_ge(x_added, 2 * ROUNDS * N_EXP)
            with dve.If(overflow < 1):
                for a in range(TT):
                    add_result(N_EXP - 1, a)
                dve.wait_ge(x_added, 2 * N_EXP)
            nc.vector.memset(flag[:, 1:2], 0).then_inc(x_ready, 1)

            normalise(3)
            scale_low(3, 0, ROW["ple_norm"])
            for a in range(TT):
                for h in range(2):
                    cols = slice(h * 512, (h + 1) * 512)
                    dve.wait_ge(ple_sig_ready, 2 * a + h + 1)
                    own(nc.vector.tensor_tensor(ple_sig[:, a, cols], ple_sig[:, a, cols],
                                                ps[:, 4 + 2 * a + h, :], ALU.mult))
                    last = nc.vector.tensor_tensor(x_sb[:, a, cols], x_sb[:, a, cols], ple_sig[:, a, cols], ALU.add)
                last.then_inc(ple_x_ready, 1)
            dve.wait_ge(gain_loaded, 16)
            for a in range(TT):
                dve.wait_ge(final_rms, a + 1)
                own(nc.vector.reciprocal(rstd[:, a:a + 1], rms[:, a:a + 1]))
                nc.vector.scalar_tensor_tensor(out=final_out[:, a, :], in0=x_sb[:, a, :], scalar=rstd[:, a:a + 1],
                                               in1=final_gain, op0=ALU.mult, op1=ALU.mult).then_inc(final_ready, 1)

        @block.tensor
        def _(pe):
            def transpose_xs(n, bank):
                pe.wait_ge(xs_ready, n)
                for k in range(KT):
                    for a in range(TT):
                        col = 256 * (k % 2) + P * a
                        last = nc.tensor.transpose(ps[:, bank + k // 2, col:col + P], xs[:, a, k * P:(k + 1) * P],
                                                   ident[:, :])
                last.then_inc(xsT_done, 1)
                pe.wait_ge(hT_act, n)
                pe.wait_ge(hT_dve, n)

            pe.wait_ge(consts_ready, 7)
            pe.wait_ge(rows_loaded, 16 * (len(PARAMS) + 1))
            nc.tensor.transpose(ps[:, 0, 0:N_ROWS], prm_rows[0:N_ROWS, :], ident[0:N_ROWS, 0:N_ROWS])
            nc.tensor.transpose(ps[:, 0, P:P + CONV_K * CT], tap_rows[0:CONV_K * CT, :],
                                ident[0:CONV_K * CT, 0:CONV_K * CT]).then_inc(rowsT_done, 1)
            pe.wait_ge(p_loaded, 16)
            for k in range(PLE // P):
                for a in range(TT):
                    last = nc.tensor.transpose(ps[:, 1, T * k + P * a:T * k + P * (a + 1)],
                                               p_sb[:, a, k * P:(k + 1) * P], ident[:, :])
            last.then_inc(pT_done, 1)
            pe.wait_ge(sgu_masked, 1)
            for h in range(4):
                last = nc.tensor.transpose(ps[:, 2, P * h:P * (h + 1)], sgu_in[:, h, :], ident[:, :])
            last.then_inc(sguT_done, 1)
            transpose_xs(1, 4)

            def mixer_unit(u, first=True):
                slot, turn = mix_slot(u)
                if first:
                    pe.wait_ge(up_loaded[slot], 16 * turn)
                return up_ring[:, slot, :]

            for n, (name, col) in enumerate(CHUNKS):
                if n == 0:
                    pe.wait_ge(prm_ready, 1)
                    pe.wait_ge(sguT_ready, 1)
                elif n == 3:
                    pe.wait_ge(a_read, 1)
                elif n >= 2:
                    pe.wait_ge(chunk_read, n - 1 - (n > 2))
                w = [mixer_unit(2 * n + s).rearrange("p (c n) -> p c n", c=4) for s in range(2)]
                bank = 2 * (n % 2)
                outs = TT if name == "v" else CT
                for c in range(outs):
                    for k in range(KT):
                        wk = w[k // 4][:, k % 4, :]
                        if name == "v":
                            last = nc.tensor.matmul(ps[:, bank + c, :], hT[:, k, c * P:(c + 1) * P], wk,
                                                    start=(k == 0), stop=(k == KT - 1))
                        else:
                            last = nc.tensor.matmul(quarter(bank)[:, c, :], wk[:, c * P:(c + 1) * P], hT[:, k, :],
                                                    start=(k == 0), stop=(k == KT - 1))
                        if c == outs - 1 and k == 3:
                            last.then_inc(w_used, 1)
                last.then_inc(w_used, 1)
                if n == 6:
                    pe.wait_ge(mats_loaded, 48)
                    pe.wait_ge(pooled_ready, 1)
                    for g in range(4):
                        last = nc.tensor.matmul(quarter(4)[:, g, :], pool_mix[:, g, :], pooled[:, g, :],
                                                start=True, stop=True)
                    last.then_inc(pool_mixed, 1)
                    pe.wait_ge(v_ready, 1)
                    for h in range(4):
                        for a in range(TT):
                            last = nc.tensor.matmul(quarter(6)[:, h, a * P:(a + 1) * P],
                                                    v_sb[:, a, h * P:(h + 1) * P], sguT[:, h, :],
                                                    start=True, stop=True)
                    last.then_inc(sgu_done, 1)
                if n == 7:
                    pe.wait_ge(conv_step, 4 * CONV_K)
                    pe.wait_ge(yaT_ready, 1)
                    for c in range(CT):
                        last = nc.tensor.matmul(ps[:, 4, 0:T], mean_mat[:, :], convT[:, c, :], start=(c == 0),
                                                stop=(c == CT - 1))
                    last.then_inc(mean_done, 1)
                if n == 8:
                    pe.wait_ge(sq_ready, 1)
                    for c in range(CT):
                        last = nc.tensor.matmul(ps[:, 5, 0:T], mean_mat[:, :], squares[:, c, :], start=(c == 0),
                                                stop=(c == CT - 1))
                    last.then_inc(var_done, 1)

            pe.wait_ge(yaT_ready, 1)
            pe.wait_ge(ycT_ready, 1)
            pe.wait_ge(ybT_ready, 1)
            pe.wait_ge(chunk_read, N_CHUNKS - 1)
            branch = [yaT, convT, uT]
            for d in range(KT):
                if d >= 2:
                    pe.wait_ge(proj_read, d - 1)
                for k in range(N_BRANCH):
                    w = mixer_unit(BRANCH_UNIT0 + N_BRANCH * (d // 4) + k, d % 4 == 0)
                    w = w.rearrange("p (c n) -> p c n", c=4)
                    for c in range(CT):
                        last = nc.tensor.matmul(quarter(2 * (d % 2))[:, k, :], w[:, c, (d % 4) * P:(d % 4 + 1) * P],
                                                branch[k][:, c, :], start=(c == 0), stop=(c == CT - 1))
                    if d % 4 == 3:
                        last.then_inc(w_used, 1)
                if d % 4 != 3:
                    last.then_inc(proj_done, 1)
            for d in range(KT):
                pe.wait_ge(merged_ready, d + 1)
                w = mixer_unit(OUT_UNIT0 + d // 2, d % 2 == 0).rearrange("p (c n) -> p c n", c=2)
                for a in range(TT):
                    for h in range(2):
                        last = nc.tensor.matmul(ps[:, 4 + 2 * a + h, :], hT[:, d, a * P:(a + 1) * P],
                                                w[:, d % 2, h * 512:(h + 1) * 512], start=(d == 0),
                                                stop=(d == KT - 1))
                if d % 2:
                    last.then_inc(w_used, 1)

            transpose_xs(2, 4)
            for a in range(TT):
                for k in range(KT):
                    last = nc.tensor.matmul(ps[:, 0, N_EXP * a:N_EXP * (a + 1)], hT[:, k, a * P:(a + 1) * P],
                                            rw[:, k, :], start=(k == 0), stop=(k == KT - 1))
            last.then_inc(logits_done, 1)
            pe.wait_ge(chosen_ready, 1)
            nc.tensor.matmul(ps[:, 1, 0:N_EXP], before[:, :], chosen[:, 0, :], start=True, stop=True)
            nc.tensor.matmul(ps[:, 1, N_EXP:2 * N_EXP], ones[:, :], chosen[:, 0, :], start=True, stop=False)
            nc.tensor.matmul(ps[:, 1, N_EXP:2 * N_EXP], before[:, :], chosen[:, 1, :], start=False, stop=True)
            nc.tensor.matmul(ps[:, 1, 2 * N_EXP:3 * N_EXP], ones[:, :], chosen[:, 0, :], start=True, stop=False)
            nc.tensor.matmul(ps[:, 1, 2 * N_EXP:3 * N_EXP], ones[:, :], chosen[:, 1, :], start=False,
                             stop=True).then_inc(pos_done, 1)

            def gather(q, b):
                pe.wait_ge(select_ready, q + 1)
                wait_past(pe, xe_ready, q)
                for k in range(KT):
                    for a in range(TT):
                        last = nc.tensor.matmul(ps[:, GATHER, k * SLOTS:(k + 1) * SLOTS],
                                                xs[:, a, k * P:(k + 1) * P], select[:, b, a, :],
                                                start=(a == 0), stop=(a == TT - 1))
                last.then_inc(gather_done, 1)

            gather(0, 0)
            pe.wait_ge(gates_ready, 1)
            for a in range(TT):
                last = nc.tensor.transpose(ps[0:N_EXP, WT, a * P:(a + 1) * P], gate_w[:, a, 0:N_EXP], ident[:, :])
            last.then_inc(gateT_done, 1)
            pe.wait_ge(gateT_ready, 1)
            pe.wait_ge(bdown_loaded, 16)
            for a in range(TT):
                for h in range(2):
                    last = nc.tensor.matmul(ps[:, 4 + 2 * a + h, :], gateT[:, a * P:(a + 1) * P],
                                            b_down[:, h * 512:(h + 1) * 512], start=True, stop=True)
            last.then_inc(bdown_done, 1)
            pe.wait_ge(bdown_added, 1)
            pe.wait_ge(bup_loaded, 64)

            def expert(q, j, turn, first=False):
                pe.wait_ge(xe_ready, q + 1)
                wait_past(pe, lin_ready, q)
                for k in range(UP_UNITS):
                    slot = UP_UNITS * j + k
                    pe.wait_ge(up_loaded[slot], 16 * turn + up_value(slot, 1))
                    for part in range(2):
                        for g in range(2):
                            last = nc.tensor.matmul(ps[64 * g:64 * g + 64, GLU + part, :], xe[:, j, k, :],
                                                    up_ring[:, slot, D * part + 512 * g:D * part + 512 * (g + 1)],
                                                    start=(k == 0), stop=False)
                    last.then_inc(w_used, 1)
                pe.wait_ge(pick_ready, q + 1)
                for part in range(2):
                    for g in range(2):
                        last = nc.tensor.matmul(ps[64 * g:64 * g + 64, GLU + part, :],
                                                pick_bias[:, 2 * part + g, :], b_up, start=False, stop=True)
                last.then_inc(up_done, 1)
                if not first:
                    pe.wait_ge(y_ready, q)
                    pe.wait_ge(weightT_ready, q)
                    to_tokens(q - 1, 0)
                gather(q + 1, 1 - j)
                pe.wait_ge(weight_ready, q + 1)
                wait_past(pe, weightT_ready, q)
                for a in range(TT):
                    last = nc.tensor.transpose(ps[:, WT, a * P:(a + 1) * P], weight[:, a, :], ident[:, :])
                last.then_inc(weightT_done, 1)
                pe.wait_ge(prod_ready, 2 * q + 2)
                wait_past(pe, actT_ready, q)
                for m in range(4):
                    last = nc.tensor.transpose(ps[:, ACTT, m * P:(m + 1) * P], lin[:, m * P:(m + 1) * P], ident[:, :])
                last.then_inc(actT_done, 1)
                if not first:
                    to_tokens(q - 1, 1)
                pe.wait_ge(actT_ready, q + 1)
                wait_past(pe, y_ready, q)
                for k in range(KT):
                    c = k // 2
                    if k % 2 == 0:
                        pe.wait_ge(down_loaded[c], 16 * q + 16)
                    for g in range(2):
                        col = D * (k % 2) + 512 * g
                        last = nc.tensor.matmul(ps[64 * g:64 * g + 64, Y, :], actT[:, k % 4, k // 4, :],
                                                down_ring[:, c, col:col + 512], start=(k == 0), stop=(k == KT - 1))
                    if k % 2:
                        last.then_inc(w_used, 1)

            def to_tokens(q, a):
                wait_past(pe, x_added, 2 * q + a)
                for g in range(2):
                    last = nc.tensor.matmul(ps[:, COMB + g, :], weightT[64 * g:64 * g + 64, a, :],
                                            y_sb[64 * g:64 * g + 64, :], start=True, stop=True)
                last.then_inc(comb_done, 1)

            def last_to_tokens(q):
                pe.wait_ge(y_ready, q + 1)
                pe.wait_ge(weightT_ready, q + 1)
                for a in range(TT):
                    to_tokens(q, a)

            for q in range(2):
                expert(q, q, 0, first=q == 0)
            with pe.Fori(1, N_EXP // 2) as i:
                for j in range(2):
                    expert(2 * i + j, j, i)
            pe.wait_ge(flag_ready, 1)
            overflow = pe.value_load(flag[0:1, 0:1], min_val=0, max_val=1)
            with pe.If(overflow > 0):
                with pe.Fori(N_EXP // 2, ROUNDS * N_EXP // 2) as i:
                    for j in range(2):
                        expert(2 * i + j, j, i)
                last_to_tokens(ROUNDS * N_EXP - 1)
            with pe.If(overflow < 1):
                last_to_tokens(N_EXP - 1)

            pe.wait_ge(x_ready, 2)
            pe.wait_ge(ple_loaded, 16 * 5)
            wp = up_ring[:, 4, :].rearrange("p (c n) -> p c n", c=2)
            for a in range(TT):
                for h in range(2):
                    for k in range(PLE // P):
                        last = nc.tensor.matmul(ps[:, 4 + 2 * a + h, :], pT[:, k, a * P:(a + 1) * P],
                                                wp[:, k, h * 512:(h + 1) * 512], start=(k == 0),
                                                stop=(k == PLE // P - 1))
            transpose_xs(3, 0)
            for a in range(TT):
                for h in range(2):
                    for k in range(KT):
                        wg = up_ring[:, k // 2, :].rearrange("p (c n) -> p c n", c=2)
                        last = nc.tensor.matmul(ps[:, 2 * a + h, :], hT[:, k, a * P:(a + 1) * P],
                                                wg[:, k % 2, h * 512:(h + 1) * 512], start=(k == 0),
                                                stop=(k == KT - 1))
                    last.then_inc(ple_gate_done, 1)


_INS = ["x", "p", "mix_norm", "w_in", "b_in", "pool_w", "pool_scale", "conv_w", "conv_b", "conv_norm_g",
        "conv_norm_b", "sgu_norm_g", "sgu_norm_b", "sgu_w", "sgu_b", "branch_w", "branch_b", "w_out",
        "moe_norm", "router_w", "router_b", "expert_w_up", "expert_b_up", "expert_w_down",
        "expert_b_down", "ple_norm", "ple_gate_w", "ple_proj_w", "final_norm"]


def kernel(**inputs):
    import numpy as np
    import concourse.bacc as bacc
    from concourse.bass_utils import run_bass_kernel_spmd

    nc = bacc.Bacc("TRN2", target_bir_lowering=False, num_devices=1)
    arrays, args = {}, []
    for name in _INS:
        a = np.ascontiguousarray(inputs[name])
        arrays[f"in_{name}_dram"] = a
        args.append(nc.dram_tensor(f"in_{name}_dram", a.shape, mybir.dt.from_np(a.dtype),
                                   kind="ExternalInput").ap())
    args.append(nc.dram_tensor("out_dram", (1, T, D), F32, kind="ExternalOutput").ap())
    build(nc, *args)
    return run_bass_kernel_spmd(nc, [arrays], core_ids=[0]).results[0]["out_dram"]
```

```python
from contextlib import ExitStack

import concourse.bass as bass
from concourse import mybir

F32 = mybir.dt.float32
F32R = mybir.dt.float32r
I32 = mybir.dt.int32
U32 = mybir.dt.uint32
ALU = mybir.AluOpType
ACT = mybir.ActivationFunctionType
AX = mybir.AxisListType.X

P = 128
T = 256
TT = T // P
D = 1024
KT = D // P
CH = 512
CT = CH // P
CONV_K = 31
POOL_PAD = 16
N_EXP = 32
TOP_K = 4
SLOTS = 64
ROUNDS = T // SLOTS
N_BRANCH = 3
PLE = 256
EPS = 1e-6
LIMIT = 7.0
ALPHA = 1.702

UNIT = 2048
UP_SLOTS, DOWN_SLOTS = 16, 4
UP_UNITS, DOWN_UNITS = 8, 4
PER_EXPERT = UP_UNITS + DOWN_UNITS
MIX_SLOTS = 8
HI_SLOT, HI_BUFS = 8, 3
H_LO_SLOT = 11
TEMP_SLOT = 12

CHUNKS = [("gate", 1024), ("a", 512), ("pool", 0), ("v", 2048), ("u", 1536)] + \
         [("g", 2560 + CH * g) for g in range(N_BRANCH * D // CH)]
N_CHUNKS = len(CHUNKS)
MIX_UNITS = 2 * N_CHUNKS + 2 * N_BRANCH + KT // 2
BRANCH_UNIT0 = 2 * N_CHUNKS
OUT_UNIT0 = BRANCH_UNIT0 + 2 * N_BRANCH

PARAMS = [("mix_norm", 8), ("b_in", 44), ("pool_scale", 4), ("conv_b", 4), ("conv_norm_g", 4),
          ("conv_norm_b", 4), ("branch_b", 24), ("moe_norm", 8), ("ple_norm", 8)]
ROW = {}
N_ROWS = 0
for _name, _rows in PARAMS:
    ROW[_name] = N_ROWS
    N_ROWS += _rows


def mix_slot(unit):
    return unit % MIX_SLOTS, unit // MIX_SLOTS + 1


def lo_by_gpsimd(unit):
    return unit >= MIX_SLOTS and unit % HI_BUFS == 2


def lo_count(unit, gpsimd):
    return sum(lo_by_gpsimd(u) == gpsimd for u in range(unit + 1))


CONV_UNIT = 6
CONV_TAPS = [2, 2, 3, 2, 2, 3, 2, 2, 3, 2, 2, 3, 2]
assert sum(CONV_TAPS) == CONV_K - 1


MIX_USES = [sum(mix_slot(u)[0] == s for u in range(MIX_UNITS)) for s in range(UP_SLOTS)]


def build(nc, x, p, mix_norm, w_in, b_in, pool_w, pool_scale, conv_w, conv_b, conv_norm_g,
          conv_norm_b, sgu_norm_g, sgu_norm_b, sgu_w, sgu_b, branch_w, branch_b, w_out, moe_norm,
          router_w, router_b, expert_w_up, expert_b_up, expert_w_down, expert_b_down, ple_norm,
          ple_gate_w, ple_proj_w, final_norm, out):
    with ExitStack() as ctx:
        def sb(name, shape, dt=F32):
            return ctx.enter_context(nc.sbuf_tensor(name, shape, dt))

        def sem(name):
            return ctx.enter_context(nc.semaphore(name))

        up_ring = sb("up_ring", [P, UP_SLOTS, UNIT])
        ring_at = nc.sbuf_base - UP_SLOTS * UNIT * 4
        down_ring = sb("down_ring", [P, DOWN_SLOTS, UNIT])
        x_sb = sb("x_sb", [P, TT, D])
        xs = sb("xs", [P, TT, D])
        hT = sb("hT", [P, KT, T])
        hT_at = nc.sbuf_base - KT * T * 4
        h_hi = nc.alloc_sbuf_tensor_at("h_hi", [P, KT, T], F32R, offset=hT_at)
        h_lo = nc.alloc_sbuf_tensor_at("h_lo", [P, KT, T], F32R, offset=ring_at + H_LO_SLOT * UNIT * 4)
        w_hi = nc.alloc_sbuf_tensor_at("w_hi", [P, HI_BUFS, UNIT], F32R, offset=ring_at + HI_SLOT * UNIT * 4)
        w_lo = nc.alloc_sbuf_tensor_at("w_lo", [P, MIX_SLOTS, UNIT], F32R, offset=ring_at)
        work = sb("work", [P, 6 * 512])
        ident = sb("ident", [P, P])
        ones = sb("ones", [P, P])
        mean_mat = sb("mean_mat", [P, P])
        before = sb("before", [P, P])
        slot_ids = sb("slot_ids", [P, 2, SLOTS])
        prm = sb("prm", [P, N_ROWS])
        conv_taps = sb("conv_taps", [P, CONV_K, CT])
        pool_mix = sb("pool_mix", [P, CT, P])
        pT = sb("pT", [P, PLE // P, T])
        rw = sb("rw", [P, KT, N_EXP])
        rb = sb("rb", [P, N_EXP])
        QPAD = ROUNDS * N_EXP + 2
        pos = sb("pos", [P, TT, QPAD])
        gate_w = sb("gate_w", [P, TT, QPAD])
        small = sb("small", [P, 64])
        flag = sb("flag", [P, 2], I32)
        fold = sb("fold", [P, N_EXP])

        eps = small[:, 0:1]
        ssq = small[:, 1:3]
        rms = small[:, 3:5]
        rstd = small[:, 5:7]
        vstat = small[:, 8:20]
        vmv = small[:, 20:24]
        vrms = small[:, 24:26]
        vrstd = small[:, 26:28]
        wsum = small[:, 28:30]
        wrec = small[:, 30:32]
        most = small[:, 32:33]
        half_ssq = small[:, 36:40]
        frstd = small[:, 40:42]

        spare = up_ring[:, TEMP_SLOT:, :].rearrange("p a b -> p (a b)")
        PW = POOL_PAD + T
        z_pool = spare[:, 0:4 * PW].rearrange("p (g t) -> p g t", g=4)
        sum2 = spare[:, 1088:2176].rearrange("p (g t) -> p g t", g=4)
        sum4 = spare[:, 2176:2992].rearrange("p (g t) -> p g t", g=3)
        sum8 = spare[:, 2992:3536].rearrange("p (g t) -> p g t", g=2)
        sum16 = spare[:, 3536:3808].rearrange("p (g t) -> p g t", g=1)
        inv_count = spare[:, 3808:4832].rearrange("p (g t) -> p g t", g=4)
        pooled = spare[:, 4832:5856].rearrange("p (g t) -> p g t", g=4)
        yaT = spare[:, 5856:6880].rearrange("p (g t) -> p g t", g=4)
        p_sb = spare[:, 5856:6368].rearrange("p (a b) -> p a b", a=TT)
        sguT = spare[:, 6880:7392].rearrange("p (h t) -> p h t", h=4)
        sgub = spare[:, 7392:7904].rearrange("p (h t) -> p h t", h=4)
        squares = spare[:, 1088:2112].rearrange("p (g t) -> p g t", g=4)
        sgu_mix = spare[:, 2176:3200].rearrange("p (g t) -> p g t", g=4)
        gated = spare[:, 0:768].rearrange("p (g t) -> p g t", g=3)
        spare_d = down_ring[:, :, :].rearrange("p a b -> p (a b)")
        gates = spare_d[:, 0:6144].rearrange("p (k c t) -> p k c t", k=N_BRANCH, c=KT)
        CW = CONV_K - 1 + T
        y_pad = spare_d[:, 6144:6144 + 4 * CW].rearrange("p (c t) -> p c t", c=CT)
        conv_rstd = spare_d[:, 7288:7544]
        prm_rows = spare_d[:, 7544:7672]
        tap_rows = spare_d[:, 7672:7800]
        convT = xs[:, 0, :].rearrange("p (c t) -> p c t", c=CT)
        uT = xs[:, 1, :].rearrange("p (c t) -> p c t", c=CT)
        v_sb = work[:, 0:1024].rearrange("p (n c) -> p n c", n=TT)
        v_bias = work[:, 1024:1536]
        v_gain = work[:, 1536:2048]
        v_shift = work[:, 2048:2560]
        sgu_in = work[:, 2560:3072].rearrange("p (h t) -> p h t", h=4)
        sig_gate = pooled

        onehot = work[:, 1024:1280].rearrange("p (a j e) -> p a j e", a=TT, j=TOP_K)
        weighted = work[:, 1280:1536].rearrange("p (a j e) -> p a j e", a=TT, j=TOP_K)
        logits = work[:, 2304:2368].rearrange("p (a e) -> p a e", a=TT)
        chosen = work[:, 2368:2432].rearrange("p (a e) -> p a e", a=TT)
        pos0 = work[:, 2432:2496].rearrange("p (a e) -> p a e", a=TT)
        top = work[:, 2496:2512].rearrange("p (a e) -> p a e", a=TT)
        top_i = work[:, 2512:2528].bitcast(U32).rearrange("p (a e) -> p a e", a=TT)
        top_f = work[:, 2528:2544].rearrange("p (a e) -> p a e", a=TT)
        top_e = work[:, 2544:2552].rearrange("p (a e) -> p a e", a=TT)
        gateT = work[0:N_EXP, 2560:2816]
        partial = work[:, 2816:3072]

        glu = work[:, 0:512]
        lin = work[:, 512:1024]
        sig = work[:, 1024:1536]
        b_up = work[:, 1536:2048]
        select = work[:, 2048:2304].rearrange("p (b a s) -> p b a s", b=2, a=TT)
        weight = work[:, 2304:2560].rearrange("p (a s) -> p a s", a=TT)
        weightT = work[:, 2560:2816].rearrange("p (a t) -> p a t", a=TT)
        pick_bias = work[:, 2816:3072].rearrange("p (c s) -> p c s", c=4)
        hT_flat = hT[:, :, :].rearrange("p a b -> p (a b)")
        xe = hT_flat[:, 0:1024].rearrange("p (b k s) -> p b k s", b=2, k=KT)
        actT = hT_flat[:, 1024:1536].rearrange("p (m g s) -> p m g s", m=4, g=2)
        y_sb = hT_flat[:, 1536:2048]
        b_down = [pool_mix[0:N_EXP, :, :].rearrange("p a b -> p (a b)"), y_sb[0:N_EXP, :]]
        ident_e = ident[:, :].rearrange("p (c e) -> p c e", c=4)

        ple_sig = up_ring[:, 8:9, :].rearrange("p a (b c) -> p (a b) c", b=TT)
        final_out = up_ring[:, 9:10, :].rearrange("p a (b c) -> p (a b) c", b=TT)
        final_gain = work[:, 0:1024]

        ps = ctx.enter_context(nc.psum_tensor("ps", [P, 8, 512], F32))
        GLU, LIN, GATHER, ACTT, WT, Y, COMB = 0, 1, 2, 3, 4, 5, 6

        def quarter(bank, n=4):
            return ps[:, bank:bank + 2, :].rearrange("p a (b t) -> p (a b) t", t=T)[:, 0:n, :]

        x_loaded = sem("x_loaded")
        rows_loaded = sem("rows_loaded")
        p_loaded = sem("p_loaded")
        sgu_loaded = sem("sgu_loaded")
        vbc_loaded = sem("vbc_loaded")
        mats_loaded = sem("mats_loaded")
        bdown_loaded = sem("bdown_loaded")
        bup_loaded = sem("bup_loaded")
        gain_loaded = sem("gain_loaded")
        up_loaded = [sem(f"up_loaded{s}") for s in range(UP_SLOTS)]
        down_loaded = [sem(f"down_loaded{s}") for s in range(DOWN_SLOTS)]
        w_used = sem("w_used")
        consts_ready = sem("consts_ready")
        pool_order = sem("pool_order")
        dve_order = sem("dve_order")
        act_order = sem("act_order")
        eps_ready = sem("eps_ready")
        sgu_masked = sem("sgu_masked")
        rowsT_done = sem("rowsT_done")
        prm_ready = sem("prm_ready")
        taps_ready = sem("taps_ready")
        pT_done = sem("pT_done")
        sguT_done = sem("sguT_done")
        sguT_ready = sem("sguT_ready")
        x_ready = sem("x_ready")
        x_final = sem("x_final")
        rstd_ready = sem("rstd_ready")
        rms_ready = sem("rms_ready")
        xs_ready = sem("xs_ready")
        xsT_done = sem("xsT_done")
        hT_act = sem("hT_act")
        hT_dve = sem("hT_dve")
        h_lo_ready = sem("h_lo_ready")
        w_hi_ready = sem("w_hi_ready")
        w_lo_dve = sem("w_lo_dve")
        w_lo_pool = sem("w_lo_pool")
        chunk_read = sem("chunk_read")
        a_read = sem("a_read")
        conv_step = sem("conv_step")
        y_pad_ready = sem("y_pad_ready")
        pool_sums_free = sem("pool_sums_free")
        inv_ready = sem("inv_ready")
        count_ready = sem("count_ready")
        pooled_ready = sem("pooled_ready")
        pool_mixed = sem("pool_mixed")
        yaT_ready = sem("yaT_ready")
        v_rms_ready = sem("v_rms_ready")
        v_var_ready = sem("v_var_ready")
        v_ready = sem("v_ready")
        sgu_done = sem("sgu_done")
        ycT_ready = sem("ycT_ready")
        mean_done = sem("mean_done")
        centred = sem("centred")
        sq_ready = sem("sq_ready")
        var_done = sem("var_done")
        conv_rms_ready = sem("conv_rms_ready")
        conv_normed = sem("conv_normed")
        ybT_ready = sem("ybT_ready")
        proj_done = sem("proj_done")
        proj_read = sem("proj_read")
        merged_ready = sem("merged_ready")
        fold_ready = sem("fold_ready")
        partial_done = sem("partial_done")
        partial_ready = sem("partial_ready")
        logits_done = sem("logits_done")
        top_ready = sem("top_ready")
        top_exp = sem("top_exp")
        chosen_ready = sem("chosen_ready")
        pos_done = sem("pos_done")
        totals_done = sem("totals_done")
        gates_ready = sem("gates_ready")
        gateT_done = sem("gateT_done")
        gateT_ready = sem("gateT_ready")
        bdown_done = sem("bdown_done")
        bdown_added = sem("bdown_added")
        flag_ready = sem("flag_ready")
        select_ready = sem("select_ready")
        gather_done = sem("gather_done")
        xe_ready = sem("xe_ready")
        pick_ready = sem("pick_ready")
        weight_ready = sem("weight_ready")
        weightT_done = sem("weightT_done")
        weightT_ready = sem("weightT_ready")
        up_done = sem("up_done")
        glu_ready = sem("glu_ready")
        lin_ready = sem("lin_ready")
        sig_ready = sem("sig_ready")
        prod_ready = sem("prod_ready")
        act_ready = sem("act_ready")
        actT_done = sem("actT_done")
        actT_ready = sem("actT_ready")
        y_ready = sem("y_ready")
        comb_done = sem("comb_done")
        x_added = sem("x_added")
        ple_loaded = sem("ple_loaded")
        ple_proj_done = sem("ple_proj_done")
        ple_gate_done = sem("ple_gate_done")
        ple_sig_ready = sem("ple_sig_ready")
        ple_x_ready = sem("ple_x_ready")
        final_rms = sem("final_rms")
        final_ready = sem("final_ready")
        stored = sem("stored")

        mixer_small = {"mix_norm": mix_norm, "b_in": b_in, "pool_scale": pool_scale, "conv_b": conv_b,
                       "conv_norm_g": conv_norm_g, "conv_norm_b": conv_norm_b, "branch_b": branch_b,
                       "moe_norm": moe_norm, "ple_norm": ple_norm}

        def rows128(ap):
            if len(ap.shape) == 3:
                ap = ap.rearrange("a b c -> a (b c)")
            return ap.rearrange("a (r c) -> (a r) c", c=P)

        def on_all(ap_row):
            return ap_row.partition_broadcast(P)

        def wait_past(eng, semaphore, value):
            if isinstance(value, int) and value <= 0:
                return
            eng.wait_ge(semaphore, value)

        def used_before(q):
            return MIX_UNITS + PER_EXPERT * q

        def comb_before(q):
            return TT * (q + 1)

        def up_value(slot, turn):
            return 16 * (MIX_USES[slot] + turn)

        def w_lo_part(engine, unit):
            slot = mix_slot(unit)[0]
            return engine.tensor_tensor(w_lo[:, slot, :], up_ring[:, slot, :],
                                        w_hi[:, unit % HI_BUFS, :].bitcast(F32), ALU.subtract)

        block = ctx.enter_context(nc.Block())

        @block.sync
        def _(sp):
            sp.dma_start(x_sb[:, :, :], x[0].rearrange("(a p) d -> p a d", p=P)).then_inc(x_loaded, 16)
            for name, _ in PARAMS:
                rows = rows128(mixer_small[name])
                sp.dma_start(prm_rows[ROW[name]:ROW[name] + rows.shape[0], :], rows).then_inc(rows_loaded, 16)
            sp.dma_start(tap_rows[0:CONV_K * CT, :], conv_w[0].rearrange("k (c n) -> (k c) n", n=P)
                          ).then_inc(rows_loaded, 16)

            def mix_source(u):
                if u < BRANCH_UNIT0:
                    col = CHUNKS[u // 2][1]
                    col += (u % 2) * 256
                    return w_in[0, :, col:col + 256].rearrange("(c p) n -> p c n", p=P)
                if u < OUT_UNIT0:
                    half, br = divmod(u - BRANCH_UNIT0, N_BRANCH)
                    return branch_w[0, br, :, half * 512:(half + 1) * 512].rearrange("(c p) n -> p c n", p=P)
                m = u - OUT_UNIT0
                return w_out[0, m * 256:(m + 1) * 256, :].rearrange("(c p) n -> p c n", p=P)

            def load_up(j, c, e):
                sp.dma_start(up_ring[:, UP_UNITS * j + c, :],
                             up_rows(e)[:, c, :]).then_inc(up_loaded[UP_UNITS * j + c], 16)

            def up_rows(e):
                return expert_w_up[0, bass.ds(e, 1)].rearrange("a (c p) n -> p (a c) n", p=P)

            def load_down(c, e):
                rows = expert_w_down[0, bass.ds(e, 1)].rearrange("a (c p) n -> p (a c) n", p=P)
                sp.dma_start(down_ring[:, c, :].rearrange("p (c n) -> p c n", c=2),
                             rows[:, 2 * c:2 * c + 2, :]).then_inc(down_loaded[c], 16)

            for u in range(MIX_UNITS):
                if u == 2:
                    sp.wait_ge(mats_loaded, 48)
                if u == MIX_UNITS - 2:
                    sp.wait_ge(w_used, BRANCH_UNIT0)
                    for c in range(HI_SLOT, TEMP_SLOT):
                        load_up(1, c - UP_UNITS, 1)
                if u >= MIX_SLOTS:
                    sp.wait_ge(w_used, u - MIX_SLOTS + 1)
                slot = mix_slot(u)[0]
                src = mix_source(u)
                dst = up_ring[:, slot, :].rearrange("p (c n) -> p c n", c=src.shape[1])
                sp.dma_start(dst, src).then_inc(up_loaded[slot], 16)

            for c in range(MIX_SLOTS):
                sp.wait_ge(w_used, MIX_UNITS - MIX_SLOTS + c + 1)
                load_up(0, c, 0)
                if c == 3:
                    sp.wait_ge(merged_ready, KT)
                    for c4 in range(DOWN_UNITS):
                        load_down(c4, 0)
                if c == 6:
                    for c4 in range(TEMP_SLOT, UP_SLOTS):
                        load_up(1, c4 - UP_UNITS, 1)
            with sp.Fori(1, N_EXP // 2) as i:
                for j in range(2):
                    for c in range(UP_UNITS):
                        sp.wait_ge(w_used, used_before(2 * i + j - 2) + c + 1)
                        load_up(j, c, 2 * i + j)
                    for c in range(DOWN_UNITS):
                        sp.wait_ge(w_used, used_before(2 * i + j - 2) + UP_UNITS + c + 1)
                        load_down(c, 2 * i + j - 1)
            for c in range(DOWN_UNITS):
                sp.wait_ge(w_used, used_before(N_EXP - 2) + UP_UNITS + c + 1)
                load_down(c, N_EXP - 1)

            sp.wait_ge(flag_ready, 1)
            overflow = sp.value_load(flag[0:1, 0:1], min_val=0, max_val=1)
            with sp.If(overflow > 0):
                with sp.Fori(1, ROUNDS) as r:
                    with sp.Fori(0, N_EXP // 2) as i:
                        for j in range(2):
                            q = N_EXP * r + 2 * i + j
                            for c in range(UP_UNITS):
                                sp.wait_ge(w_used, used_before(q - 2) + c + 1)
                                load_up(j, c, 2 * i + j)
                            for c in range(DOWN_UNITS):
                                sp.wait_ge(w_used, used_before(q - 1) + UP_UNITS + c + 1)
                                load_down(c, 2 * i + j)
                sp.wait_ge(w_used, used_before(ROUNDS * N_EXP))
            sp.wait_ge(w_used, used_before(N_EXP - 2) + UP_UNITS)
            sp.dma_start(up_ring[:, 4, :].rearrange("p (c n) -> p c n", c=2),
                         ple_proj_w[0].rearrange("(c p) n -> p c n", p=P)).then_inc(ple_loaded, 16)
            for m in range(4):
                sp.dma_start(up_ring[:, m, :].rearrange("p (c n) -> p c n", c=2),
                             ple_gate_w[0, m * 256:(m + 1) * 256, :].rearrange("(c p) n -> p c n", p=P)
                             ).then_inc(ple_loaded, 16)
            for a in range(TT):
                for h in range(2):
                    sp.wait_ge(final_ready, 2 * a + h + 1)
                    sp.dma_start(out[0, a * P:(a + 1) * P, h * 512:(h + 1) * 512],
                                 final_out[:, a, h * 512:(h + 1) * 512]).then_inc(stored, 16)
            sp.wait_ge(stored, 16 * 2 * TT)

        @block.gpsimd
        def _(pool):
            nc.gpsimd.memset(ident[:, :], 0.0).then_inc(pool_order, 1)
            nc.gpsimd.memset(before[:, :], 1.0).then_inc(pool_order, 1)
            nc.gpsimd.memset(ones[:, :], 1.0).then_inc(consts_ready, 1)
            nc.gpsimd.memset(mean_mat[:, :], 1.0 / CH).then_inc(consts_ready, 1)
            nc.gpsimd.iota(slot_ids[:, :, :], [[0, 2], [1, SLOTS]], base=0, channel_multiplier=0,
                           allow_small_or_imprecise_dtypes=True).then_inc(consts_ready, 1)
            nc.gpsimd.memset(z_pool[:, :, 0:POOL_PAD], 0.0).then_inc(consts_ready, 1)
            nc.gpsimd.memset(y_pad[:, :, 0:CONV_K - 1], 0.0).then_inc(consts_ready, 1)
            pool.wait_ge(pool_order, 2)
            nc.gpsimd.affine_select(out=ident[:, :], in_=ident[:, :], compare_op=ALU.not_equal, fill=1.0,
                                    base=0, pattern=[[-1, P]], channel_multiplier=1).then_inc(consts_ready, 1)
            nc.gpsimd.affine_select(out=before[:, :], in_=before[:, :], compare_op=ALU.is_gt, fill=0.0,
                                    base=0, pattern=[[1, P]], channel_multiplier=-1).then_inc(consts_ready, 1)
            pool.dma_start(sgu_in[:, :, :], sgu_w[0].rearrange("h t s -> t h s")).then_inc(sgu_loaded, 16)
            pool.dma_start(sgub[:, :, :], on_all(sgu_b[0])).then_inc(sgu_loaded, 16)
            pool.dma_start(p_sb[:, :, :], p[0, 0].rearrange("(a p) d -> p a d", p=P)).then_inc(p_loaded, 16)
            pool.dma_start(v_bias, on_all(b_in[0, 2048:2560])).then_inc(vbc_loaded, 16)
            pool.dma_start(v_gain, on_all(sgu_norm_g[0])).then_inc(vbc_loaded, 16)
            pool.dma_start(v_shift, on_all(sgu_norm_b[0])).then_inc(vbc_loaded, 16)
            pool.dma_start(pool_mix[:, :, :], pool_w[0].rearrange("g c d -> c g d")).then_inc(mats_loaded, 16)
            pool.dma_start(rw[:, :, :], router_w[0].rearrange("(c p) e -> p c e", p=P)).then_inc(mats_loaded, 16)
            pool.dma_start(rb[:, :], on_all(router_b[0])).then_inc(mats_loaded, 16)
            pool.wait_ge(sgu_loaded, 32)
            nc.gpsimd.affine_select(out=sgu_in[:, :, :], in_=sgu_in[:, :, :], compare_op=ALU.is_ge, fill=0.0,
                                    base=0, pattern=[[0, 4], [-1, P]], channel_multiplier=1).then_inc(sgu_masked, 1)
            nc.gpsimd.iota(inv_count[:, :, :], [[0, 4], [1, T]], base=1, channel_multiplier=0,
                           allow_small_or_imprecise_dtypes=True).then_inc(pool_order, 1)
            pool.wait_ge(pool_order, 3)
            for g in range(4):
                last = nc.gpsimd.tensor_scalar(inv_count[:, g, :], inv_count[:, g, :], float(2 << g), None, ALU.min)
            last.then_inc(count_ready, 1)

            def split(u):
                pool.wait_ge(w_hi_ready, u + 1)
                w_lo_part(nc.gpsimd, u).then_inc(w_lo_pool, 1)

            split(8)
            pool.wait_ge(chunk_read, 2)
            nc.gpsimd.tensor_tensor(sum2[:, :, 1:PW], z_pool[:, :, 1:PW], z_pool[:, :, 0:PW - 1],
                                    ALU.add).then_inc(pool_order, 1)
            pool.wait_ge(pool_order, 4)
            nc.gpsimd.tensor_tensor(sum4[:, :, 3:PW], sum2[:, 1:4, 3:PW], sum2[:, 1:4, 1:PW - 2],
                                    ALU.add).then_inc(pool_order, 1)
            pool.wait_ge(pool_order, 5)
            nc.gpsimd.tensor_tensor(sum8[:, :, 7:PW], sum4[:, 1:3, 7:PW], sum4[:, 1:3, 3:PW - 4],
                                    ALU.add).then_inc(pool_order, 1)
            pool.wait_ge(pool_order, 6)
            nc.gpsimd.tensor_tensor(sum16[:, :, 15:PW], sum8[:, 1:2, 15:PW], sum8[:, 1:2, 7:PW - 8],
                                    ALU.add).then_inc(pool_order, 1)
            pool.wait_ge(pool_order, 7)
            pool.wait_ge(inv_ready, 1)
            pool.wait_ge(a_read, 1)
            for g, s in enumerate((sum2, sum4, sum8, sum16)):
                nc.gpsimd.tensor_tensor(pooled[:, g, :], s[:, 0, POOL_PAD:PW], inv_count[:, g, :],
                                        ALU.mult).then_inc(pool_order, 1)
            pool.wait_ge(pool_order, 11)
            nc.gpsimd.tensor_tensor(pooled[:, :, :], pooled[:, :, :], z_pool[:, :, POOL_PAD:PW],
                                    ALU.subtract).then_inc(pooled_ready, 1)
            for u in range(MIX_SLOTS + 1, BRANCH_UNIT0):
                if lo_by_gpsimd(u):
                    split(u)

        @block.scalar
        def _(act):
            steps = [0]

            def own(ins):
                steps[0] += 1
                ins.then_inc(act_order, 1)
                act.wait_ge(act_order, steps[0])

            def square_sum(a):
                own(nc.scalar.activation(xs[:, a, :], x_sb[:, a, :], ACT.Square, accum_out=ssq[:, a:a + 1]))

            def root():
                return nc.scalar.activation(rms, ssq, ACT.Sqrt, bias=eps, scale=1.0 / D)

            def scale_high(bank, gain, dst=hT):
                for k in range(4, KT):
                    last = nc.scalar.activation(dst[:, k, :], ps[:, bank + k // 2, 256 * (k % 2):256 * (k % 2) + 256], ACT.Copy,
                                                scale=prm[:, gain + k:gain + k + 1])
                last.then_inc(hT_act, 1)

            act.wait_ge(eps_ready, 1)
            nc.scalar.activation(small[:, 34:35], eps, ACT.Sqrt)
            act.wait_ge(x_loaded, 16)
            for a in range(TT):
                square_sum(a)
            root().then_inc(rms_ready, 1)

            def split(u):
                slot, turn = mix_slot(u)
                act.wait_ge(up_loaded[slot], 16 * turn)
                if u >= HI_BUFS:
                    act.wait_ge(w_used, u - HI_BUFS + 1)
                nc.scalar.activation(w_hi[:, u % HI_BUFS, :], up_ring[:, slot, :], ACT.Copy
                                     ).then_inc(w_hi_ready, 1)

            act.wait_ge(xsT_done, 1)
            act.wait_ge(prm_ready, 1)
            scale_high(4, ROW["mix_norm"], h_hi)
            for u in range(HI_BUFS):
                split(u)

            act.wait_ge(consts_ready, 7)
            for n, (name, col) in enumerate(CHUNKS):
                if 2 * n + 3 < BRANCH_UNIT0:
                    split(2 * n + 3)
                if n == 9:
                    act.wait_ge(v_var_ready, 1)
                    nc.scalar.activation(vrms, vmv.rearrange("p (a b) -> p a b", b=2)[:, :, 1], ACT.Sqrt,
                                         bias=eps).then_inc(v_rms_ready, 1)
                    act.wait_ge(centred, 1)
                    nc.scalar.activation(squares[:, :, :], convT[:, :, :], ACT.Square).then_inc(sq_ready, 1)
                act.wait_ge(w_used, 2 * n + 2)
                if 2 * n + 4 < BRANCH_UNIT0:
                    split(2 * n + 4)
                if name == "a":
                    continue
                bank = 2 * (n % 2)
                tile4 = quarter(bank)
                if name == "v":
                    last = nc.scalar.activation(v_sb[:, :, :], ps[:, bank:bank + 2, :], ACT.Copy)
                for c in range(CT):
                    if name == "v":
                        break
                    bias = prm[:, ROW["b_in"] + col // P + c:ROW["b_in"] + col // P + c + 1]
                    func = ACT.Sigmoid if name in ("gate", "g") else ACT.Identity
                    if name == "gate":
                        dst = sig_gate[:, c, :]
                    elif name == "pool":
                        dst = z_pool[:, c, POOL_PAD:PW]
                    elif name == "u":
                        dst = uT[:, c, :]
                    else:
                        k, d0 = divmod(col - 2560, D)
                        dst = gates[:, k, d0 // P + c, :]
                    last = nc.scalar.activation(dst, tile4[:, c, :], func, bias=bias)
                last.then_inc(chunk_read, 1)
                if n == 6:
                    act.wait_ge(pool_mixed, 1)
                    for c in range(CT):
                        row = ROW["pool_scale"] + c
                        last = nc.scalar.activation(yaT[:, c, :], quarter(4)[:, c, :], ACT.Copy,
                                                    scale=prm[:, row:row + 1])
                    last.then_inc(yaT_ready, 1)
                if n == 9:
                    act.wait_ge(var_done, 1)
                    nc.scalar.activation(conv_rstd, ps[:, 5, 0:T], ACT.Sqrt, bias=eps).then_inc(conv_rms_ready, 1)
                    act.wait_ge(conv_normed, 1)
                    for c in range(CT):
                        g, b = ROW["conv_norm_g"] + c, ROW["conv_norm_b"] + c
                        last = nc.scalar.activation(convT[:, c, :], convT[:, c, :], ACT.Silu,
                                                    scale=prm[:, g:g + 1], bias=prm[:, b:b + 1])
                    last.then_inc(ybT_ready, 1)

            for c in range(4):
                act.dma_start(b_up[N_EXP * c:N_EXP * (c + 1), :],
                              expert_b_up[0, :, 512 * c:512 * (c + 1)]).then_inc(bup_loaded, 16)
            act.dma_start(b_down[0], expert_b_down[0, :, 0:512]).then_inc(bdown_loaded, 16)
            for a in range(TT):
                act.wait_ge(x_ready, a + 1)
                square_sum(a)
            act.wait_ge(xsT_done, 2)
            scale_high(0, ROW["moe_norm"])
            root().then_inc(rms_ready, 1)
            act.wait_ge(logits_done, 1)
            act.dma_start(b_down[1], expert_b_down[0, :, 512:1024]).then_inc(bdown_loaded, 16)
            act.wait_ge(top_ready, 1)
            nc.scalar.activation(top_e[:, :, :], top_e[:, :, :], ACT.Exp).then_inc(top_exp, 1)
            act.wait_ge(gateT_done, 1)
            nc.scalar.activation(gateT, ps[0:N_EXP, WT, 0:T], ACT.Copy).then_inc(gateT_ready, 1)

            def expert(q):
                act.wait_ge(glu_ready, q + 1)
                wait_past(act, prod_ready, 2 * q)
                nc.scalar.activation(sig, glu, ACT.Sigmoid, scale=ALPHA).then_inc(sig_ready, 1)
                act.wait_ge(actT_done, q + 1)
                act.wait_ge(w_used, used_before(q))
                nc.scalar.activation(actT[:, :, :, :].rearrange("p m g s -> p (m g s)"), ps[:, ACTT, :],
                                     ACT.Copy).then_inc(actT_ready, 1)
                act.wait_ge(weightT_done, q + 1)
                act.wait_ge(comb_done, comb_before(q))
                nc.scalar.activation(weightT[:, :, :].rearrange("p a t -> p (a t)"), ps[:, WT, 0:2 * P],
                                     ACT.Copy).then_inc(weightT_ready, 1)
                act.wait_ge(w_used, used_before(q + 1))
                nc.scalar.activation(y_sb, ps[:, Y, :], ACT.Copy).then_inc(y_ready, 1)

            for q in range(2):
                expert(q)
            with act.Fori(1, N_EXP // 2) as i:
                for j in range(2):
                    expert(2 * i + j)
            act.wait_ge(flag_ready, 1)
            overflow = act.value_load(flag[0:1, 0:1], min_val=0, max_val=1)
            with act.If(overflow > 0):
                with act.Fori(N_EXP // 2, ROUNDS * N_EXP // 2) as i:
                    for j in range(2):
                        expert(2 * i + j)

            for a in range(TT):
                act.wait_ge(x_final, a + 1)
                if a == 0:
                    act.dma_start(final_gain, on_all(final_norm)).then_inc(gain_loaded, 16)
                square_sum(a)
            act.wait_ge(xsT_done, 3)
            scale_high(0, ROW["ple_norm"])
            root().then_inc(rms_ready, 1)
            act.wait_ge(rstd_ready, 2)
            for a in range(TT):
                for h in range(2):
                    act.wait_ge(ple_gate_done, 2 * a + h + 1)
                    nc.scalar.activation(ple_sig[:, a, h * 512:(h + 1) * 512], ps[:, 2 * a + h, :],
                                         ACT.Sigmoid, scale=rstd[:, a:a + 1]).then_inc(ple_sig_ready, 1)
            for a in range(TT):
                for h in range(2):
                    act.wait_ge(ple_x_ready, 2 * a + h + 1)
                    own(nc.scalar.activation(xs[:, a, h * 512:(h + 1) * 512], x_sb[:, a, h * 512:(h + 1) * 512],
                                             ACT.Square, accum_out=half_ssq[:, 2 * a + h:2 * a + h + 1]))
                own(nc.scalar.activation(ssq[:, a:a + 1], half_ssq[:, 2 * a:2 * a + 1], ACT.Identity,
                                         bias=half_ssq[:, 2 * a + 1:2 * a + 2]))
                nc.scalar.activation(rms[:, a:a + 1], ssq[:, a:a + 1], ACT.Sqrt, bias=eps,
                                     scale=1.0 / D).then_inc(final_rms, 1)

        @block.vector
        def _(dve):
            steps = [0]

            def own(ins):
                steps[0] += 1
                ins.then_inc(dve_order, 1)
                dve.wait_ge(dve_order, steps[0])

            def normalise(n):
                dve.wait_ge(rms_ready, n)
                if n == 1:
                    own(nc.vector.reciprocal(rstd, rms))
                for a in range(TT):
                    last = nc.vector.tensor_scalar(xs[:, a, :], x_sb[:, a, :], rstd[:, a:a + 1], None, ALU.mult)
                last.then_inc(xs_ready, 1)

            def scale_low(n, bank, gain, dst=hT):
                dve.wait_ge(xsT_done, n)
                for k in range(4):
                    last = nc.vector.tensor_scalar(dst[:, k, :], ps[:, bank + k // 2, 256 * (k % 2):256 * (k % 2) + 256],
                                                   prm[:, gain + k:gain + k + 1], None, ALU.mult)
                last.then_inc(hT_dve, 1)

            nc.vector.memset(eps, EPS).then_inc(eps_ready, 1)
            dve.wait_ge(consts_ready, 7)
            nc.vector.tensor_reduce(fold[:, :], ident[:, :].rearrange("p (c e) -> p e c", c=4), axis=AX,
                                    op=ALU.add).then_inc(fold_ready, 1)
            dve.wait_ge(x_loaded, 16)
            normalise(1)
            dve.wait_ge(rowsT_done, 1)
            nc.vector.tensor_copy(prm[:, :], ps[:, 0, 0:N_ROWS]).then_inc(prm_ready, 1)
            nc.vector.tensor_copy(conv_taps[:, :, :].rearrange("p k c -> p (k c)"),
                                  ps[:, 0, P:P + CONV_K * CT]).then_inc(taps_ready, 1)
            dve.wait_ge(prm_ready, 1)
            scale_low(1, 4, ROW["mix_norm"], h_hi)
            dve.wait_ge(hT_dve, 1)
            for k in range(KT):
                if k == 4:
                    dve.wait_ge(hT_act, 1)
                g = ROW["mix_norm"] + k
                last = nc.vector.scalar_tensor_tensor(
                    out=h_lo[:, k, :], in0=ps[:, 4 + k // 2, 256 * (k % 2):256 * (k % 2) + 256],
                    scalar=prm[:, g:g + 1], in1=h_hi[:, k, :].bitcast(F32), op0=ALU.mult, op1=ALU.subtract)
            last.then_inc(h_lo_ready, 1)

            def split(u):
                dve.wait_ge(w_hi_ready, u + 1)
                w_lo_part(nc.vector, u).then_inc(w_lo_dve, 1)

            for u in range(HI_BUFS):
                split(u)
            dve.wait_ge(count_ready, 1)
            nc.vector.reciprocal(inv_count[:, :, :], inv_count[:, :, :]).then_inc(inv_ready, 1)
            dve.wait_ge(pT_done, 1)
            nc.vector.tensor_copy(pT[:, :, :].rearrange("p a t -> p (a t)"), ps[:, 4, :])
            dve.wait_ge(sguT_done, 1)
            nc.vector.tensor_copy(sguT[:, :, :].rearrange("p h t -> p (h t)"), ps[:, 5, :]).then_inc(sguT_ready, 1)
            for u in range(HI_BUFS, CONV_UNIT):
                split(u)

            dve.wait_ge(w_used, 4)
            dve.wait_ge(chunk_read, 1)
            dve.wait_ge(consts_ready, 7)
            for c in range(CT):
                b = ROW["b_in"] + 4 + c
                last = nc.vector.scalar_tensor_tensor(out=y_pad[:, c, CONV_K - 1:CW], in0=quarter(2)[:, c, :],
                                                      scalar=prm[:, b:b + 1], in1=sig_gate[:, c, :],
                                                      op0=ALU.add, op1=ALU.mult)
            last.then_inc(a_read, 1)
            dve.wait_ge(a_read, 1)
            dve.wait_ge(taps_ready, 1)
            for c in range(CT):
                b = ROW["conv_b"] + c
                nc.vector.tensor_scalar(convT[:, c, :], y_pad[:, c, 0:T], conv_taps[:, 0, c:c + 1],
                                        prm[:, b:b + 1], ALU.mult, ALU.add).then_inc(conv_step, 1)
            tap = 1
            for i, taps in enumerate(CONV_TAPS):
                with dve.Fori(tap, tap + taps) as k:
                    for c in range(CT):
                        dve.wait_ge(conv_step, 4 * k + (c - 3))
                        nc.vector.scalar_tensor_tensor(out=convT[:, c, :], in0=y_pad[:, c, bass.ds(k, T)],
                                                       scalar=conv_taps[:, bass.ds(k, 1), c],
                                                       in1=convT[:, c, :], op0=ALU.mult, op1=ALU.add
                                                       ).then_inc(conv_step, 1)
                tap += taps
                if not lo_by_gpsimd(CONV_UNIT + i):
                    split(CONV_UNIT + i)
            split(CONV_UNIT + len(CONV_TAPS))

            dve.wait_ge(chunk_read, 3)
            dve.wait_ge(vbc_loaded, 48)
            for a in range(TT):
                own(nc.vector.tensor_tensor(v_sb[:, a, :], v_sb[:, a, :], v_bias, ALU.add))
                own(nc.vector.bn_stats(vstat[:, 6 * a:6 * a + 6], v_sb[:, a, :]))
                last = nc.vector.bn_aggr(vmv[:, 2 * a:2 * a + 2], vstat[:, 6 * a:6 * a + 6])
            last.then_inc(v_var_ready, 1)
            dve.wait_ge(mean_done, 1)
            nc.vector.tensor_tensor(convT[:, :, :], convT[:, :, :],
                                    ps[:, 4:5, 0:T].to_broadcast([P, CT, T]), ALU.subtract).then_inc(centred, 1)
            split(BRANCH_UNIT0 - 1)
            dve.wait_ge(v_rms_ready, 1)
            own(nc.vector.reciprocal(vrstd, vrms))
            for a in range(TT):
                own(nc.vector.tensor_scalar(v_sb[:, a, :], v_sb[:, a, :], vmv[:, 2 * a:2 * a + 1],
                                            vrstd[:, a:a + 1], ALU.subtract, ALU.mult))
                own(nc.vector.tensor_tensor(v_sb[:, a, :], v_sb[:, a, :], v_gain, ALU.mult))
                last = nc.vector.tensor_tensor(v_sb[:, a, :], v_sb[:, a, :], v_shift, ALU.add)
            last.then_inc(v_ready, 1)

            dve.wait_ge(conv_rms_ready, 1)
            own(nc.vector.reciprocal(conv_rstd, conv_rstd))
            nc.vector.tensor_tensor(convT[:, :, :], convT[:, :, :],
                                    conv_rstd.rearrange("p (a t) -> p a t", a=1).to_broadcast([P, CT, T]),
                                    ALU.mult).then_inc(conv_normed, 1)

            dve.wait_ge(sgu_done, 1)
            dve.wait_ge(sgu_loaded, 32)
            dve.wait_ge(pooled_ready, 1)
            for n in range(TT):
                own(nc.vector.tensor_tensor(sgu_mix[:, :, n * P:(n + 1) * P], quarter(6)[:, :, n * P:(n + 1) * P],
                                            sgub[:, :, :], ALU.add))
            dve.wait_ge(chunk_read, 4)
            nc.vector.tensor_tensor(uT[:, :, :], uT[:, :, :], sgu_mix[:, :, :], ALU.mult).then_inc(ycT_ready, 1)

            dve.wait_ge(chunk_read, N_CHUNKS - 1)
            for d in range(KT):
                if d % 4 == 3:
                    dve.wait_ge(w_used, BRANCH_UNIT0 + N_BRANCH * (d // 4 + 1))
                else:
                    dve.wait_ge(proj_done, d + 1 - d // 4)
                for k in range(N_BRANCH):
                    b = ROW["branch_b"] + KT * k + d
                    last = nc.vector.scalar_tensor_tensor(out=gated[:, k, :], in0=quarter(2 * (d % 2))[:, k, :],
                                                          scalar=prm[:, b:b + 1], in1=gates[:, k, d, :],
                                                          op0=ALU.add, op1=ALU.mult)
                last.then_inc(proj_read, 1)
                dve.wait_ge(proj_read, d + 1)
                own(nc.vector.tensor_tensor(gated[:, 0, :], gated[:, 0, :], gated[:, 1, :], ALU.add))
                nc.vector.tensor_tensor(hT[:, d, :], gated[:, 0, :], gated[:, 2, :], ALU.add
                                        ).then_inc(merged_ready, 1)
                dve.wait_ge(merged_ready, d + 1)
            dve.wait_ge(w_used, MIX_UNITS)
            for a in range(TT):
                nc.vector.tensor_tensor(x_sb[:, a, :], x_sb[:, a, :],
                                        ps[:, 4 + 2 * a:6 + 2 * a, :].rearrange("p a b -> p (a b)"),
                                        ALU.add).then_inc(x_ready, 1)

            scale_low(2, 0, ROW["moe_norm"])
            dve.wait_ge(rms_ready, 2)
            nc.vector.reciprocal(rstd, rms).then_inc(rstd_ready, 1)
            dve.wait_ge(rstd_ready, 1)

            dve.wait_ge(partial_done, 1)
            nc.vector.tensor_copy(partial, ps[:, 4, 0:T]).then_inc(partial_ready, 1)
            normalise(2)

            dve.wait_ge(logits_done, 1)
            for a in range(TT):
                own(nc.vector.scalar_tensor_tensor(out=logits[:, a, :], in0=ps[:, 5, N_EXP * a:N_EXP * (a + 1)],
                                                   scalar=rstd[:, a:a + 1], in1=rb[:, :], op0=ALU.mult,
                                                   op1=ALU.add))
            for a in range(TT):
                own(nc.vector.max(top[:, a, :], logits[:, a, :]))
                own(nc.vector.max_index(top_i[:, a, :], top[:, a, :], logits[:, a, :]))
            nc.vector.tensor_tensor(top_e[:, :, :], top[:, :, 0:TOP_K],
                                    top[:, :, 0:1].to_broadcast([P, TT, TOP_K]), ALU.subtract).then_inc(top_ready, 1)
            own(nc.vector.tensor_copy(top_f[:, :, :], top_i[:, :, :]))
            for a in range(TT):
                own(nc.vector.tensor_tensor(onehot[:, a, :, :],
                                            slot_ids[:, 0:1, 0:N_EXP].to_broadcast([P, TOP_K, N_EXP]),
                                            top_f[:, a, 0:TOP_K].unsqueeze(2).to_broadcast([P, TOP_K, N_EXP]),
                                            ALU.is_equal))
            for a in range(TT):
                last = nc.vector.tensor_reduce(chosen[:, a, :], onehot[:, a, :, :].rearrange("p j e -> p e j"),
                                               axis=AX, op=ALU.add)
            last.then_inc(chosen_ready, 1)
            dve.wait_ge(pos_done, 1)
            own(nc.vector.tensor_copy(pos0[:, :, :], ps[:, 1, 0:TT * N_EXP].rearrange("p (a e) -> p a e", a=TT)))
            own(nc.vector.scalar_tensor_tensor(out=pos0[:, :, :], in0=pos0[:, :, :], scalar=1.0,
                                               in1=chosen[:, :, :], op0=ALU.add, op1=ALU.mult))
            for r in range(ROUNDS):
                nc.vector.tensor_scalar(pos[:, :, N_EXP * r:N_EXP * (r + 1)], pos0[:, :, :],
                                        -1.0 - SLOTS * r, None, ALU.add)
            own(nc.vector.memset(pos[:, :, ROUNDS * N_EXP:QPAD], -1.0))

            def make_select(q):
                for a in range(TT):
                    last = nc.vector.tensor_scalar(select_of(q)[:, a, :], slot_ids[:, 0, :],
                                                   pos[:, a, bass.ds(q, 1)], None, ALU.is_equal)
                last.then_inc(select_ready, 1)

            half = [0]

            def select_of(q):
                return select[:, half[0]]

            make_select(0)
            dve.wait_ge(top_exp, 1)
            own(nc.vector.tensor_reduce(wsum, top_e[:, :, :], axis=AX, op=ALU.add))
            own(nc.vector.reciprocal(wrec, wsum))
            own(nc.vector.tensor_tensor(top_e[:, :, :], top_e[:, :, :],
                                        wrec.unsqueeze(2).to_broadcast([P, TT, TOP_K]), ALU.mult))
            for a in range(TT):
                own(nc.vector.tensor_tensor(weighted[:, a, :, :], onehot[:, a, :, :],
                                            top_e[:, a, :].unsqueeze(2).to_broadcast([P, TOP_K, N_EXP]), ALU.mult))
            for a in range(TT):
                own(nc.vector.tensor_reduce(gate_w[:, a, 0:N_EXP], weighted[:, a, :, :].rearrange("p j e -> p e j"),
                                            axis=AX, op=ALU.add))
            for r in range(1, ROUNDS):
                last = nc.vector.tensor_copy(gate_w[:, :, N_EXP * r:N_EXP * (r + 1)], gate_w[:, :, 0:N_EXP])
            last.then_inc(gates_ready, 1)
            dve.wait_ge(gates_ready, 1)

            def scale_xe(q, b):
                dve.wait_ge(gather_done, q + 1)
                gain = prm[:, ROW["moe_norm"]:ROW["moe_norm"] + KT].unsqueeze(2).to_broadcast([P, KT, SLOTS])
                nc.vector.tensor_tensor(xe[:, b, :, :], ps[:, GATHER, :].rearrange("p (k s) -> p k s", k=KT),
                                        gain, ALU.mult).then_inc(xe_ready, 1)

            scale_xe(0, 0)
            dve.wait_ge(totals_done, 1)
            own(nc.vector.reduce_max(most, ps[:, 6, 0:N_EXP], AX))
            nc.vector.tensor_scalar(flag[:, 0:1], most, float(SLOTS), None, ALU.is_gt).then_inc(flag_ready, 1)
            def expert(q, e, j):
                wait_past(dve, up_done, q)
                nc.vector.tensor_copy(pick_bias[:, :, :],
                                      ident_e[:, :, bass.ds(e, 1)].to_broadcast([P, 4, SLOTS])).then_inc(pick_ready, 1)
                wait_past(dve, weightT_done, q)
                for a in range(TT):
                    last = nc.vector.tensor_scalar(weight[:, a, :], slot_ids[:, :, :].rearrange("p a s -> p (a s)"),
                                                   pos[:, a, bass.ds(q, 1)], gate_w[:, a, bass.ds(q, 1)],
                                                   ALU.is_equal, ALU.mult)
                last.then_inc(weight_ready, 1)
                dve.wait_ge(gather_done, q + 1)
                half[0] = 1 - j
                make_select(q + 1)
                dve.wait_ge(up_done, q + 1)
                nc.vector.tensor_scalar(glu, ps[:, GLU, :], LIMIT, None, ALU.min).then_inc(glu_ready, 1)
                nc.vector.tensor_scalar(lin, ps[:, LIN, :], LIMIT, -LIMIT, ALU.min, ALU.max).then_inc(lin_ready, 1)
                dve.wait_ge(glu_ready, q + 1)
                dve.wait_ge(lin_ready, q + 1)
                nc.vector.scalar_tensor_tensor(out=lin, in0=lin, scalar=1.0, in1=glu, op0=ALU.add,
                                               op1=ALU.mult).then_inc(prod_ready, 1)
                dve.wait_ge(prod_ready, 2 * q + 1)
                dve.wait_ge(sig_ready, q + 1)
                nc.vector.tensor_tensor(lin, lin, sig, ALU.mult).then_inc(prod_ready, 1)
                add_result(q - 1, 0)
                scale_xe(q + 1, 1 - j)
                add_result(q - 1, 1)

            def add_result(q, a, done=x_added):
                dve.wait_ge(comb_done, comb_before(q) + a + 1)
                nc.vector.tensor_tensor(x_sb[:, a, :], x_sb[:, a, :],
                                        ps[:, COMB:COMB + 2, :].rearrange("p a b -> p (a b)"),
                                        ALU.add).then_inc(done, 1)

            for q in range(2):
                expert(q, q, q)
            with dve.Fori(1, N_EXP // 2) as i:
                for j in range(2):
                    expert(2 * i + j, 2 * i + j, j)
            overflow = dve.value_load(flag[0:1, 0:1], min_val=0, max_val=1)
            with dve.If(overflow > 0):
                with dve.Fori(1, ROUNDS) as r:
                    with dve.Fori(0, N_EXP // 2) as i:
                        for j in range(2):
                            expert(N_EXP * r + 2 * i + j, 2 * i + j, j)
                for a in range(TT):
                    add_result(ROUNDS * N_EXP - 1, a, x_final)
            with dve.If(overflow < 1):
                for a in range(TT):
                    add_result(N_EXP - 1, a, x_final)

            scale_low(3, 0, ROW["ple_norm"])
            dve.wait_ge(rms_ready, 3)
            nc.vector.reciprocal(rstd, rms).then_inc(rstd_ready, 1)
            for a in range(TT):
                for h in range(2):
                    cols = slice(h * 512, (h + 1) * 512)
                    dve.wait_ge(ple_sig_ready, 2 * a + h + 1)
                    own(nc.vector.tensor_tensor(ple_sig[:, a, cols], ple_sig[:, a, cols],
                                                ps[:, 4 + 2 * a + h, :], ALU.mult))
                    nc.vector.tensor_tensor(x_sb[:, a, cols], x_sb[:, a, cols], ple_sig[:, a, cols],
                                            ALU.add).then_inc(ple_x_ready, 1)
            dve.wait_ge(gain_loaded, 16)
            for a in range(TT):
                dve.wait_ge(final_rms, a + 1)
                own(nc.vector.reciprocal(frstd[:, a:a + 1], rms[:, a:a + 1]))
                for h in range(2):
                    cols = slice(h * 512, (h + 1) * 512)
                    nc.vector.scalar_tensor_tensor(out=final_out[:, a, cols], in0=x_sb[:, a, cols],
                                                   scalar=frstd[:, a:a + 1], in1=final_gain[:, cols],
                                                   op0=ALU.mult, op1=ALU.mult).then_inc(final_ready, 1)

        @block.tensor
        def _(pe):
            def transpose_tokens(src, a, bank):
                for k in range(KT):
                    col = 256 * (k % 2) + P * a
                    last = nc.tensor.transpose(ps[:, bank + k // 2, col:col + P], src[:, a, k * P:(k + 1) * P],
                                               ident[:, :])
                return last

            def hT_written(n):
                pe.wait_ge(hT_act, n)
                pe.wait_ge(hT_dve, n)

            pe.wait_ge(consts_ready, 7)
            pe.wait_ge(xs_ready, 1)
            transpose_tokens(xs, 0, 4)
            transpose_tokens(xs, 1, 4).then_inc(xsT_done, 1)
            pe.wait_ge(rows_loaded, 16 * (len(PARAMS) + 1))
            nc.tensor.transpose(ps[:, 0, 0:N_ROWS], prm_rows[0:N_ROWS, :], ident[0:N_ROWS, 0:N_ROWS])
            nc.tensor.transpose(ps[:, 0, P:P + CONV_K * CT], tap_rows[0:CONV_K * CT, :],
                                ident[0:CONV_K * CT, 0:CONV_K * CT]).then_inc(rowsT_done, 1)
            hT_written(1)
            pe.wait_ge(h_lo_ready, 1)

            def mixer_unit(u, first=True):
                slot, turn = mix_slot(u)
                if first:
                    pe.wait_ge(up_loaded[slot], 16 * turn)
                return up_ring[:, slot, :]

            for n, (name, col) in enumerate(CHUNKS):
                if n == 0:
                    pe.wait_ge(taps_ready, 1)
                elif n == 3:
                    pe.wait_ge(a_read, 1)
                elif n >= 2:
                    pe.wait_ge(chunk_read, n - 1 - (n > 2))
                bank = 2 * (n % 2)
                for s in range(2):
                    u = 2 * n + s
                    if lo_by_gpsimd(u):
                        pe.wait_ge(w_lo_pool, lo_count(u, True))
                    else:
                        pe.wait_ge(w_lo_dve, lo_count(u, False))
                    hi = w_hi[:, u % HI_BUFS, :].rearrange("p (k n) -> p k n", k=KT)
                    lo = w_lo[:, mix_slot(u)[0], :].rearrange("p (k n) -> p k n", k=KT)
                    for c in range(2):
                        for k in range(KT):
                            for i, (wk, hk) in enumerate(((hi, h_hi), (hi, h_lo), (lo, h_hi))):
                                start, stop = k + i == 0, k + i == KT + 1
                                if name == "v":
                                    last = nc.tensor.matmul(ps[:, bank + c, s * 256:(s + 1) * 256],
                                                            hk[:, k, c * P:(c + 1) * P], wk[:, k, :],
                                                            start=start, stop=stop)
                                else:
                                    last = nc.tensor.matmul(quarter(bank)[:, 2 * s + c, :],
                                                            wk[:, k, c * P:(c + 1) * P], hk[:, k, :],
                                                            start=start, stop=stop)
                    last.then_inc(w_used, 1)
                    if u == 18:
                        pe.wait_ge(conv_step, 4 * CONV_K)
                        pe.wait_ge(yaT_ready, 1)
                        for c in range(CT):
                            last = nc.tensor.matmul(ps[:, 4, 0:T], mean_mat[:, :], convT[:, c, :], start=(c == 0),
                                                    stop=(c == CT - 1))
                        last.then_inc(mean_done, 1)
                    if u == 19:
                        pe.wait_ge(sq_ready, 1)
                        for c in range(CT):
                            last = nc.tensor.matmul(ps[:, 5, 0:T], mean_mat[:, :], squares[:, c, :],
                                                    start=(c == 0), stop=(c == CT - 1))
                        last.then_inc(var_done, 1)
                    if u == 20:
                        pe.wait_ge(v_ready, 1)
                        for h in range(4):
                            for a in range(TT):
                                last = nc.tensor.matmul(quarter(6)[:, h, a * P:(a + 1) * P],
                                                        v_sb[:, a, h * P:(h + 1) * P], sguT[:, h, :],
                                                        start=True, stop=True)
                        last.then_inc(sgu_done, 1)
                if n == 0:
                    pe.wait_ge(p_loaded, 16)
                    for k in range(PLE // P):
                        for a in range(TT):
                            last = nc.tensor.transpose(ps[:, 4, T * k + P * a:T * k + P * (a + 1)],
                                                       p_sb[:, a, k * P:(k + 1) * P], ident[:, :])
                    last.then_inc(pT_done, 1)
                    pe.wait_ge(sgu_masked, 1)
                    for h in range(4):
                        last = nc.tensor.transpose(ps[:, 5, P * h:P * (h + 1)], sgu_in[:, h, :], ident[:, :])
                    last.then_inc(sguT_done, 1)
                if n == 5:
                    pe.wait_ge(mats_loaded, 48)
                    pe.wait_ge(pooled_ready, 1)
                    pe.wait_ge(sguT_ready, 1)
                    for g in range(4):
                        last = nc.tensor.matmul(quarter(4)[:, g, :], pool_mix[:, g, :], pooled[:, g, :],
                                                start=True, stop=True)
                    last.then_inc(pool_mixed, 1)

            pe.wait_ge(yaT_ready, 1)
            pe.wait_ge(ycT_ready, 1)
            pe.wait_ge(ybT_ready, 1)
            pe.wait_ge(chunk_read, N_CHUNKS - 1)
            branch = [yaT, convT, uT]
            for d in range(KT):
                if d >= 2:
                    pe.wait_ge(proj_read, d - 1)
                for k in range(N_BRANCH):
                    w = mixer_unit(BRANCH_UNIT0 + N_BRANCH * (d // 4) + k, d % 4 == 0)
                    w = w.rearrange("p (c n) -> p c n", c=4)
                    for c in range(CT):
                        last = nc.tensor.matmul(quarter(2 * (d % 2))[:, k, :], w[:, c, (d % 4) * P:(d % 4 + 1) * P],
                                                branch[k][:, c, :], start=(c == 0), stop=(c == CT - 1))
                    if d % 4 == 3:
                        last.then_inc(w_used, 1)
                if d % 4 != 3:
                    last.then_inc(proj_done, 1)
            for d in range(KT):
                pe.wait_ge(merged_ready, d + 1)
                w = mixer_unit(OUT_UNIT0 + d // 2, d % 2 == 0).rearrange("p (c n) -> p c n", c=2)
                for a in range(TT):
                    for h in range(2):
                        last = nc.tensor.matmul(ps[:, 4 + 2 * a + h, :], hT[:, d, a * P:(a + 1) * P],
                                                w[:, d % 2, h * 512:(h + 1) * 512], start=(d == 0),
                                                stop=(d == KT - 1))
                if d % 2:
                    last.then_inc(w_used, 1)

            for a in range(TT):
                pe.wait_ge(x_ready, a + 1)
                last = transpose_tokens(x_sb, a, 0)
            last.then_inc(xsT_done, 1)
            hT_written(2)
            for half in range(2):
                for g in range(4):
                    k = 4 * half + g
                    last = nc.tensor.matmul(ps[32 * g:32 * g + 32, 4, 0:T], rw[:, k, :], hT[:, k, :],
                                            start=(half == 0), stop=(half == 1))
            last.then_inc(partial_done, 1)
            pe.wait_ge(partial_ready, 1)
            pe.wait_ge(fold_ready, 1)
            for a in range(TT):
                last = nc.tensor.matmul(ps[:, 5, N_EXP * a:N_EXP * (a + 1)], partial[:, a * P:(a + 1) * P],
                                        fold[:, :], start=True, stop=True)
            last.then_inc(logits_done, 1)
            pe.wait_ge(chosen_ready, 1)
            nc.tensor.matmul(ps[:, 1, 0:N_EXP], before[:, :], chosen[:, 0, :], start=True, stop=True)
            nc.tensor.matmul(ps[:, 1, N_EXP:2 * N_EXP], ones[:, :], chosen[:, 0, :], start=True, stop=False)
            nc.tensor.matmul(ps[:, 1, N_EXP:2 * N_EXP], before[:, :], chosen[:, 1, :], start=False,
                             stop=True).then_inc(pos_done, 1)

            def gather(q, b):
                pe.wait_ge(select_ready, q + 1)
                wait_past(pe, xe_ready, q)
                for k in range(KT):
                    for a in range(TT):
                        last = nc.tensor.matmul(ps[:, GATHER, k * SLOTS:(k + 1) * SLOTS],
                                                xs[:, a, k * P:(k + 1) * P], select[:, b, a, :],
                                                start=(a == 0), stop=(a == TT - 1))
                last.then_inc(gather_done, 1)

            pe.wait_ge(xs_ready, 2)
            gather(0, 0)
            nc.tensor.matmul(ps[:, 6, 0:N_EXP], ones[:, :], chosen[:, 0, :], start=True, stop=False)
            nc.tensor.matmul(ps[:, 6, 0:N_EXP], ones[:, :], chosen[:, 1, :], start=False,
                             stop=True).then_inc(totals_done, 1)
            pe.wait_ge(bup_loaded, 64)

            def biases_to_tokens(a):
                pe.wait_ge(flag_ready, 1)
                wait_past(pe, x_added, a)
                for h in range(2):
                    last = nc.tensor.matmul(ps[:, COMB + h, :], gateT[:, a * P:(a + 1) * P], b_down[h],
                                            start=True, stop=True)
                last.then_inc(comb_done, 1)

            def expert(q, j, turn, first=False):
                pe.wait_ge(xe_ready, q + 1)
                wait_past(pe, lin_ready, q)
                for k in range(UP_UNITS):
                    slot = UP_UNITS * j + k
                    pe.wait_ge(up_loaded[slot], 16 * turn + up_value(slot, 1))
                    for part in range(2):
                        for g in range(2):
                            last = nc.tensor.matmul(ps[64 * g:64 * g + 64, GLU + part, :], xe[:, j, k, :],
                                                    up_ring[:, slot, D * part + 512 * g:D * part + 512 * (g + 1)],
                                                    start=(k == 0), stop=False)
                    last.then_inc(w_used, 1)
                pe.wait_ge(pick_ready, q + 1)
                for part in range(2):
                    for g in range(2):
                        last = nc.tensor.matmul(ps[64 * g:64 * g + 64, GLU + part, :],
                                                pick_bias[:, 2 * part + g, :], b_up, start=False, stop=True)
                last.then_inc(up_done, 1)
                if first:
                    pe.wait_ge(gates_ready, 1)
                    for a in range(TT):
                        last = nc.tensor.transpose(ps[0:N_EXP, WT, a * P:(a + 1) * P], gate_w[:, a, 0:N_EXP],
                                                   ident[:, :])
                    last.then_inc(gateT_done, 1)
                else:
                    pe.wait_ge(y_ready, q)
                    pe.wait_ge(weightT_ready, q)
                    to_tokens(q - 1, 0)
                gather(q + 1, 1 - j)
                if first:
                    pe.wait_ge(gateT_ready, 1)
                    pe.wait_ge(bdown_loaded, 32)
                    biases_to_tokens(0)
                pe.wait_ge(weight_ready, q + 1)
                wait_past(pe, weightT_ready, q)
                for a in range(TT):
                    last = nc.tensor.transpose(ps[:, WT, a * P:(a + 1) * P], weight[:, a, :], ident[:, :])
                last.then_inc(weightT_done, 1)
                pe.wait_ge(prod_ready, 2 * q + 2)
                wait_past(pe, actT_ready, q)
                for m in range(4):
                    last = nc.tensor.transpose(ps[:, ACTT, m * P:(m + 1) * P], lin[:, m * P:(m + 1) * P], ident[:, :])
                last.then_inc(actT_done, 1)
                if first:
                    biases_to_tokens(1)
                else:
                    to_tokens(q - 1, 1)
                pe.wait_ge(actT_ready, q + 1)
                wait_past(pe, y_ready, q)
                for k in range(KT):
                    c = k // 2
                    if k % 2 == 0:
                        pe.wait_ge(down_loaded[c], 16 * q + 16)
                    for g in range(2):
                        col = D * (k % 2) + 512 * g
                        last = nc.tensor.matmul(ps[64 * g:64 * g + 64, Y, :], actT[:, k % 4, k // 4, :],
                                                down_ring[:, c, col:col + 512], start=(k == 0), stop=(k == KT - 1))
                    if k % 2:
                        last.then_inc(w_used, 1)

            def to_tokens(q, a):
                wait_past(pe, x_added, comb_before(q) + a)
                for g in range(2):
                    last = nc.tensor.matmul(ps[:, COMB + g, :], weightT[64 * g:64 * g + 64, a, :],
                                            y_sb[64 * g:64 * g + 64, :], start=True, stop=True)
                last.then_inc(comb_done, 1)

            def ple_projection(a, h):
                wp = up_ring[:, 4, :].rearrange("p (c n) -> p c n", c=2)
                for k in range(PLE // P):
                    nc.tensor.matmul(ps[:, 4 + 2 * a + h, :], pT[:, k, a * P:(a + 1) * P],
                                     wp[:, k, h * 512:(h + 1) * 512], start=(k == 0), stop=(k == PLE // P - 1))

            def finish(q):
                pe.wait_ge(ple_loaded, 16 * 5)
                pe.wait_ge(weightT_ready, q + 1)
                ple_projection(0, 0)
                pe.wait_ge(y_ready, q + 1)
                to_tokens(q, 0)
                ple_projection(0, 1)
                pe.wait_ge(x_final, 1)
                for g in range(2):
                    last = nc.tensor.matmul(ps[:, COMB + g, :], weightT[64 * g:64 * g + 64, 1, :],
                                            y_sb[64 * g:64 * g + 64, :], start=True, stop=True)
                last.then_inc(comb_done, 1)
                transpose_tokens(x_sb, 0, 0)
                pe.wait_ge(x_final, 2)
                transpose_tokens(x_sb, 1, 0).then_inc(xsT_done, 1)

            for q in range(2):
                expert(q, q, 0, first=q == 0)
            with pe.Fori(1, N_EXP // 2) as i:
                for j in range(2):
                    expert(2 * i + j, j, i)
            pe.wait_ge(flag_ready, 1)
            overflow = pe.value_load(flag[0:1, 0:1], min_val=0, max_val=1)
            with pe.If(overflow > 0):
                with pe.Fori(N_EXP // 2, ROUNDS * N_EXP // 2) as i:
                    for j in range(2):
                        expert(2 * i + j, j, i)
                finish(ROUNDS * N_EXP - 1)
            with pe.If(overflow < 1):
                finish(N_EXP - 1)

            for h in range(2):
                ple_projection(1, h)
            hT_written(3)
            for a in range(TT):
                for h in range(2):
                    for k in range(KT):
                        wg = up_ring[:, k // 2, :].rearrange("p (c n) -> p c n", c=2)
                        last = nc.tensor.matmul(ps[:, 2 * a + h, :], hT[:, k, a * P:(a + 1) * P],
                                                wg[:, k % 2, h * 512:(h + 1) * 512], start=(k == 0),
                                                stop=(k == KT - 1))
                    last.then_inc(ple_gate_done, 1)


_INS = ["x", "p", "mix_norm", "w_in", "b_in", "pool_w", "pool_scale", "conv_w", "conv_b", "conv_norm_g",
        "conv_norm_b", "sgu_norm_g", "sgu_norm_b", "sgu_w", "sgu_b", "branch_w", "branch_b", "w_out",
        "moe_norm", "router_w", "router_b", "expert_w_up", "expert_b_up", "expert_w_down",
        "expert_b_down", "ple_norm", "ple_gate_w", "ple_proj_w", "final_norm"]


def kernel(**inputs):
    import numpy as np
    import concourse.bacc as bacc
    from concourse.bass_utils import run_bass_kernel_spmd

    nc = bacc.Bacc("TRN2", target_bir_lowering=False, num_devices=1)
    arrays, args = {}, []
    for name in _INS:
        a = np.ascontiguousarray(inputs[name])
        arrays[f"in_{name}_dram"] = a
        args.append(nc.dram_tensor(f"in_{name}_dram", a.shape, mybir.dt.from_np(a.dtype),
                                   kind="ExternalInput").ap())
    args.append(nc.dram_tensor("out_dram", (1, T, D), F32, kind="ExternalOutput").ap())
    build(nc, *args)
    return run_bass_kernel_spmd(nc, [arrays], core_ids=[0]).results[0]["out_dram"]
```

```python
from contextlib import ExitStack

import concourse.bass as bass
from concourse import mybir

F32 = mybir.dt.float32
F32R = mybir.dt.float32r
I32 = mybir.dt.int32
U32 = mybir.dt.uint32
ALU = mybir.AluOpType
ACT = mybir.ActivationFunctionType
AX = mybir.AxisListType.X

P = 128
T = 256
TT = T // P
D = 1024
KT = D // P
CH = 512
CT = CH // P
CONV_K = 31
POOL_PAD = 16
N_EXP = 32
TOP_K = 4
SLOTS = 64
ROUNDS = T // SLOTS
N_BRANCH = 3
PLE = 256
EPS = 1e-6
LIMIT = 7.0
ALPHA = 1.702

UNIT = 2048
UP_SLOTS, DOWN_SLOTS = 16, 4
UP_UNITS, DOWN_UNITS = 8, 4
PER_EXPERT = UP_UNITS + DOWN_UNITS
AHEAD_PAIRS = 11
MIX_SLOTS = 4
HI_SLOT, HI_BUFS = 8, 3
ACT_SLOT = 11
TEMP_SLOT = 12

CHUNKS = [("gate", 1024), ("a", 512), ("pool", 0), ("v", 2048), ("u", 1536)] + \
         [("g", 2560 + CH * g) for g in range(N_BRANCH * D // CH)]
N_CHUNKS = len(CHUNKS)
GPSIMD_FIRST = 8
MIX_UNITS = 2 * N_CHUNKS + 2 * N_BRANCH + KT // 2
BRANCH_UNIT0 = 2 * N_CHUNKS
OUT_UNIT0 = BRANCH_UNIT0 + 2 * N_BRANCH
POOL_BR, CONV_BR, SGU_BR = range(N_BRANCH)
BRANCH_ORDER = [POOL_BR, SGU_BR, CONV_BR]

PARAMS = [("mix_norm", 8), ("b_in", 44), ("pool_scale", 4), ("conv_b", 4), ("conv_norm_g", 4),
          ("conv_norm_b", 4), ("branch_b", 24), ("moe_norm", 8), ("ple_norm", 8)]
ROW = {}
N_ROWS = 0
for _name, _rows in PARAMS:
    ROW[_name] = N_ROWS
    N_ROWS += _rows


def mix_slot(unit):
    return unit % MIX_SLOTS, unit // MIX_SLOTS + 1


def lo_by_gpsimd(unit):
    return unit >= GPSIMD_FIRST and unit % HI_BUFS == 2


def lo_count(unit, gpsimd):
    return sum(lo_by_gpsimd(u) == gpsimd for u in range(unit + 1))


CONV_UNIT = 6
CONV_TAPS = [2, 2, 3, 2, 2, 3, 2, 2, 3, 2, 2, 3, 2]
assert sum(CONV_TAPS) == CONV_K - 1


MIX_USES = [sum(mix_slot(u)[0] == s for u in range(MIX_UNITS)) for s in range(UP_SLOTS)]


def build(nc, x, p, mix_norm, w_in, b_in, pool_w, pool_scale, conv_w, conv_b, conv_norm_g,
          conv_norm_b, sgu_norm_g, sgu_norm_b, sgu_w, sgu_b, branch_w, branch_b, w_out, moe_norm,
          router_w, router_b, expert_w_up, expert_b_up, expert_w_down, expert_b_down, ple_norm,
          ple_gate_w, ple_proj_w, final_norm, out):
    with ExitStack() as ctx:
        def sb(name, shape, dt=F32):
            return ctx.enter_context(nc.sbuf_tensor(name, shape, dt))

        def sem(name):
            return ctx.enter_context(nc.semaphore(name))

        up_ring = sb("up_ring", [P, UP_SLOTS, UNIT])
        ring_at = nc.sbuf_base - UP_SLOTS * UNIT * 4
        down_ring = sb("down_ring", [P, DOWN_SLOTS, UNIT])
        x_sb = sb("x_sb", [P, TT, D])
        xs = sb("xs", [P, TT, D])
        xs_at = nc.sbuf_base - TT * D * 4
        hT = sb("hT", [P, KT, T])
        hT_at = nc.sbuf_base - KT * T * 4
        h_hi = nc.alloc_sbuf_tensor_at("h_hi", [P, KT, T], F32R, offset=hT_at)
        h_lo = nc.alloc_sbuf_tensor_at("h_lo", [P, KT, T], F32R, offset=ring_at + ACT_SLOT * UNIT * 4)
        w_hi = nc.alloc_sbuf_tensor_at("w_hi", [P, HI_BUFS, UNIT], F32R, offset=ring_at + HI_SLOT * UNIT * 4)
        m_hi = nc.alloc_sbuf_tensor_at("m_hi", [P, KT, T], F32R, offset=ring_at + ACT_SLOT * UNIT * 4)
        m_lo = nc.alloc_sbuf_tensor_at("m_lo", [P, KT, T], F32R, offset=hT_at)
        w_lo = nc.alloc_sbuf_tensor_at("w_lo", [P, MIX_SLOTS, UNIT], F32R, offset=ring_at)
        work = sb("work", [P, 6 * 512])
        ident = sb("ident", [P, P])
        ones = sb("ones", [P, P])
        mean_mat = sb("mean_mat", [P, P])
        before = sb("before", [P, P])
        slot_ids = sb("slot_ids", [P, 2, SLOTS])
        prm = sb("prm", [P, N_ROWS])
        conv_taps = sb("conv_taps", [P, CONV_K, CT])
        pool_mix = sb("pool_mix", [P, CT, P])
        pT = sb("pT", [P, PLE // P, T])
        rw = sb("rw", [P, KT, N_EXP])
        rb = sb("rb", [P, N_EXP])
        QPAD = ROUNDS * N_EXP + 2
        pos = sb("pos", [P, TT, QPAD])
        gate_w = sb("gate_w", [P, TT, QPAD])
        small = sb("small", [P, 64])
        flag = sb("flag", [P, 2], I32)
        fold = sb("fold", [P, N_EXP])

        eps = small[:, 0:1]
        ssq = small[:, 1:3]
        rms = small[:, 3:5]
        rstd = small[:, 5:7]
        vstat = small[:, 8:20]
        vmv = small[:, 20:24]
        vrms = small[:, 24:26]
        vrstd = small[:, 26:28]
        wsum = small[:, 28:30]
        wrec = small[:, 30:32]
        most = small[:, 32:33]
        half_ssq = small[:, 36:40]
        frstd = small[:, 40:42]

        spare = up_ring[:, TEMP_SLOT:, :].rearrange("p a b -> p (a b)")
        PW = POOL_PAD + T
        z_pool = spare[:, 0:4 * PW].rearrange("p (g t) -> p g t", g=4)
        sum2 = spare[:, 1088:2176].rearrange("p (g t) -> p g t", g=4)
        sum4 = spare[:, 2176:2992].rearrange("p (g t) -> p g t", g=3)
        sum8 = spare[:, 2992:3536].rearrange("p (g t) -> p g t", g=2)
        sum16 = spare[:, 3536:3808].rearrange("p (g t) -> p g t", g=1)
        inv_count = spare[:, 3808:4832].rearrange("p (g t) -> p g t", g=4)
        pooled = spare[:, 4832:5856].rearrange("p (g t) -> p g t", g=4)
        yaT = spare[:, 5856:6880].rearrange("p (g t) -> p g t", g=4)
        p_sb = spare[:, 5856:6368].rearrange("p (a b) -> p a b", a=TT)
        sguT = spare[:, 6880:7392].rearrange("p (h t) -> p h t", h=4)
        sgub = spare[:, 7392:7904].rearrange("p (h t) -> p h t", h=4)
        squares = spare[:, 1088:2112].rearrange("p (g t) -> p g t", g=4)
        sgu_mix = spare[:, 2176:3200].rearrange("p (g t) -> p g t", g=4)
        gated = spare[:, 0:1024].rearrange("p (g t) -> p g t", g=4)
        spare_d = down_ring[:, :, :].rearrange("p a b -> p (a b)")
        gates = spare_d[:, 0:6144].rearrange("p (k c t) -> p k c t", k=N_BRANCH, c=KT)
        CW = CONV_K - 1 + T
        y_pad = spare_d[:, 6144:6144 + 4 * CW].rearrange("p (c t) -> p c t", c=CT)
        conv_rstd = spare_d[:, 7288:7544]
        prm_rows = spare_d[:, 7544:7672]
        tap_rows = spare_d[:, 7672:7800]
        convT = xs[:, 0, :].rearrange("p (c t) -> p c t", c=CT)
        uT = xs[:, 1, :].rearrange("p (c t) -> p c t", c=CT)
        v_sb = work[:, 0:1024].rearrange("p (n c) -> p n c", n=TT)
        v_bias = work[:, 1024:1536]
        v_gain = work[:, 1536:2048]
        v_shift = work[:, 2048:2560]
        sgu_in = work[:, 2560:3072].rearrange("p (h t) -> p h t", h=4)
        temp_at = ring_at + TEMP_SLOT * UNIT * 4
        ya_hi = nc.alloc_sbuf_tensor_at("ya_hi", [P, CT, T], F32R, offset=temp_at + 4832 * 4)
        yb_hi = nc.alloc_sbuf_tensor_at("yb_hi", [P, CT, T], F32R, offset=temp_at + 1088 * 4)
        yc_hi = nc.alloc_sbuf_tensor_at("yc_hi", [P, CT, T], F32R, offset=temp_at + 3808 * 4)
        ya_lo = nc.alloc_sbuf_tensor_at("ya_lo", [P, CT, T], F32R, offset=temp_at + 5856 * 4)
        yb_lo = nc.alloc_sbuf_tensor_at("yb_lo", [P, CT, T], F32R, offset=xs_at)
        yc_lo = nc.alloc_sbuf_tensor_at("yc_lo", [P, CT, T], F32R, offset=xs_at + D * 4)
        sig_gate = pooled

        onehot = work[:, 1024:1280].rearrange("p (a j e) -> p a j e", a=TT, j=TOP_K)
        weighted = work[:, 1280:1536].rearrange("p (a j e) -> p a j e", a=TT, j=TOP_K)
        logits = work[:, 2304:2368].rearrange("p (a e) -> p a e", a=TT)
        chosen = work[:, 2368:2432].rearrange("p (a e) -> p a e", a=TT)
        pos0 = work[:, 2432:2496].rearrange("p (a e) -> p a e", a=TT)
        top = work[:, 2496:2512].rearrange("p (a e) -> p a e", a=TT)
        top_i = work[:, 2512:2528].bitcast(U32).rearrange("p (a e) -> p a e", a=TT)
        top_f = work[:, 2528:2544].rearrange("p (a e) -> p a e", a=TT)
        top_e = work[:, 2544:2552].rearrange("p (a e) -> p a e", a=TT)
        gateT = work[0:N_EXP, 2560:2816]
        partial = work[:, 2816:3072]

        glu = work[:, 0:512]
        lin = work[:, 512:1024]
        sig = work[:, 1024:1536]
        b_up = work[:, 1536:2048]
        select = work[:, 2048:2304].rearrange("p (b a s) -> p b a s", b=2, a=TT)
        weight = work[:, 2304:2560].rearrange("p (a s) -> p a s", a=TT)
        weightT = work[:, 2560:2816].rearrange("p (a t) -> p a t", a=TT)
        pick_bias = work[:, 2816:3072].rearrange("p (c s) -> p c s", c=4)
        hT_flat = hT[:, :, :].rearrange("p a b -> p (a b)")
        xe = hT_flat[:, 0:1024].rearrange("p (b k s) -> p b k s", b=2, k=KT)
        actT = hT_flat[:, 1024:1536].rearrange("p (m g s) -> p m g s", m=4, g=2)
        y_sb = hT_flat[:, 1536:2048]
        b_down = [pool_mix[0:N_EXP, :, :].rearrange("p a b -> p (a b)"), y_sb[0:N_EXP, :]]
        ident_e = ident[:, :].rearrange("p (c e) -> p c e", c=4)

        ple_sig = up_ring[:, 8:9, :].rearrange("p a (b c) -> p (a b) c", b=TT)
        final_out = up_ring[:, 9:10, :].rearrange("p a (b c) -> p (a b) c", b=TT)
        final_gain = work[:, 0:1024]

        ps = ctx.enter_context(nc.psum_tensor("ps", [P, 8, 512], F32))
        GLU, LIN, GATHER, ACTT, WT, Y, COMB = 0, 1, 2, 3, 4, 5, 6

        def quarter(bank, n=4):
            return ps[:, bank:bank + 2, :].rearrange("p a (b t) -> p (a b) t", t=T)[:, 0:n, :]

        x_loaded = sem("x_loaded")
        rows_loaded = sem("rows_loaded")
        p_loaded = sem("p_loaded")
        sgu_loaded = sem("sgu_loaded")
        vbc_loaded = sem("vbc_loaded")
        mats_loaded = sem("mats_loaded")
        bdown_loaded = sem("bdown_loaded")
        bup_loaded = sem("bup_loaded")
        gain_loaded = sem("gain_loaded")
        up_loaded = [sem(f"up_loaded{s}") for s in range(UP_SLOTS)]
        down_loaded = [sem(f"down_loaded{s}") for s in range(DOWN_SLOTS)]
        w_used = sem("w_used")
        consts_ready = sem("consts_ready")
        pool_order = sem("pool_order")
        dve_order = sem("dve_order")
        act_order = sem("act_order")
        eps_ready = sem("eps_ready")
        sgu_masked = sem("sgu_masked")
        rowsT_done = sem("rowsT_done")
        prm_ready = sem("prm_ready")
        taps_ready = sem("taps_ready")
        pT_done = sem("pT_done")
        sguT_done = sem("sguT_done")
        sguT_ready = sem("sguT_ready")
        x_ready = sem("x_ready")
        x_final = sem("x_final")
        rstd_ready = sem("rstd_ready")
        rms_ready = sem("rms_ready")
        xs_ready = sem("xs_ready")
        xsT_done = sem("xsT_done")
        hT_act = sem("hT_act")
        hT_dve = sem("hT_dve")
        h_lo_ready = sem("h_lo_ready")
        ya_hi_ready = sem("ya_hi_ready")
        ya_lo_ready = sem("ya_lo_ready")
        yb_hi_ready = sem("yb_hi_ready")
        yb_lo_ready = sem("yb_lo_ready")
        yc_hi_ready = sem("yc_hi_ready")
        yc_lo_ready = sem("yc_lo_ready")
        m_hi_ready = sem("m_hi_ready")
        m_lo_ready = sem("m_lo_ready")
        w_hi_ready = sem("w_hi_ready")
        w_lo_dve = sem("w_lo_dve")
        w_lo_pool = sem("w_lo_pool")
        chunk_read = sem("chunk_read")
        a_read = sem("a_read")
        conv_step = sem("conv_step")
        y_pad_ready = sem("y_pad_ready")
        pool_sums_free = sem("pool_sums_free")
        inv_ready = sem("inv_ready")
        count_ready = sem("count_ready")
        pooled_ready = sem("pooled_ready")
        pool_mixed = sem("pool_mixed")
        yaT_ready = sem("yaT_ready")
        v_rms_ready = sem("v_rms_ready")
        v_var_ready = sem("v_var_ready")
        v_ready = sem("v_ready")
        sgu_done = sem("sgu_done")
        ycT_ready = sem("ycT_ready")
        mean_done = sem("mean_done")
        centred = sem("centred")
        sq_ready = sem("sq_ready")
        var_done = sem("var_done")
        conv_rms_ready = sem("conv_rms_ready")
        conv_normed = sem("conv_normed")
        ybT_ready = sem("ybT_ready")
        proj_read = sem("proj_read")
        merged_ready = sem("merged_ready")
        fold_ready = sem("fold_ready")
        partial_done = sem("partial_done")
        partial_ready = sem("partial_ready")
        logits_done = sem("logits_done")
        top_ready = sem("top_ready")
        top_exp = sem("top_exp")
        chosen_ready = sem("chosen_ready")
        pos_done = sem("pos_done")
        totals_done = sem("totals_done")
        gates_ready = sem("gates_ready")
        gateT_done = sem("gateT_done")
        gateT_ready = sem("gateT_ready")
        bdown_done = sem("bdown_done")
        bdown_added = sem("bdown_added")
        flag_ready = sem("flag_ready")
        select_ready = sem("select_ready")
        gather_done = sem("gather_done")
        xe_ready = sem("xe_ready")
        pick_ready = sem("pick_ready")
        weight_ready = sem("weight_ready")
        weightT_done = sem("weightT_done")
        weightT_ready = sem("weightT_ready")
        up_done = sem("up_done")
        glu_ready = sem("glu_ready")
        lin_ready = sem("lin_ready")
        sig_ready = sem("sig_ready")
        prod_ready = sem("prod_ready")
        act_ready = sem("act_ready")
        actT_done = sem("actT_done")
        actT_ready = sem("actT_ready")
        y_ready = sem("y_ready")
        comb_done = sem("comb_done")
        x_added = sem("x_added")
        ple_proj_loaded = sem("ple_proj_loaded")
        ple_gate_loaded = [sem(f"ple_gate_loaded{m}") for m in range(4)]
        ple_proj_done = sem("ple_proj_done")
        ple_gate_done = sem("ple_gate_done")
        ple_sig_ready = sem("ple_sig_ready")
        ple_x_ready = sem("ple_x_ready")
        final_rms = sem("final_rms")
        final_ready = sem("final_ready")
        stored = sem("stored")

        mixer_small = {"mix_norm": mix_norm, "b_in": b_in, "pool_scale": pool_scale, "conv_b": conv_b,
                       "conv_norm_g": conv_norm_g, "conv_norm_b": conv_norm_b, "branch_b": branch_b,
                       "moe_norm": moe_norm, "ple_norm": ple_norm}

        def rows128(ap):
            if len(ap.shape) == 3:
                ap = ap.rearrange("a b c -> a (b c)")
            return ap.rearrange("a (r c) -> (a r) c", c=P)

        def on_all(ap_row):
            return ap_row.partition_broadcast(P)

        def wait_past(eng, semaphore, value):
            if isinstance(value, int) and value <= 0:
                return
            eng.wait_ge(semaphore, value)

        def used_before(q):
            return MIX_UNITS + PER_EXPERT * q

        def comb_before(q):
            return TT * (q + 1)

        def up_value(slot, turn):
            return 16 * (MIX_USES[slot] + turn)

        def w_lo_part(engine, unit):
            slot = mix_slot(unit)[0]
            return engine.tensor_tensor(w_lo[:, slot, :], up_ring[:, slot, :],
                                        w_hi[:, unit % HI_BUFS, :].bitcast(F32), ALU.subtract)

        def branch_bank(i):
            return 2 * ((i + 1) % 2)

        block = ctx.enter_context(nc.Block())

        @block.sync
        def _(sp):
            sp.dma_start(x_sb[:, :, :], x[0].rearrange("(a p) d -> p a d", p=P)).then_inc(x_loaded, 16)

            def mix_source(u):
                if u < BRANCH_UNIT0:
                    col = CHUNKS[u // 2][1]
                    col += (u % 2) * 256
                    return w_in[0, :, col:col + 256].rearrange("(c p) n -> p c n", p=P)
                if u < OUT_UNIT0:
                    half, i = divmod(u - BRANCH_UNIT0, N_BRANCH)
                    return branch_w[0, BRANCH_ORDER[i], :, half * 512:(half + 1) * 512].rearrange("(c p) n -> p c n", p=P)
                m = u - OUT_UNIT0
                return w_out[0, m * 256:(m + 1) * 256, :].rearrange("(c p) n -> p c n", p=P)

            def load_mixer(u):
                slot = mix_slot(u)[0]
                src = mix_source(u)
                dst = up_ring[:, slot, :].rearrange("p (c n) -> p c n", c=src.shape[1])
                sp.dma_start(dst, src).then_inc(up_loaded[slot], 16)

            load_mixer(0)
            for name, _ in PARAMS:
                rows = rows128(mixer_small[name])
                sp.dma_start(prm_rows[ROW[name]:ROW[name] + rows.shape[0], :], rows).then_inc(rows_loaded, 16)
            sp.dma_start(tap_rows[0:CONV_K * CT, :], conv_w[0].rearrange("k (c n) -> (k c) n", n=P)
                          ).then_inc(rows_loaded, 16)

            def load_up(j, c, e):
                sp.dma_start(up_ring[:, UP_UNITS * j + c, :],
                             up_rows(e)[:, c, :]).then_inc(up_loaded[UP_UNITS * j + c], 16)

            def up_rows(e):
                return expert_w_up[0, bass.ds(e, 1)].rearrange("a (c p) n -> p (a c) n", p=P)

            def load_down(c, e):
                rows = expert_w_down[0, bass.ds(e, 1)].rearrange("a (c p) n -> p (a c) n", p=P)
                sp.dma_start(down_ring[:, c, :].rearrange("p (c n) -> p c n", c=2),
                             rows[:, 2 * c:2 * c + 2, :]).then_inc(down_loaded[c], 16)

            for u in range(1, MIX_UNITS):
                if u == 2:
                    sp.wait_ge(mats_loaded, 48)
                if u in range(UP_UNITS, UP_UNITS + UP_UNITS - MIX_SLOTS):
                    load_up(0, u - MIX_SLOTS, 0)
                if u == 25:
                    sp.wait_ge(conv_normed, 1)
                    load_down(3, 0)
                if u >= MIX_SLOTS:
                    sp.wait_ge(w_used, u - MIX_SLOTS + 1)
                load_mixer(u)
                if u >= MIX_UNITS - 3:
                    i = u - (MIX_UNITS - 3)
                    sp.wait_ge(proj_read, N_BRANCH + i + 1)
                    load_down(BRANCH_ORDER[i], 0)
            for c in range(MIX_SLOTS):
                sp.wait_ge(w_used, MIX_UNITS - MIX_SLOTS + c + 1)
                load_up(0, c, 0)
                if c == 0:
                    sp.wait_ge(merged_ready, 2)
                    for c4 in range(TEMP_SLOT, UP_SLOTS):
                        load_up(1, c4 - UP_UNITS, 1)
            for c in range(HI_SLOT, TEMP_SLOT):
                load_up(1, c - UP_UNITS, 1)
            def refill_up(q, j, e):
                for c in range(UP_UNITS):
                    sp.wait_ge(w_used, used_before(q - 2) + c + 1)
                    load_up(j, c, e)

            def refill_down(q, e):
                for c in range(DOWN_UNITS):
                    sp.wait_ge(w_used, used_before(q - 1) + UP_UNITS + c + 1)
                    load_down(c, e)

            with sp.Fori(1, AHEAD_PAIRS) as i:
                for j in range(2):
                    refill_up(2 * i + j, j, 2 * i + j)
                    refill_down(2 * i + j - 1, 2 * i + j - 1)
            q = 2 * AHEAD_PAIRS
            refill_up(q, 0, q)
            refill_down(q - 1, q - 1)
            refill_down(q, q)
            refill_up(q + 1, 1, q + 1)
            refill_down(q + 1, q + 1)
            with sp.Fori(AHEAD_PAIRS + 1, N_EXP // 2) as i:
                for j in range(2):
                    refill_up(2 * i + j, j, 2 * i + j)
                    refill_down(2 * i + j, 2 * i + j)

            sp.wait_ge(flag_ready, 1)
            overflow = sp.value_load(flag[0:1, 0:1], min_val=0, max_val=1)
            with sp.If(overflow > 0):
                with sp.Fori(1, ROUNDS) as r:
                    with sp.Fori(0, N_EXP // 2) as i:
                        for j in range(2):
                            q = N_EXP * r + 2 * i + j
                            refill_up(q, j, 2 * i + j)
                            refill_down(q, 2 * i + j)
                sp.wait_ge(w_used, used_before(ROUNDS * N_EXP))
            sp.wait_ge(w_used, used_before(N_EXP - 2) + UP_UNITS)
            sp.dma_start(up_ring[:, 4, :].rearrange("p (c n) -> p c n", c=2),
                         ple_proj_w[0].rearrange("(c p) n -> p c n", p=P)).then_inc(ple_proj_loaded, 16)
            for m in range(4):
                sp.dma_start(up_ring[:, m, :].rearrange("p (c n) -> p c n", c=2),
                             ple_gate_w[0, m * 256:(m + 1) * 256, :].rearrange("(c p) n -> p c n", p=P)
                             ).then_inc(ple_gate_loaded[m], 16)
            for a in range(TT):
                for h in range(2):
                    sp.wait_ge(final_ready, 2 * a + h + 1)
                    sp.dma_start(out[0, a * P:(a + 1) * P, h * 512:(h + 1) * 512],
                                 final_out[:, a, h * 512:(h + 1) * 512]).then_inc(stored, 16)
            sp.wait_ge(stored, 16 * 2 * TT)

        @block.gpsimd
        def _(pool):
            nc.gpsimd.memset(ident[:, :], 0.0).then_inc(pool_order, 1)
            nc.gpsimd.memset(before[:, :], 1.0).then_inc(pool_order, 1)
            nc.gpsimd.memset(ones[:, :], 1.0).then_inc(consts_ready, 1)
            nc.gpsimd.memset(mean_mat[:, :], 1.0 / CH).then_inc(consts_ready, 1)
            nc.gpsimd.iota(slot_ids[:, :, :], [[0, 2], [1, SLOTS]], base=0, channel_multiplier=0,
                           allow_small_or_imprecise_dtypes=True).then_inc(consts_ready, 1)
            nc.gpsimd.memset(z_pool[:, :, 0:POOL_PAD], 0.0).then_inc(consts_ready, 1)
            nc.gpsimd.memset(y_pad[:, :, 0:CONV_K - 1], 0.0).then_inc(consts_ready, 1)
            pool.wait_ge(pool_order, 2)
            nc.gpsimd.affine_select(out=ident[:, :], in_=ident[:, :], compare_op=ALU.not_equal, fill=1.0,
                                    base=0, pattern=[[-1, P]], channel_multiplier=1).then_inc(consts_ready, 1)
            nc.gpsimd.affine_select(out=before[:, :], in_=before[:, :], compare_op=ALU.is_gt, fill=0.0,
                                    base=0, pattern=[[1, P]], channel_multiplier=-1).then_inc(consts_ready, 1)
            pool.dma_start(sgu_in[:, :, :], sgu_w[0].rearrange("h t s -> t h s")).then_inc(sgu_loaded, 16)
            pool.dma_start(sgub[:, :, :], on_all(sgu_b[0])).then_inc(sgu_loaded, 16)
            pool.dma_start(p_sb[:, :, :], p[0, 0].rearrange("(a p) d -> p a d", p=P)).then_inc(p_loaded, 16)
            pool.dma_start(v_bias, on_all(b_in[0, 2048:2560])).then_inc(vbc_loaded, 16)
            pool.dma_start(v_gain, on_all(sgu_norm_g[0])).then_inc(vbc_loaded, 16)
            pool.dma_start(v_shift, on_all(sgu_norm_b[0])).then_inc(vbc_loaded, 16)
            pool.dma_start(pool_mix[:, :, :], pool_w[0].rearrange("g c d -> c g d")).then_inc(mats_loaded, 16)
            pool.dma_start(rw[:, :, :], router_w[0].rearrange("(c p) e -> p c e", p=P)).then_inc(mats_loaded, 16)
            pool.dma_start(rb[:, :], on_all(router_b[0])).then_inc(mats_loaded, 16)
            pool.wait_ge(sgu_loaded, 32)
            nc.gpsimd.affine_select(out=sgu_in[:, :, :], in_=sgu_in[:, :, :], compare_op=ALU.is_ge, fill=0.0,
                                    base=0, pattern=[[0, 4], [-1, P]], channel_multiplier=1).then_inc(sgu_masked, 1)
            nc.gpsimd.iota(inv_count[:, :, :], [[0, 4], [1, T]], base=1, channel_multiplier=0,
                           allow_small_or_imprecise_dtypes=True).then_inc(pool_order, 1)
            pool.wait_ge(pool_order, 3)
            for g in range(4):
                last = nc.gpsimd.tensor_scalar(inv_count[:, g, :], inv_count[:, g, :], float(2 << g), None, ALU.min)
            last.then_inc(count_ready, 1)

            def split(u):
                pool.wait_ge(w_hi_ready, u + 1)
                w_lo_part(nc.gpsimd, u).then_inc(w_lo_pool, 1)

            split(GPSIMD_FIRST)
            pool.wait_ge(chunk_read, 2)
            nc.gpsimd.tensor_tensor(sum2[:, :, 1:PW], z_pool[:, :, 1:PW], z_pool[:, :, 0:PW - 1],
                                    ALU.add).then_inc(pool_order, 1)
            pool.wait_ge(pool_order, 4)
            nc.gpsimd.tensor_tensor(sum4[:, :, 3:PW], sum2[:, 1:4, 3:PW], sum2[:, 1:4, 1:PW - 2],
                                    ALU.add).then_inc(pool_order, 1)
            pool.wait_ge(pool_order, 5)
            nc.gpsimd.tensor_tensor(sum8[:, :, 7:PW], sum4[:, 1:3, 7:PW], sum4[:, 1:3, 3:PW - 4],
                                    ALU.add).then_inc(pool_order, 1)
            pool.wait_ge(pool_order, 6)
            nc.gpsimd.tensor_tensor(sum16[:, :, 15:PW], sum8[:, 1:2, 15:PW], sum8[:, 1:2, 7:PW - 8],
                                    ALU.add).then_inc(pool_order, 1)
            pool.wait_ge(pool_order, 7)
            pool.wait_ge(inv_ready, 1)
            pool.wait_ge(a_read, 1)
            for g, s in enumerate((sum2, sum4, sum8, sum16)):
                nc.gpsimd.tensor_tensor(pooled[:, g, :], s[:, 0, POOL_PAD:PW], inv_count[:, g, :],
                                        ALU.mult).then_inc(pool_order, 1)
            pool.wait_ge(pool_order, 11)
            nc.gpsimd.tensor_tensor(pooled[:, :, :], pooled[:, :, :], z_pool[:, :, POOL_PAD:PW],
                                    ALU.subtract).then_inc(pooled_ready, 1)
            for u in range(GPSIMD_FIRST + 1, MIX_UNITS):
                if u == 15:
                    pool.wait_ge(ya_hi_ready, 1)
                    nc.gpsimd.tensor_tensor(ya_lo[:, :, :], yaT[:, :, :], ya_hi[:, :, :].bitcast(F32),
                                            ALU.subtract).then_inc(ya_lo_ready, 1)
                if u == 21:
                    pool.wait_ge(yb_hi_ready, 1)
                    nc.gpsimd.tensor_tensor(yb_lo[:, :, :], convT[:, :, :], yb_hi[:, :, :].bitcast(F32),
                                            ALU.subtract).then_inc(yb_lo_ready, 1)
                if u in (27, 30):
                    d = 0 if u == 27 else 4
                    pool.wait_ge(m_hi_ready, d // 4 + 1)
                    nc.gpsimd.tensor_tensor(m_lo[:, d:d + 4, :], hT[:, d:d + 4, :],
                                            m_hi[:, d:d + 4, :].bitcast(F32), ALU.subtract).then_inc(m_lo_ready, 1)
                if lo_by_gpsimd(u):
                    split(u)

        @block.scalar
        def _(act):
            steps = [0]

            def own(ins):
                steps[0] += 1
                ins.then_inc(act_order, 1)
                act.wait_ge(act_order, steps[0])

            def square_sum(a):
                own(nc.scalar.activation(xs[:, a, :], x_sb[:, a, :], ACT.Square, accum_out=ssq[:, a:a + 1]))

            def root():
                return nc.scalar.activation(rms, ssq, ACT.Sqrt, bias=eps, scale=1.0 / D)

            def scale_high(bank, gain, dst=hT):
                for k in range(4, KT):
                    last = nc.scalar.activation(dst[:, k, :], ps[:, bank + k // 2, 256 * (k % 2):256 * (k % 2) + 256], ACT.Copy,
                                                scale=prm[:, gain + k:gain + k + 1])
                last.then_inc(hT_act, 1)

            act.wait_ge(eps_ready, 1)
            nc.scalar.activation(small[:, 34:35], eps, ACT.Sqrt)
            act.wait_ge(x_loaded, 16)
            for a in range(TT):
                square_sum(a)
            root().then_inc(rms_ready, 1)

            def split(u):
                slot, turn = mix_slot(u)
                act.wait_ge(up_loaded[slot], 16 * turn)
                if u >= HI_BUFS:
                    act.wait_ge(w_used, u - HI_BUFS + 1)
                nc.scalar.activation(w_hi[:, u % HI_BUFS, :], up_ring[:, slot, :], ACT.Copy
                                     ).then_inc(w_hi_ready, 1)

            split(0)
            act.wait_ge(xsT_done, 1)
            act.wait_ge(prm_ready, 1)
            scale_high(4, ROW["mix_norm"], h_hi)
            for u in range(1, HI_BUFS):
                split(u)

            act.wait_ge(consts_ready, 7)
            for n, (name, col) in enumerate(CHUNKS):
                split(2 * n + 3)
                if n == 9:
                    act.wait_ge(v_var_ready, 1)
                    nc.scalar.activation(vrms, vmv.rearrange("p (a b) -> p a b", b=2)[:, :, 1], ACT.Sqrt,
                                         bias=eps).then_inc(v_rms_ready, 1)
                    act.wait_ge(centred, 1)
                    nc.scalar.activation(squares[:, :, :], convT[:, :, :], ACT.Square).then_inc(sq_ready, 1)
                if n == 10:
                    act.wait_ge(ycT_ready, 1)
                    nc.scalar.activation(yc_hi[:, :, :], uT[:, :, :], ACT.Copy).then_inc(yc_hi_ready, 1)
                act.wait_ge(w_used, 2 * n + 2)
                split(2 * n + 4)
                if name == "a":
                    continue
                bank = 2 * (n % 2)
                tile4 = quarter(bank)
                if name == "v":
                    last = nc.scalar.activation(v_sb[:, :, :], ps[:, bank:bank + 2, :], ACT.Copy)
                for c in range(CT):
                    if name == "v":
                        break
                    bias = prm[:, ROW["b_in"] + col // P + c:ROW["b_in"] + col // P + c + 1]
                    func = ACT.Sigmoid if name in ("gate", "g") else ACT.Identity
                    if name == "gate":
                        dst = sig_gate[:, c, :]
                    elif name == "pool":
                        dst = z_pool[:, c, POOL_PAD:PW]
                    elif name == "u":
                        dst = uT[:, c, :]
                    else:
                        k, d0 = divmod(col - 2560, D)
                        dst = gates[:, k, d0 // P + c, :]
                    last = nc.scalar.activation(dst, tile4[:, c, :], func, bias=bias)
                last.then_inc(chunk_read, 1)
                if n == 6:
                    act.wait_ge(pool_mixed, 1)
                    for c in range(CT):
                        row = ROW["pool_scale"] + c
                        last = nc.scalar.activation(yaT[:, c, :], quarter(4)[:, c, :], ACT.Copy,
                                                    scale=prm[:, row:row + 1])
                    last.then_inc(yaT_ready, 1)
                    act.wait_ge(yaT_ready, 1)
                    nc.scalar.activation(ya_hi[:, :, :], yaT[:, :, :], ACT.Copy).then_inc(ya_hi_ready, 1)
                if n == 9:
                    act.wait_ge(var_done, 1)
                    nc.scalar.activation(conv_rstd, ps[:, 5, 0:T], ACT.Sqrt, bias=eps).then_inc(conv_rms_ready, 1)
                    act.wait_ge(conv_normed, 1)
                    for c in range(CT):
                        g, b = ROW["conv_norm_g"] + c, ROW["conv_norm_b"] + c
                        last = nc.scalar.activation(convT[:, c, :], convT[:, c, :], ACT.Silu,
                                                    scale=prm[:, g:g + 1], bias=prm[:, b:b + 1])
                    last.then_inc(ybT_ready, 1)
                    act.wait_ge(ybT_ready, 1)
                    nc.scalar.activation(yb_hi[:, :, :], convT[:, :, :], ACT.Copy).then_inc(yb_hi_ready, 1)

            for u in range(BRANCH_UNIT0 + 3, MIX_UNITS):
                if u in (28, 31):
                    d = 0 if u == 28 else 4
                    act.wait_ge(merged_ready, d // 4 + 1)
                    nc.scalar.activation(m_hi[:, d:d + 4, :], hT[:, d:d + 4, :], ACT.Copy).then_inc(m_hi_ready, 1)
                split(u)

            for c in range(4):
                act.dma_start(b_up[N_EXP * c:N_EXP * (c + 1), :],
                              expert_b_up[0, :, 512 * c:512 * (c + 1)]).then_inc(bup_loaded, 16)
            act.dma_start(b_down[0], expert_b_down[0, :, 0:512]).then_inc(bdown_loaded, 16)
            for a in range(TT):
                act.wait_ge(x_ready, a + 1)
                square_sum(a)
            act.wait_ge(xsT_done, 2)
            scale_high(0, ROW["moe_norm"])
            root().then_inc(rms_ready, 1)
            act.wait_ge(logits_done, 1)
            act.dma_start(b_down[1], expert_b_down[0, :, 512:1024]).then_inc(bdown_loaded, 16)
            act.wait_ge(top_ready, 1)
            nc.scalar.activation(top_e[:, :, :], top_e[:, :, :], ACT.Exp).then_inc(top_exp, 1)
            act.wait_ge(gateT_done, 1)
            nc.scalar.activation(gateT, ps[0:N_EXP, WT, 0:T], ACT.Copy).then_inc(gateT_ready, 1)

            def expert(q):
                act.wait_ge(glu_ready, q + 1)
                wait_past(act, prod_ready, 2 * q)
                nc.scalar.activation(sig, glu, ACT.Sigmoid, scale=ALPHA).then_inc(sig_ready, 1)
                act.wait_ge(actT_done, q + 1)
                act.wait_ge(w_used, used_before(q))
                nc.scalar.activation(actT[:, :, :, :].rearrange("p m g s -> p (m g s)"), ps[:, ACTT, :],
                                     ACT.Copy).then_inc(actT_ready, 1)
                act.wait_ge(weightT_done, q + 1)
                act.wait_ge(comb_done, comb_before(q))
                nc.scalar.activation(weightT[:, :, :].rearrange("p a t -> p (a t)"), ps[:, WT, 0:2 * P],
                                     ACT.Copy).then_inc(weightT_ready, 1)
                act.wait_ge(w_used, used_before(q + 1))
                nc.scalar.activation(y_sb, ps[:, Y, :], ACT.Copy).then_inc(y_ready, 1)

            for q in range(2):
                expert(q)
            with act.Fori(1, N_EXP // 2) as i:
                for j in range(2):
                    expert(2 * i + j)
            act.wait_ge(flag_ready, 1)
            overflow = act.value_load(flag[0:1, 0:1], min_val=0, max_val=1)
            with act.If(overflow > 0):
                with act.Fori(N_EXP // 2, ROUNDS * N_EXP // 2) as i:
                    for j in range(2):
                        expert(2 * i + j)

            for a in range(TT):
                act.wait_ge(x_final, a + 1)
                if a == 0:
                    act.dma_start(final_gain, on_all(final_norm)).then_inc(gain_loaded, 16)
                square_sum(a)
            act.wait_ge(xsT_done, 3)
            scale_high(0, ROW["ple_norm"])
            root().then_inc(rms_ready, 1)
            act.wait_ge(rstd_ready, 2)
            for a in range(TT):
                for h in range(2):
                    act.wait_ge(ple_gate_done, 2 * a + h + 1)
                    nc.scalar.activation(ple_sig[:, a, h * 512:(h + 1) * 512], ps[:, 2 * a + h, :],
                                         ACT.Sigmoid, scale=rstd[:, a:a + 1]).then_inc(ple_sig_ready, 1)
            for a in range(TT):
                for h in range(2):
                    act.wait_ge(ple_x_ready, 2 * a + h + 1)
                    own(nc.scalar.activation(xs[:, a, h * 512:(h + 1) * 512], x_sb[:, a, h * 512:(h + 1) * 512],
                                             ACT.Square, accum_out=half_ssq[:, 2 * a + h:2 * a + h + 1]))
                own(nc.scalar.activation(ssq[:, a:a + 1], half_ssq[:, 2 * a:2 * a + 1], ACT.Identity,
                                         bias=half_ssq[:, 2 * a + 1:2 * a + 2]))
                nc.scalar.activation(rms[:, a:a + 1], ssq[:, a:a + 1], ACT.Sqrt, bias=eps,
                                     scale=1.0 / D).then_inc(final_rms, 1)

        @block.vector
        def _(dve):
            steps = [0]

            def own(ins):
                steps[0] += 1
                ins.then_inc(dve_order, 1)
                dve.wait_ge(dve_order, steps[0])

            def normalise(n):
                dve.wait_ge(rms_ready, n)
                if n == 1:
                    own(nc.vector.reciprocal(rstd, rms))
                for a in range(TT):
                    last = nc.vector.tensor_scalar(xs[:, a, :], x_sb[:, a, :], rstd[:, a:a + 1], None, ALU.mult)
                last.then_inc(xs_ready, 1)

            def scale_low(n, bank, gain, dst=hT):
                dve.wait_ge(xsT_done, n)
                for k in range(4):
                    last = nc.vector.tensor_scalar(dst[:, k, :], ps[:, bank + k // 2, 256 * (k % 2):256 * (k % 2) + 256],
                                                   prm[:, gain + k:gain + k + 1], None, ALU.mult)
                last.then_inc(hT_dve, 1)

            nc.vector.memset(eps, EPS).then_inc(eps_ready, 1)
            dve.wait_ge(consts_ready, 7)
            nc.vector.tensor_reduce(fold[:, :], ident[:, :].rearrange("p (c e) -> p e c", c=4), axis=AX,
                                    op=ALU.add).then_inc(fold_ready, 1)
            dve.wait_ge(x_loaded, 16)
            normalise(1)

            def split(u):
                dve.wait_ge(w_hi_ready, u + 1)
                w_lo_part(nc.vector, u).then_inc(w_lo_dve, 1)

            split(0)
            dve.wait_ge(rowsT_done, 1)
            nc.vector.tensor_copy(prm[:, :], ps[:, 0, 0:N_ROWS]).then_inc(prm_ready, 1)
            nc.vector.tensor_copy(conv_taps[:, :, :].rearrange("p k c -> p (k c)"),
                                  ps[:, 0, P:P + CONV_K * CT]).then_inc(taps_ready, 1)
            dve.wait_ge(prm_ready, 1)
            scale_low(1, 4, ROW["mix_norm"], h_hi)
            dve.wait_ge(hT_dve, 1)
            for k in range(KT):
                if k == 4:
                    dve.wait_ge(hT_act, 1)
                g = ROW["mix_norm"] + k
                last = nc.vector.scalar_tensor_tensor(
                    out=h_lo[:, k, :], in0=ps[:, 4 + k // 2, 256 * (k % 2):256 * (k % 2) + 256],
                    scalar=prm[:, g:g + 1], in1=h_hi[:, k, :].bitcast(F32), op0=ALU.mult, op1=ALU.subtract)
            last.then_inc(h_lo_ready, 1)

            for u in range(1, HI_BUFS):
                split(u)
            dve.wait_ge(count_ready, 1)
            nc.vector.reciprocal(inv_count[:, :, :], inv_count[:, :, :]).then_inc(inv_ready, 1)
            dve.wait_ge(pT_done, 1)
            nc.vector.tensor_copy(pT[:, :, :].rearrange("p a t -> p (a t)"), ps[:, 4, :])
            dve.wait_ge(sguT_done, 1)
            nc.vector.tensor_copy(sguT[:, :, :].rearrange("p h t -> p (h t)"), ps[:, 5, :]).then_inc(sguT_ready, 1)
            for u in range(HI_BUFS, CONV_UNIT):
                split(u)

            dve.wait_ge(w_used, 4)
            dve.wait_ge(chunk_read, 1)
            dve.wait_ge(consts_ready, 7)
            for c in range(CT):
                b = ROW["b_in"] + 4 + c
                last = nc.vector.scalar_tensor_tensor(out=y_pad[:, c, CONV_K - 1:CW], in0=quarter(2)[:, c, :],
                                                      scalar=prm[:, b:b + 1], in1=sig_gate[:, c, :],
                                                      op0=ALU.add, op1=ALU.mult)
            last.then_inc(a_read, 1)
            dve.wait_ge(a_read, 1)
            dve.wait_ge(taps_ready, 1)
            for c in range(CT):
                b = ROW["conv_b"] + c
                nc.vector.tensor_scalar(convT[:, c, :], y_pad[:, c, 0:T], conv_taps[:, 0, c:c + 1],
                                        prm[:, b:b + 1], ALU.mult, ALU.add).then_inc(conv_step, 1)
            tap = 1
            for i, taps in enumerate(CONV_TAPS):
                with dve.Fori(tap, tap + taps) as k:
                    for c in range(CT):
                        dve.wait_ge(conv_step, 4 * k + (c - 3))
                        nc.vector.scalar_tensor_tensor(out=convT[:, c, :], in0=y_pad[:, c, bass.ds(k, T)],
                                                       scalar=conv_taps[:, bass.ds(k, 1), c],
                                                       in1=convT[:, c, :], op0=ALU.mult, op1=ALU.add
                                                       ).then_inc(conv_step, 1)
                tap += taps
                if not lo_by_gpsimd(CONV_UNIT + i):
                    split(CONV_UNIT + i)
            split(CONV_UNIT + len(CONV_TAPS))

            dve.wait_ge(chunk_read, 3)
            dve.wait_ge(vbc_loaded, 48)
            for a in range(TT):
                own(nc.vector.tensor_tensor(v_sb[:, a, :], v_sb[:, a, :], v_bias, ALU.add))
                own(nc.vector.bn_stats(vstat[:, 6 * a:6 * a + 6], v_sb[:, a, :]))
                last = nc.vector.bn_aggr(vmv[:, 2 * a:2 * a + 2], vstat[:, 6 * a:6 * a + 6])
            last.then_inc(v_var_ready, 1)
            dve.wait_ge(mean_done, 1)
            nc.vector.tensor_tensor(convT[:, :, :], convT[:, :, :],
                                    ps[:, 4:5, 0:T].to_broadcast([P, CT, T]), ALU.subtract).then_inc(centred, 1)
            split(BRANCH_UNIT0 - 1)
            dve.wait_ge(v_rms_ready, 1)
            own(nc.vector.reciprocal(vrstd, vrms))
            for a in range(TT):
                own(nc.vector.tensor_scalar(v_sb[:, a, :], v_sb[:, a, :], vmv[:, 2 * a:2 * a + 1],
                                            vrstd[:, a:a + 1], ALU.subtract, ALU.mult))
                own(nc.vector.tensor_tensor(v_sb[:, a, :], v_sb[:, a, :], v_gain, ALU.mult))
                last = nc.vector.tensor_tensor(v_sb[:, a, :], v_sb[:, a, :], v_shift, ALU.add)
            last.then_inc(v_ready, 1)

            dve.wait_ge(conv_rms_ready, 1)
            own(nc.vector.reciprocal(conv_rstd, conv_rstd))
            nc.vector.tensor_tensor(convT[:, :, :], convT[:, :, :],
                                    conv_rstd.rearrange("p (a t) -> p a t", a=1).to_broadcast([P, CT, T]),
                                    ALU.mult).then_inc(conv_normed, 1)
            split(BRANCH_UNIT0)
            dve.wait_ge(sgu_done, 1)
            dve.wait_ge(sgu_loaded, 32)
            dve.wait_ge(pooled_ready, 1)
            for n in range(TT):
                own(nc.vector.tensor_tensor(sgu_mix[:, :, n * P:(n + 1) * P], quarter(6)[:, :, n * P:(n + 1) * P],
                                            sgub[:, :, :], ALU.add))
            dve.wait_ge(chunk_read, 4)
            nc.vector.tensor_tensor(uT[:, :, :], uT[:, :, :], sgu_mix[:, :, :], ALU.mult).then_inc(ycT_ready, 1)
            dve.wait_ge(yc_hi_ready, 1)
            nc.vector.tensor_tensor(yc_lo[:, :, :], uT[:, :, :], yc_hi[:, :, :].bitcast(F32),
                                    ALU.subtract).then_inc(yc_lo_ready, 1)

            dve.wait_ge(chunk_read, N_CHUNKS - 1)
            for i in range(2 * N_BRANCH):
                if not lo_by_gpsimd(BRANCH_UNIT0 + 2 + i):
                    split(BRANCH_UNIT0 + 2 + i)
                half, j = divmod(i, N_BRANCH)
                br = BRANCH_ORDER[j]
                tiles = hT[:, CT * half:CT * half + CT, :]
                dve.wait_ge(w_used, BRANCH_UNIT0 + i + 1)
                for c in range(CT):
                    d = CT * half + c
                    b = ROW["branch_b"] + KT * br + d
                    dst = hT[:, d, :] if j == 0 else gated[:, c, :]
                    last = nc.vector.scalar_tensor_tensor(out=dst, in0=quarter(branch_bank(i))[:, c, :],
                                                          scalar=prm[:, b:b + 1], in1=gates[:, br, d, :],
                                                          op0=ALU.add, op1=ALU.mult)
                last.then_inc(proj_read, 1)
                dve.wait_ge(proj_read, i + 1)
                if j > 0:
                    last = nc.vector.tensor_tensor(tiles, tiles, gated[:, :, :], ALU.add)
                    if j == N_BRANCH - 1:
                        last.then_inc(merged_ready, 1)
                        dve.wait_ge(merged_ready, half + 1)
                    else:
                        own(last)
            for u in range(BRANCH_UNIT0 + 2 + 2 * N_BRANCH, MIX_UNITS):
                split(u)
            dve.wait_ge(w_used, MIX_UNITS)
            for a in range(TT):
                nc.vector.tensor_tensor(x_sb[:, a, :], x_sb[:, a, :],
                                        ps[:, 4 + 2 * a:6 + 2 * a, :].rearrange("p a b -> p (a b)"),
                                        ALU.add).then_inc(x_ready, 1)

            scale_low(2, 0, ROW["moe_norm"])
            dve.wait_ge(rms_ready, 2)
            nc.vector.reciprocal(rstd, rms).then_inc(rstd_ready, 1)
            dve.wait_ge(rstd_ready, 1)

            dve.wait_ge(partial_done, 1)
            nc.vector.tensor_copy(partial, ps[:, 4, 0:T]).then_inc(partial_ready, 1)
            normalise(2)

            dve.wait_ge(logits_done, 1)
            for a in range(TT):
                own(nc.vector.scalar_tensor_tensor(out=logits[:, a, :], in0=ps[:, 5, N_EXP * a:N_EXP * (a + 1)],
                                                   scalar=rstd[:, a:a + 1], in1=rb[:, :], op0=ALU.mult,
                                                   op1=ALU.add))
            for a in range(TT):
                own(nc.vector.max(top[:, a, :], logits[:, a, :]))
                own(nc.vector.max_index(top_i[:, a, :], top[:, a, :], logits[:, a, :]))
            nc.vector.tensor_tensor(top_e[:, :, :], top[:, :, 0:TOP_K],
                                    top[:, :, 0:1].to_broadcast([P, TT, TOP_K]), ALU.subtract).then_inc(top_ready, 1)
            own(nc.vector.tensor_copy(top_f[:, :, :], top_i[:, :, :]))
            for a in range(TT):
                own(nc.vector.tensor_tensor(onehot[:, a, :, :],
                                            slot_ids[:, 0:1, 0:N_EXP].to_broadcast([P, TOP_K, N_EXP]),
                                            top_f[:, a, 0:TOP_K].unsqueeze(2).to_broadcast([P, TOP_K, N_EXP]),
                                            ALU.is_equal))
            for a in range(TT):
                last = nc.vector.tensor_reduce(chosen[:, a, :], onehot[:, a, :, :].rearrange("p j e -> p e j"),
                                               axis=AX, op=ALU.add)
            last.then_inc(chosen_ready, 1)
            dve.wait_ge(pos_done, 1)
            own(nc.vector.tensor_copy(pos0[:, :, :], ps[:, 1, 0:TT * N_EXP].rearrange("p (a e) -> p a e", a=TT)))
            own(nc.vector.scalar_tensor_tensor(out=pos0[:, :, :], in0=pos0[:, :, :], scalar=1.0,
                                               in1=chosen[:, :, :], op0=ALU.add, op1=ALU.mult))
            for r in range(ROUNDS):
                nc.vector.tensor_scalar(pos[:, :, N_EXP * r:N_EXP * (r + 1)], pos0[:, :, :],
                                        -1.0 - SLOTS * r, None, ALU.add)
            own(nc.vector.memset(pos[:, :, ROUNDS * N_EXP:QPAD], -1.0))

            def make_select(q):
                for a in range(TT):
                    last = nc.vector.tensor_scalar(select_of(q)[:, a, :], slot_ids[:, 0, :],
                                                   pos[:, a, bass.ds(q, 1)], None, ALU.is_equal)
                last.then_inc(select_ready, 1)

            half = [0]

            def select_of(q):
                return select[:, half[0]]

            make_select(0)
            dve.wait_ge(top_exp, 1)
            own(nc.vector.tensor_reduce(wsum, top_e[:, :, :], axis=AX, op=ALU.add))
            own(nc.vector.reciprocal(wrec, wsum))
            own(nc.vector.tensor_tensor(top_e[:, :, :], top_e[:, :, :],
                                        wrec.unsqueeze(2).to_broadcast([P, TT, TOP_K]), ALU.mult))
            for a in range(TT):
                own(nc.vector.tensor_tensor(weighted[:, a, :, :], onehot[:, a, :, :],
                                            top_e[:, a, :].unsqueeze(2).to_broadcast([P, TOP_K, N_EXP]), ALU.mult))
            for a in range(TT):
                own(nc.vector.tensor_reduce(gate_w[:, a, 0:N_EXP], weighted[:, a, :, :].rearrange("p j e -> p e j"),
                                            axis=AX, op=ALU.add))
            for r in range(1, ROUNDS):
                last = nc.vector.tensor_copy(gate_w[:, :, N_EXP * r:N_EXP * (r + 1)], gate_w[:, :, 0:N_EXP])
            last.then_inc(gates_ready, 1)
            dve.wait_ge(gates_ready, 1)

            def scale_xe(q, b):
                dve.wait_ge(gather_done, q + 1)
                gain = prm[:, ROW["moe_norm"]:ROW["moe_norm"] + KT].unsqueeze(2).to_broadcast([P, KT, SLOTS])
                nc.vector.tensor_tensor(xe[:, b, :, :], ps[:, GATHER, :].rearrange("p (k s) -> p k s", k=KT),
                                        gain, ALU.mult).then_inc(xe_ready, 1)

            scale_xe(0, 0)
            dve.wait_ge(totals_done, 1)
            own(nc.vector.reduce_max(most, ps[:, 6, 0:N_EXP], AX))
            nc.vector.tensor_scalar(flag[:, 0:1], most, float(SLOTS), None, ALU.is_gt).then_inc(flag_ready, 1)
            def expert(q, e, j):
                wait_past(dve, up_done, q)
                nc.vector.tensor_copy(pick_bias[:, :, :],
                                      ident_e[:, :, bass.ds(e, 1)].to_broadcast([P, 4, SLOTS])).then_inc(pick_ready, 1)
                wait_past(dve, weightT_done, q)
                for a in range(TT):
                    last = nc.vector.tensor_scalar(weight[:, a, :], slot_ids[:, :, :].rearrange("p a s -> p (a s)"),
                                                   pos[:, a, bass.ds(q, 1)], gate_w[:, a, bass.ds(q, 1)],
                                                   ALU.is_equal, ALU.mult)
                last.then_inc(weight_ready, 1)
                dve.wait_ge(gather_done, q + 1)
                half[0] = 1 - j
                make_select(q + 1)
                dve.wait_ge(up_done, q + 1)
                nc.vector.tensor_scalar(glu, ps[:, GLU, :], LIMIT, None, ALU.min).then_inc(glu_ready, 1)
                nc.vector.tensor_scalar(lin, ps[:, LIN, :], LIMIT, -LIMIT, ALU.min, ALU.max).then_inc(lin_ready, 1)
                dve.wait_ge(glu_ready, q + 1)
                dve.wait_ge(lin_ready, q + 1)
                nc.vector.scalar_tensor_tensor(out=lin, in0=lin, scalar=1.0, in1=glu, op0=ALU.add,
                                               op1=ALU.mult).then_inc(prod_ready, 1)
                dve.wait_ge(prod_ready, 2 * q + 1)
                dve.wait_ge(sig_ready, q + 1)
                nc.vector.tensor_tensor(lin, lin, sig, ALU.mult).then_inc(prod_ready, 1)
                add_result(q - 1, 0)
                scale_xe(q + 1, 1 - j)
                add_result(q - 1, 1)

            def add_result(q, a, done=x_added):
                dve.wait_ge(comb_done, comb_before(q) + a + 1)
                nc.vector.tensor_tensor(x_sb[:, a, :], x_sb[:, a, :],
                                        ps[:, COMB:COMB + 2, :].rearrange("p a b -> p (a b)"),
                                        ALU.add).then_inc(done, 1)

            for q in range(2):
                expert(q, q, q)
            with dve.Fori(1, N_EXP // 2) as i:
                for j in range(2):
                    expert(2 * i + j, 2 * i + j, j)
            overflow = dve.value_load(flag[0:1, 0:1], min_val=0, max_val=1)
            with dve.If(overflow > 0):
                with dve.Fori(1, ROUNDS) as r:
                    with dve.Fori(0, N_EXP // 2) as i:
                        for j in range(2):
                            expert(N_EXP * r + 2 * i + j, 2 * i + j, j)
                for a in range(TT):
                    add_result(ROUNDS * N_EXP - 1, a, x_final)
            with dve.If(overflow < 1):
                for a in range(TT):
                    add_result(N_EXP - 1, a, x_final)

            scale_low(3, 0, ROW["ple_norm"])
            dve.wait_ge(rms_ready, 3)
            nc.vector.reciprocal(rstd, rms).then_inc(rstd_ready, 1)
            for a in range(TT):
                for h in range(2):
                    cols = slice(h * 512, (h + 1) * 512)
                    dve.wait_ge(ple_sig_ready, 2 * a + h + 1)
                    own(nc.vector.tensor_tensor(ple_sig[:, a, cols], ple_sig[:, a, cols],
                                                ps[:, 4 + 2 * a + h, :], ALU.mult))
                    nc.vector.tensor_tensor(x_sb[:, a, cols], x_sb[:, a, cols], ple_sig[:, a, cols],
                                            ALU.add).then_inc(ple_x_ready, 1)
            dve.wait_ge(gain_loaded, 16)
            for a in range(TT):
                dve.wait_ge(final_rms, a + 1)
                own(nc.vector.reciprocal(frstd[:, a:a + 1], rms[:, a:a + 1]))
                for h in range(2):
                    cols = slice(h * 512, (h + 1) * 512)
                    nc.vector.scalar_tensor_tensor(out=final_out[:, a, cols], in0=x_sb[:, a, cols],
                                                   scalar=frstd[:, a:a + 1], in1=final_gain[:, cols],
                                                   op0=ALU.mult, op1=ALU.mult).then_inc(final_ready, 1)

        @block.tensor
        def _(pe):
            def transpose_tokens(src, a, bank):
                for k in range(KT):
                    col = 256 * (k % 2) + P * a
                    last = nc.tensor.transpose(ps[:, bank + k // 2, col:col + P], src[:, a, k * P:(k + 1) * P],
                                               ident[:, :])
                return last

            def hT_written(n):
                pe.wait_ge(hT_act, n)
                pe.wait_ge(hT_dve, n)

            pe.wait_ge(consts_ready, 7)
            pe.wait_ge(xs_ready, 1)
            transpose_tokens(xs, 0, 4)
            transpose_tokens(xs, 1, 4).then_inc(xsT_done, 1)
            pe.wait_ge(rows_loaded, 16 * (len(PARAMS) + 1))
            nc.tensor.transpose(ps[:, 0, 0:N_ROWS], prm_rows[0:N_ROWS, :], ident[0:N_ROWS, 0:N_ROWS])
            nc.tensor.transpose(ps[:, 0, P:P + CONV_K * CT], tap_rows[0:CONV_K * CT, :],
                                ident[0:CONV_K * CT, 0:CONV_K * CT]).then_inc(rowsT_done, 1)
            hT_written(1)

            def mixer_unit(u):
                if lo_by_gpsimd(u):
                    pe.wait_ge(w_lo_pool, lo_count(u, True))
                else:
                    pe.wait_ge(w_lo_dve, lo_count(u, False))
                return w_hi[:, u % HI_BUFS, :], w_lo[:, mix_slot(u)[0], :]

            for n, (name, col) in enumerate(CHUNKS):
                if n == 0:
                    pe.wait_ge(taps_ready, 1)
                elif n == 3:
                    pe.wait_ge(a_read, 1)
                elif n >= 2:
                    pe.wait_ge(chunk_read, n - 1 - (n > 2))
                bank = 2 * (n % 2)
                for s in range(2):
                    u = 2 * n + s
                    hi, lo = [w.rearrange("p (k n) -> p k n", k=KT) for w in mixer_unit(u)]
                    for c in range(2):
                        passes = [(w, h_hi, k) for k in range(KT) for w in (hi, lo)] + \
                                 [(hi, h_lo, k) for k in range(KT)]
                        for i, (w, h, k) in enumerate(passes):
                            if u == 0 and c == 0 and i == 2 * KT:
                                pe.wait_ge(h_lo_ready, 1)
                            start, stop = i == 0, i == len(passes) - 1
                            if name == "v":
                                last = nc.tensor.matmul(ps[:, bank + c, s * 256:(s + 1) * 256],
                                                        h[:, k, c * P:(c + 1) * P], w[:, k, :],
                                                        start=start, stop=stop)
                            else:
                                last = nc.tensor.matmul(quarter(bank)[:, 2 * s + c, :],
                                                        w[:, k, c * P:(c + 1) * P], h[:, k, :],
                                                        start=start, stop=stop)
                    last.then_inc(w_used, 1)
                    if u == 18:
                        pe.wait_ge(conv_step, 4 * CONV_K)
                        pe.wait_ge(yaT_ready, 1)
                        for c in range(CT):
                            last = nc.tensor.matmul(ps[:, 4, 0:T], mean_mat[:, :], convT[:, c, :], start=(c == 0),
                                                    stop=(c == CT - 1))
                        last.then_inc(mean_done, 1)
                    if u == 19:
                        pe.wait_ge(sq_ready, 1)
                        for c in range(CT):
                            last = nc.tensor.matmul(ps[:, 5, 0:T], mean_mat[:, :], squares[:, c, :],
                                                    start=(c == 0), stop=(c == CT - 1))
                        last.then_inc(var_done, 1)
                    if u == 20:
                        pe.wait_ge(v_ready, 1)
                        for h in range(4):
                            for a in range(TT):
                                last = nc.tensor.matmul(quarter(6)[:, h, a * P:(a + 1) * P],
                                                        v_sb[:, a, h * P:(h + 1) * P], sguT[:, h, :],
                                                        start=True, stop=True)
                        last.then_inc(sgu_done, 1)
                if n == 0:
                    pe.wait_ge(p_loaded, 16)
                    for k in range(PLE // P):
                        for a in range(TT):
                            last = nc.tensor.transpose(ps[:, 4, T * k + P * a:T * k + P * (a + 1)],
                                                       p_sb[:, a, k * P:(k + 1) * P], ident[:, :])
                    last.then_inc(pT_done, 1)
                    pe.wait_ge(sgu_masked, 1)
                    for h in range(4):
                        last = nc.tensor.transpose(ps[:, 5, P * h:P * (h + 1)], sgu_in[:, h, :], ident[:, :])
                    last.then_inc(sguT_done, 1)
                if n == 5:
                    pe.wait_ge(mats_loaded, 48)
                    pe.wait_ge(pooled_ready, 1)
                    pe.wait_ge(sguT_ready, 1)
                    for g in range(4):
                        last = nc.tensor.matmul(quarter(4)[:, g, :], pool_mix[:, g, :], pooled[:, g, :],
                                                start=True, stop=True)
                    last.then_inc(pool_mixed, 1)

            results = {POOL_BR: (ya_hi, ya_lo, ya_lo_ready), CONV_BR: (yb_hi, yb_lo, yb_lo_ready),
                       SGU_BR: (yc_hi, yc_lo, yc_lo_ready)}
            for i in range(2 * N_BRANCH):
                y_hi, y_lo, y_split = results[BRANCH_ORDER[i % N_BRANCH]]
                pe.wait_ge(y_split, 1)
                if i < 2:
                    pe.wait_ge(chunk_read, N_CHUNKS - 2 + i)
                else:
                    pe.wait_ge(proj_read, i - 1)
                hi, lo = [w.rearrange("p (c n) -> p c n", c=CT) for w in mixer_unit(BRANCH_UNIT0 + i)]
                for t in range(CT):
                    passes = [(w, y, c) for c in range(CT) for w, y in ((hi, y_hi), (hi, y_lo), (lo, y_hi))]
                    for m, (w, y, c) in enumerate(passes):
                        last = nc.tensor.matmul(quarter(branch_bank(i))[:, t, :], w[:, c, t * P:(t + 1) * P],
                                                y[:, c, :], start=(m == 0), stop=(m == len(passes) - 1))
                last.then_inc(w_used, 1)
            for m in range(KT // 2):
                pe.wait_ge(m_lo_ready, m // 2 + 1)
                hi, lo = [w.rearrange("p (c n) -> p c n", c=2) for w in mixer_unit(OUT_UNIT0 + m)]
                for a in range(TT):
                    for h in range(2):
                        for s in range(2):
                            d = 2 * m + s
                            for i, (y, w) in enumerate(((m_hi, hi), (m_hi, lo), (m_lo, hi))):
                                last = nc.tensor.matmul(ps[:, 4 + 2 * a + h, :], y[:, d, a * P:(a + 1) * P],
                                                        w[:, s, h * 512:(h + 1) * 512], start=(d + i == 0),
                                                        stop=(d + i == KT + 1))
                last.then_inc(w_used, 1)

            for a in range(TT):
                pe.wait_ge(x_ready, a + 1)
                last = transpose_tokens(x_sb, a, 0)
            last.then_inc(xsT_done, 1)
            hT_written(2)
            for half in range(2):
                for g in range(4):
                    k = 4 * half + g
                    last = nc.tensor.matmul(ps[32 * g:32 * g + 32, 4, 0:T], rw[:, k, :], hT[:, k, :],
                                            start=(half == 0), stop=(half == 1))
            last.then_inc(partial_done, 1)
            pe.wait_ge(partial_ready, 1)
            pe.wait_ge(fold_ready, 1)
            for a in range(TT):
                last = nc.tensor.matmul(ps[:, 5, N_EXP * a:N_EXP * (a + 1)], partial[:, a * P:(a + 1) * P],
                                        fold[:, :], start=True, stop=True)
            last.then_inc(logits_done, 1)
            pe.wait_ge(chosen_ready, 1)
            nc.tensor.matmul(ps[:, 1, 0:N_EXP], before[:, :], chosen[:, 0, :], start=True, stop=True)
            nc.tensor.matmul(ps[:, 1, N_EXP:2 * N_EXP], ones[:, :], chosen[:, 0, :], start=True, stop=False)
            nc.tensor.matmul(ps[:, 1, N_EXP:2 * N_EXP], before[:, :], chosen[:, 1, :], start=False,
                             stop=True).then_inc(pos_done, 1)

            def gather(q, b):
                pe.wait_ge(select_ready, q + 1)
                wait_past(pe, xe_ready, q)
                for k in range(KT):
                    for a in range(TT):
                        last = nc.tensor.matmul(ps[:, GATHER, k * SLOTS:(k + 1) * SLOTS],
                                                xs[:, a, k * P:(k + 1) * P], select[:, b, a, :],
                                                start=(a == 0), stop=(a == TT - 1))
                last.then_inc(gather_done, 1)

            pe.wait_ge(xs_ready, 2)
            gather(0, 0)
            nc.tensor.matmul(ps[:, 6, 0:N_EXP], ones[:, :], chosen[:, 0, :], start=True, stop=False)
            nc.tensor.matmul(ps[:, 6, 0:N_EXP], ones[:, :], chosen[:, 1, :], start=False,
                             stop=True).then_inc(totals_done, 1)
            pe.wait_ge(bup_loaded, 64)

            def biases_to_tokens(a):
                pe.wait_ge(flag_ready, 1)
                wait_past(pe, x_added, a)
                for h in range(2):
                    last = nc.tensor.matmul(ps[:, COMB + h, :], gateT[:, a * P:(a + 1) * P], b_down[h],
                                            start=True, stop=True)
                last.then_inc(comb_done, 1)

            def expert(q, j, turn, first=False):
                pe.wait_ge(xe_ready, q + 1)
                wait_past(pe, lin_ready, q)
                for k in range(UP_UNITS):
                    slot = UP_UNITS * j + k
                    pe.wait_ge(up_loaded[slot], 16 * turn + up_value(slot, 1))
                    for part in range(2):
                        for g in range(2):
                            last = nc.tensor.matmul(ps[64 * g:64 * g + 64, GLU + part, :], xe[:, j, k, :],
                                                    up_ring[:, slot, D * part + 512 * g:D * part + 512 * (g + 1)],
                                                    start=(k == 0), stop=False)
                    last.then_inc(w_used, 1)
                pe.wait_ge(pick_ready, q + 1)
                for part in range(2):
                    for g in range(2):
                        last = nc.tensor.matmul(ps[64 * g:64 * g + 64, GLU + part, :],
                                                pick_bias[:, 2 * part + g, :], b_up, start=False, stop=True)
                last.then_inc(up_done, 1)
                if first:
                    pe.wait_ge(gates_ready, 1)
                    for a in range(TT):
                        last = nc.tensor.transpose(ps[0:N_EXP, WT, a * P:(a + 1) * P], gate_w[:, a, 0:N_EXP],
                                                   ident[:, :])
                    last.then_inc(gateT_done, 1)
                else:
                    pe.wait_ge(y_ready, q)
                    pe.wait_ge(weightT_ready, q)
                    to_tokens(q - 1, 0)
                gather(q + 1, 1 - j)
                if first:
                    pe.wait_ge(gateT_ready, 1)
                    pe.wait_ge(bdown_loaded, 32)
                    biases_to_tokens(0)
                pe.wait_ge(weight_ready, q + 1)
                wait_past(pe, weightT_ready, q)
                for a in range(TT):
                    last = nc.tensor.transpose(ps[:, WT, a * P:(a + 1) * P], weight[:, a, :], ident[:, :])
                last.then_inc(weightT_done, 1)
                pe.wait_ge(prod_ready, 2 * q + 2)
                wait_past(pe, actT_ready, q)
                for m in range(4):
                    last = nc.tensor.transpose(ps[:, ACTT, m * P:(m + 1) * P], lin[:, m * P:(m + 1) * P], ident[:, :])
                last.then_inc(actT_done, 1)
                if first:
                    biases_to_tokens(1)
                else:
                    to_tokens(q - 1, 1)
                pe.wait_ge(actT_ready, q + 1)
                wait_past(pe, y_ready, q)
                for k in range(KT):
                    c = k // 2
                    if k % 2 == 0:
                        pe.wait_ge(down_loaded[c], 16 * q + 16)
                    for g in range(2):
                        col = D * (k % 2) + 512 * g
                        last = nc.tensor.matmul(ps[64 * g:64 * g + 64, Y, :], actT[:, k % 4, k // 4, :],
                                                down_ring[:, c, col:col + 512], start=(k == 0), stop=(k == KT - 1))
                    if k % 2:
                        last.then_inc(w_used, 1)

            def to_tokens(q, a):
                wait_past(pe, x_added, comb_before(q) + a)
                for g in range(2):
                    last = nc.tensor.matmul(ps[:, COMB + g, :], weightT[64 * g:64 * g + 64, a, :],
                                            y_sb[64 * g:64 * g + 64, :], start=True, stop=True)
                last.then_inc(comb_done, 1)

            def ple_projection(a, h):
                wp = up_ring[:, 4, :].rearrange("p (c n) -> p c n", c=2)
                for k in range(PLE // P):
                    nc.tensor.matmul(ps[:, 4 + 2 * a + h, :], pT[:, k, a * P:(a + 1) * P],
                                     wp[:, k, h * 512:(h + 1) * 512], start=(k == 0), stop=(k == PLE // P - 1))

            def finish(q):
                pe.wait_ge(ple_proj_loaded, 16)
                pe.wait_ge(weightT_ready, q + 1)
                ple_projection(0, 0)
                pe.wait_ge(y_ready, q + 1)
                to_tokens(q, 0)
                ple_projection(0, 1)
                pe.wait_ge(x_final, 1)
                for g in range(2):
                    last = nc.tensor.matmul(ps[:, COMB + g, :], weightT[64 * g:64 * g + 64, 1, :],
                                            y_sb[64 * g:64 * g + 64, :], start=True, stop=True)
                last.then_inc(comb_done, 1)
                transpose_tokens(x_sb, 0, 0)
                pe.wait_ge(x_final, 2)
                transpose_tokens(x_sb, 1, 0).then_inc(xsT_done, 1)

            for q in range(2):
                expert(q, q, 0, first=q == 0)
            with pe.Fori(1, N_EXP // 2) as i:
                for j in range(2):
                    expert(2 * i + j, j, i)
            pe.wait_ge(flag_ready, 1)
            overflow = pe.value_load(flag[0:1, 0:1], min_val=0, max_val=1)
            with pe.If(overflow > 0):
                with pe.Fori(N_EXP // 2, ROUNDS * N_EXP // 2) as i:
                    for j in range(2):
                        expert(2 * i + j, j, i)
                finish(ROUNDS * N_EXP - 1)
            with pe.If(overflow < 1):
                finish(N_EXP - 1)

            for h in range(2):
                ple_projection(1, h)
            hT_written(3)
            for a in range(TT):
                for h in range(2):
                    for k in range(KT):
                        if a + h == 0 and k % 2 == 0:
                            pe.wait_ge(ple_gate_loaded[k // 2], 16)
                        wg = up_ring[:, k // 2, :].rearrange("p (c n) -> p c n", c=2)
                        last = nc.tensor.matmul(ps[:, 2 * a + h, :], hT[:, k, a * P:(a + 1) * P],
                                                wg[:, k % 2, h * 512:(h + 1) * 512], start=(k == 0),
                                                stop=(k == KT - 1))
                    last.then_inc(ple_gate_done, 1)


_INS = ["x", "p", "mix_norm", "w_in", "b_in", "pool_w", "pool_scale", "conv_w", "conv_b", "conv_norm_g",
        "conv_norm_b", "sgu_norm_g", "sgu_norm_b", "sgu_w", "sgu_b", "branch_w", "branch_b", "w_out",
        "moe_norm", "router_w", "router_b", "expert_w_up", "expert_b_up", "expert_w_down",
        "expert_b_down", "ple_norm", "ple_gate_w", "ple_proj_w", "final_norm"]


def kernel(**inputs):
    import numpy as np
    import concourse.bacc as bacc
    from concourse.bass_utils import run_bass_kernel_spmd

    nc = bacc.Bacc("TRN2", target_bir_lowering=False, num_devices=1)
    arrays, args = {}, []
    for name in _INS:
        a = np.ascontiguousarray(inputs[name])
        arrays[f"in_{name}_dram"] = a
        args.append(nc.dram_tensor(f"in_{name}_dram", a.shape, mybir.dt.from_np(a.dtype),
                                   kind="ExternalInput").ap())
    args.append(nc.dram_tensor("out_dram", (1, T, D), F32, kind="ExternalOutput").ap())
    build(nc, *args)
    return run_bass_kernel_spmd(nc, [arrays], core_ids=[0]).results[0]["out_dram"]
```
